# Optimizing a Trainium2 kernel written in Bass

```python
import functools
import jax, jax.numpy as jnp
from jax import lax
import numpy as np

D_MODEL = 1024
BATCH = 1
SEQ = 512
DEPTH = 1
DEC_BATCH = 8
DEC_SEQ = 8
PAST_LEN = 2048
PAGE_SIZE = 128

HEAD_DIM = 64
SCALE = HEAD_DIM ** -0.5
BLOCK = 128
STEPS = 128
POOL_WINDOWS = (2, 4, 8, 16)
POOL_GROUPS = len(POOL_WINDOWS)
POOL_CH = 128
POOL_WIDTH = POOL_GROUPS * POOL_CH
POOL_OUT = D_MODEL // POOL_GROUPS
POOL_STATE = max(POOL_WINDOWS) - 1
DIL_GROUPS = ((STEPS * 1, 1), (STEPS * 4, 4), (STEPS * 16, 16))
N_DIL = len(DIL_GROUPS)
DIL_HEADS = 4
DIL_WIDTH = N_DIL * DIL_HEADS * HEAD_DIM
DIL_OUT = DIL_HEADS * HEAD_DIM
SWA_WINDOW = STEPS
SWA_HEADS = 8
SWA_KV_HEADS = 2
SWA_GROUP = SWA_HEADS // SWA_KV_HEADS
N_BUCKETS = 32
MAX_DISTANCE = 2048
N_ATTN_HEADS = N_DIL * DIL_HEADS + SWA_HEADS
N_EXPERTS = 64
TOP_K = 8
EXPERT_FF = 256
SHARED_FF = 256
ROUTED_SCALE = 2.5
MOE_BLOCK = 128
EPS = 1e-6
IN_SPLITS = (POOL_WIDTH, DIL_WIDTH, DIL_WIDTH, DIL_WIDTH, SWA_HEADS * HEAD_DIM,
             SWA_KV_HEADS * HEAD_DIM, SWA_KV_HEADS * HEAD_DIM, 3 * D_MODEL)
IN_WIDTH = sum(IN_SPLITS)

kernel_name = 'hybrid_pool_dilated_swa_moe_step'

def t5_bucket(dist):
    n = np.asarray(dist, dtype=np.int64)
    exact = N_BUCKETS // 2
    log_ratio = np.log(np.maximum(n, 1) / exact) / np.log(MAX_DISTANCE / exact)
    large = np.minimum(exact + (log_ratio * (N_BUCKETS - exact)).astype(np.int64), N_BUCKETS - 1)
    return np.where(n < exact, n, large).astype(np.int32)

def step_bias(rel_bias, dil, h0, h1):
    buckets = t5_bucket(np.arange(STEPS + 1) * dil)
    return jnp.take(rel_bias, buckets, axis=0)[:, h0:h1].T.astype(jnp.float32)

def rms_norm(x, g):
    xf = x.astype(jnp.float32)
    y = xf * lax.rsqrt(jnp.mean(xf * xf, axis=-1, keepdims=True) + EPS)
    return (y * g.astype(jnp.float32)).astype(x.dtype)

def softmax_stats(s, mask, sink=None):
    s = jnp.where(mask, s, -jnp.inf)
    m = jnp.max(s, axis=-1, keepdims=True)
    if sink is not None:
        m = jnp.maximum(m, sink)
    p = jnp.exp(s - m)
    den = jnp.sum(p, axis=-1, keepdims=True)
    if sink is not None:
        den = den + jnp.exp(sink - m)
    return p / den, (m + jnp.log(den))[..., 0]

def band_attn(q, k, v, bias_s, steps, sink=None):
    bt, seq, n_h, hd = q.shape
    n_kv = k.shape[2]
    grp = n_h // n_kv
    nb = -(-seq // BLOCK)
    pad = nb * BLOCK - seq
    q, k, v = [jnp.pad(t, ((0, 0), (0, pad), (0, 0), (0, 0))) for t in (q, k, v)]
    qb = q.reshape(bt, nb, BLOCK, n_kv, grp, hd)

    def with_prev(t):
        tb = t.reshape(bt, nb, BLOCK, n_kv, hd)
        prev = jnp.pad(tb, ((0, 0), (1, 0), (0, 0), (0, 0), (0, 0)))[:, :nb]
        return jnp.concatenate([prev, tb], axis=2)

    kk, vv = with_prev(k), with_prev(v)
    dist = BLOCK + np.arange(BLOCK)[:, None] - np.arange(2 * BLOCK)[None, :]
    kpos = (np.arange(nb)[:, None, None] - 1) * BLOCK + np.arange(2 * BLOCK)[None, None, :]
    mask = (dist >= 0) & (dist <= steps) & (kpos >= 0)
    bias = bias_s[:, np.clip(dist, 0, steps)].reshape(n_kv, grp, BLOCK, 2 * BLOCK)
    s = jnp.einsum('bnqkgd,bnskd->bnkgqs', qb, kk, preferred_element_type=jnp.float32) * SCALE + bias
    p, lse = softmax_stats(s, mask[None, :, None, None], sink)
    o = jnp.einsum('bnkgqs,bnskd->bnqkgd', p.astype(vv.dtype), vv, preferred_element_type=jnp.float32)
    o = o.reshape(bt, nb * BLOCK, n_h, hd)[:, :seq].astype(q.dtype)
    lse = lse.transpose(0, 1, 4, 2, 3).reshape(bt, nb * BLOCK, n_h)[:, :seq]
    return o, lse

def dilated_prompt(q, k, v, dil, bias_s):
    bt, seq = q.shape[:2]

    def fold(t):
        return t.reshape(bt, seq // dil, dil, *t.shape[2:]).swapaxes(1, 2).reshape(bt * dil, seq // dil, *t.shape[2:])

    def unfold(t):
        return t.reshape(bt, dil, seq // dil, *t.shape[2:]).swapaxes(1, 2).reshape(bt, seq, *t.shape[2:])

    o, lse = band_attn(fold(q), fold(k), fold(v), bias_s, STEPS)
    return unfold(o), unfold(lse)

def gathered_attn(q, k_all, v_all, n_buf, dil, bias_s, steps, sink=None):
    bt, n_new, n_h, hd = q.shape
    n_kv = k_all.shape[2]
    grp = n_h // n_kv
    idx = n_buf + np.arange(n_new)[:, None] - dil * np.arange(steps + 1)[None, :]
    valid = idx >= 0
    idx = np.maximum(idx, 0)
    kg, vg = k_all[:, idx], v_all[:, idx]
    qg = q.reshape(bt, n_new, n_kv, grp, hd)
    s = jnp.einsum('btkgd,btjkd->btkgj', qg, kg, preferred_element_type=jnp.float32) * SCALE
    s = s + bias_s.reshape(n_kv, grp, steps + 1)
    p, lse = softmax_stats(s, valid[None, :, None, None, :], sink)
    o = jnp.einsum('btkgj,btjkd->btkgd', p.astype(vg.dtype), vg, preferred_element_type=jnp.float32)
    return o.reshape(bt, n_new, n_h, hd).astype(q.dtype), lse.reshape(bt, n_new, n_h)

def pool_branch(u_ext, n_past, pool_w, pool_scale):
    bt, n_ext, _ = u_ext.shape
    uf = u_ext.astype(jnp.float32)
    cs = jnp.concatenate([jnp.zeros((bt, 1, POOL_WIDTH), jnp.float32), jnp.cumsum(uf, axis=1)], axis=1)
    rows = np.arange(n_past, n_ext)
    parts = []
    for g, win in enumerate(POOL_WINDOWS):
        ch = slice(g * POOL_CH, (g + 1) * POOL_CH)
        lo = np.maximum(rows + 1 - win, 0)
        cnt = (rows + 1 - lo).astype(np.float32)[:, None]
        mean = (cs[:, n_past + 1:, ch] - cs[:, lo, ch]) / cnt
        parts.append(mean - uf[:, n_past:, ch])
    z = jnp.stack(parts, axis=2).astype(pool_w.dtype)
    y = jnp.einsum('blgc,gco->blgo', z, pool_w).reshape(bt, rows.size, D_MODEL)
    return y * pool_scale

def project(h, w_in):
    bt, n, _ = h.shape
    z = jnp.einsum('bld,de->ble', h, w_in)
    cuts = [int(i) for i in np.cumsum(IN_SPLITS)[:-1]]
    u, qb, kb, vb, qc, kc, vc, gl = jnp.split(z, cuts, axis=-1)
    dshape = (bt, n, N_DIL, DIL_HEADS, HEAD_DIM)
    return (u, qb.reshape(dshape), kb.reshape(dshape), vb.reshape(dshape),
            qc.reshape(bt, n, SWA_HEADS, HEAD_DIM), kc.reshape(bt, n, SWA_KV_HEADS, HEAD_DIM),
            vc.reshape(bt, n, SWA_KV_HEADS, HEAD_DIM), gl)

def merge(a, ob, lse, oc, gl, w_b_up, w_c_up, w_out):
    bt, n = a.shape[:2]
    alpha = jax.nn.softmax(jnp.stack(lse, axis=0), axis=0)[..., None]
    b = jnp.sum(alpha * jnp.stack(ob, axis=0).astype(jnp.float32), axis=0)
    b = b.reshape(bt, n, DIL_OUT).astype(w_b_up.dtype) @ w_b_up
    c = oc.reshape(bt, n, SWA_HEADS * HEAD_DIM) @ w_c_up
    g_a, g_b, g_c = jnp.split(jax.nn.sigmoid(gl), 3, axis=-1)
    return (g_a * a + g_b * b + g_c * c) @ w_out

def mixer_prompt(h, bias_b, bias_c, mix_w):
    w_in, pool_w, pool_scale, w_b_up, w_c_up, sinks, w_out = mix_w
    seq = h.shape[1]
    u, qb, kb, vb, qc, kc, vc, gl = project(h, w_in)
    a = pool_branch(u, 0, pool_w, pool_scale)
    ob, lse, kv_b = [], [], []
    for g, (win, dil) in enumerate(DIL_GROUPS):
        o_g, l_g = dilated_prompt(qb[:, :, g], kb[:, :, g], vb[:, :, g], dil, bias_b[g])
        ob.append(o_g)
        lse.append(l_g)
        keep = min(win, seq)
        kv_b.append(jnp.stack([kb[:, seq - keep:, g], vb[:, seq - keep:, g]], axis=2))
    sink = sinks.astype(jnp.float32).reshape(SWA_KV_HEADS, SWA_GROUP, 1, 1)
    oc, _ = band_attn(qc, kc, vc, bias_c, SWA_WINDOW, sink)
    keep = min(SWA_WINDOW, seq)
    kv_c = jnp.stack([kc[:, seq - keep:], vc[:, seq - keep:]], axis=2)
    y = merge(a, ob, lse, oc, gl, w_b_up, w_c_up, w_out)
    return y, (kv_b[0], kv_b[1], kv_b[2], kv_c, u[:, seq - POOL_STATE:])

def mixer_sample(h, caches, bias_b, bias_c, mix_w):
    w_in, pool_w, pool_scale, w_b_up, w_c_up, sinks, w_out = mix_w
    u, qb, kb, vb, qc, kc, vc, gl = project(h, w_in)
    pool_buf = caches[4]
    u_ext = jnp.concatenate([pool_buf.astype(u.dtype), u], axis=1)
    a = pool_branch(u_ext, pool_buf.shape[1], pool_w, pool_scale)
    ob, lse, kv_b = [], [], []
    for g, (win, dil) in enumerate(DIL_GROUPS):
        buf = caches[g].astype(kb.dtype)
        n_buf = buf.shape[1]
        k_all = jnp.concatenate([buf[:, :, 0], kb[:, :, g]], axis=1)
        v_all = jnp.concatenate([buf[:, :, 1], vb[:, :, g]], axis=1)
        o_g, l_g = gathered_attn(qb[:, :, g], k_all, v_all, n_buf, dil, bias_b[g], STEPS)
        ob.append(o_g)
        lse.append(l_g)
        kv_b.append(jnp.stack([k_all[:, -n_buf:], v_all[:, -n_buf:]], axis=2))
    buf = caches[3].astype(kc.dtype)
    n_buf = buf.shape[1]
    k_all = jnp.concatenate([buf[:, :, 0], kc], axis=1)
    v_all = jnp.concatenate([buf[:, :, 1], vc], axis=1)
    sink = sinks.astype(jnp.float32).reshape(SWA_KV_HEADS, SWA_GROUP, 1)
    oc, _ = gathered_attn(qc, k_all, v_all, n_buf, 1, bias_c, SWA_WINDOW, sink)
    kv_c = jnp.stack([k_all[:, -n_buf:], v_all[:, -n_buf:]], axis=2)
    y = merge(a, ob, lse, oc, gl, w_b_up, w_c_up, w_out)
    return y, (kv_b[0], kv_b[1], kv_b[2], kv_c, u_ext[:, -POOL_STATE:])

def swiglu(x, wg, wu, wd):
    return (jax.nn.silu(x @ wg) * (x @ wu)) @ wd

def routed_experts(xf, top_idx, top_w, we_gate, we_up, we_down):
    n_tok, d = xf.shape
    n_asg = n_tok * TOP_K
    e_flat = top_idx.reshape(n_asg)
    order = jnp.argsort(e_flat)
    e_sorted = e_flat[order]
    tok_sorted = (order // TOP_K).astype(jnp.int32)
    w_sorted = top_w.reshape(n_asg)[order].astype(xf.dtype)
    counts = jnp.bincount(e_flat, length=N_EXPERTS)
    padded = (counts + MOE_BLOCK - 1) // MOE_BLOCK * MOE_BLOCK
    pad_end = jnp.cumsum(padded)
    pad_start = pad_end - padded
    start = jnp.cumsum(counts) - counts
    dest = pad_start[e_sorted] + jnp.arange(n_asg, dtype=jnp.int32) - start[e_sorted]
    n_blocks = -(-(n_asg + N_EXPERTS * (MOE_BLOCK - 1)) // MOE_BLOCK)
    n_rows = n_blocks * MOE_BLOCK
    row_tok = jnp.full((n_rows,), n_tok, jnp.int32).at[dest].set(tok_sorted)
    row_w = jnp.zeros((n_rows,), xf.dtype).at[dest].set(w_sorted)
    block_exp = jnp.minimum(jnp.searchsorted(pad_end, jnp.arange(n_blocks) * MOE_BLOCK, side='right'), N_EXPERTS - 1)
    x_rows = jnp.concatenate([xf, jnp.zeros((1, d), xf.dtype)], axis=0)[row_tok].reshape(n_blocks, MOE_BLOCK, d)

    def one_block(args):
        xb, e = args
        return swiglu(xb, we_gate[e], we_up[e], we_down[e])

    y_rows = lax.map(one_block, (x_rows, block_exp)).reshape(n_rows, d)
    return jax.ops.segment_sum(y_rows * row_w[:, None], row_tok, num_segments=n_tok + 1)[:n_tok]

def moe(h, w_router, router_bias, we_gate, we_up, we_down, ws_gate, ws_up, ws_down):
    bt, n, d = h.shape
    xf = h.reshape(bt * n, d)
    scores = jax.nn.sigmoid(jnp.einsum('nd,de->ne', xf, w_router, preferred_element_type=jnp.float32))
    _, top_idx = lax.top_k(scores + router_bias.astype(jnp.float32), TOP_K)
    top_s = jnp.take_along_axis(scores, top_idx, axis=1)
    top_w = top_s / jnp.sum(top_s, axis=-1, keepdims=True) * ROUTED_SCALE
    y = routed_experts(xf, top_idx, top_w, we_gate, we_up, we_down) + swiglu(xf, ws_gate, ws_up, ws_down)
    return y.reshape(bt, n, d)

def sublayer_pair(x, c, mixer, w_ada, b_ada, g1, g2, g3, g4, moe_w):
    ada = jnp.einsum('bd,de->be', jax.nn.silu(c), w_ada) + b_ada
    sh_m, sc_m, gt_m, sh_f, sc_f, gt_f = jnp.split(ada[:, None, :], 6, axis=-1)
    m, new_state = mixer(rms_norm(x, g1) * (1 + sc_m) + sh_m)
    x = x + gt_m * rms_norm(m, g2)
    f = moe(rms_norm(x, g3) * (1 + sc_f) + sh_f, *moe_w)
    x = x + gt_f * rms_norm(f, g4)
    return x, new_state

def setup_inputs(seed: int = 0) -> dict:
    key = jax.random.key(seed)
    ks = iter(jax.random.split(key, 40))

    def nrm(shape, scale):
        return jax.random.normal(next(ks), shape, jnp.float32) * scale

    D = D_MODEL
    return {
        'x_prompt': nrm((BATCH, SEQ, D), 1.0),
        'x_sample': nrm((DEC_BATCH, DEC_SEQ, D), 1.0),
        'cache_b1': nrm((DEPTH, DEC_BATCH, min(DIL_GROUPS[0][0], PAST_LEN), 2, DIL_HEADS, HEAD_DIM), 1.0),
        'cache_b2': nrm((DEPTH, DEC_BATCH, min(DIL_GROUPS[1][0], PAST_LEN), 2, DIL_HEADS, HEAD_DIM), 1.0),
        'cache_b3': nrm((DEPTH, DEC_BATCH, min(DIL_GROUPS[2][0], PAST_LEN), 2, DIL_HEADS, HEAD_DIM), 1.0),
        'cache_c': nrm((DEPTH, DEC_BATCH, min(SWA_WINDOW, PAST_LEN), 2, SWA_KV_HEADS, HEAD_DIM), 1.0),
        'state_pool': nrm((DEPTH, DEC_BATCH, POOL_STATE, POOL_WIDTH), 1.0),
        'c_prompt': nrm((BATCH, D), 1.0),
        'c_sample': nrm((DEC_BATCH, D), 1.0),
        'rel_bias': nrm((N_BUCKETS, N_ATTN_HEADS), 0.5),
        'w_ada': nrm((DEPTH, D, 6 * D), 0.5 * D ** -0.5),
        'b_ada': nrm((DEPTH, 6 * D), 0.02),
        'g_pre_mix': 1.0 + nrm((DEPTH, D), 0.05),
        'g_post_mix': 1.0 + nrm((DEPTH, D), 0.05),
        'g_pre_ffn': 1.0 + nrm((DEPTH, D), 0.05),
        'g_post_ffn': 1.0 + nrm((DEPTH, D), 0.05),
        'w_in': nrm((DEPTH, D, IN_WIDTH), D ** -0.5),
        'pool_w': nrm((DEPTH, POOL_GROUPS, POOL_CH, POOL_OUT), POOL_CH ** -0.5),
        'pool_scale': 1.0 + nrm((DEPTH, D), 0.1),
        'w_b_up': nrm((DEPTH, DIL_OUT, D), DIL_OUT ** -0.5),
        'w_c_up': nrm((DEPTH, SWA_HEADS * HEAD_DIM, D), (SWA_HEADS * HEAD_DIM) ** -0.5),
        'sinks': nrm((DEPTH, SWA_HEADS), 1.0),
        'w_out': nrm((DEPTH, D, D), D ** -0.5),
        'w_router': nrm((DEPTH, D, N_EXPERTS), D ** -0.5),
        'router_bias': nrm((DEPTH, N_EXPERTS), 0.01),
        'we_gate': nrm((DEPTH, N_EXPERTS, D, EXPERT_FF), D ** -0.5),
        'we_up': nrm((DEPTH, N_EXPERTS, D, EXPERT_FF), D ** -0.5),
        'we_down': nrm((DEPTH, N_EXPERTS, EXPERT_FF, D), EXPERT_FF ** -0.5),
        'ws_gate': nrm((DEPTH, D, SHARED_FF), D ** -0.5),
        'ws_up': nrm((DEPTH, D, SHARED_FF), D ** -0.5),
        'ws_down': nrm((DEPTH, SHARED_FF, D), SHARED_FF ** -0.5),
    }

def reference(x_prompt, x_sample, cache_b1, cache_b2, cache_b3, cache_c, state_pool, c_prompt, c_sample,
              rel_bias, w_ada, b_ada, g_pre_mix, g_post_mix, g_pre_ffn, g_post_ffn, w_in, pool_w, pool_scale,
              w_b_up, w_c_up, sinks, w_out, w_router, router_bias, we_gate, we_up, we_down,
              ws_gate, ws_up, ws_down):
    bias_b = [step_bias(rel_bias, dil, g * DIL_HEADS, (g + 1) * DIL_HEADS) for g, (_, dil) in enumerate(DIL_GROUPS)]
    bias_c = step_bias(rel_bias, 1, N_DIL * DIL_HEADS, N_ATTN_HEADS)
    xp, xs = x_prompt, x_sample
    states_p, states_s = [], []
    for l in range(DEPTH):
        mix_w = (w_in[l], pool_w[l], pool_scale[l], w_b_up[l], w_c_up[l], sinks[l], w_out[l])
        moe_w = (w_router[l], router_bias[l], we_gate[l], we_up[l], we_down[l], ws_gate[l], ws_up[l], ws_down[l])
        layer_w = (w_ada[l], b_ada[l], g_pre_mix[l], g_post_mix[l], g_pre_ffn[l], g_post_ffn[l], moe_w)
        mix_p = functools.partial(mixer_prompt, bias_b=bias_b, bias_c=bias_c, mix_w=mix_w)
        mix_s = functools.partial(mixer_sample,
                                  caches=(cache_b1[l], cache_b2[l], cache_b3[l], cache_c[l], state_pool[l]),
                                  bias_b=bias_b, bias_c=bias_c, mix_w=mix_w)
        xp, st_p = sublayer_pair(xp, c_prompt, mix_p, *layer_w)
        xs, st_s = sublayer_pair(xs, c_sample, mix_s, *layer_w)
        states_p.append(st_p)
        states_s.append(st_s)
    b1_p, b2_p, b3_p, c_p, pool_p = [jnp.stack(s, axis=0) for s in zip(*states_p)]
    b1_s, b2_s, b3_s, c_s, pool_s = [jnp.stack(s, axis=0) for s in zip(*states_s)]
    return (xp, xs, b1_p, b2_p, b3_p, c_p, pool_p, b1_s, b2_s, b3_s, c_s, pool_s)


_drawn_inputs = setup_inputs


def setup_inputs(seed=0):
    import zlib

    import numpy as np

    out = dict(_drawn_inputs(seed))
    spreads = {}
    factors = {'g_post_ffn': 4.167, 'sinks': 8.0}
    for name, (base, spread) in spreads.items():
        noise = np.random.default_rng([zlib.crc32(name.encode()), seed]).standard_normal(out[name].shape)
        drawn = base * np.exp(spread * noise) if base else spread * noise
        out[name] = __import__('jax').numpy.asarray(drawn.astype(out[name].dtype))
    for name, factor in factors.items():
        out[name] = (out[name] * factor).astype(out[name].dtype)
    return out
```

```python
from contextlib import ExitStack

import numpy as np
import concourse.bass as bass
from concourse import mybir

F32 = mybir.dt.float32
I32 = mybir.dt.int32
U32 = mybir.dt.uint32
ACT = mybir.ActivationFunctionType
ALU = mybir.AluOpType
AX = mybir.AxisListType.X

P = 128
D = 1024
KD = D // P
SEQ = 512
NB, NT = 8, 8
NS = NB * NT
TOK = SEQ + NS
PT_ = SEQ // P
TILES = PT_ + 1
HD = 64
SCALE = HD ** -0.5
POOLW = (2, 4, 8, 16)
PSTATE = 15
GATE0 = 3584
NE, TOPK, FF = 64, 8, 256
RSCALE = 2.5
EPS = 1e-6
MASK = -1e30
NBLK = (TOK * TOPK + NE * (P - 1)) // P // 2 * 2 + 2
CACHE = (128, 512, 2048)
BINS = 33
GW = 384
NK = 136
SK = P + NS


def parts(t):
    return P if t < PT_ else NS


def toks(t):
    return slice(t * P, t * P + parts(t))


def plan():
    fills = []
    ring = {"set": list(range(8)), "n": 0}

    def fill(key, who, bank=None):
        if bank is None:
            bank = ring["set"][ring["n"] % len(ring["set"])]
            ring["n"] += 1
        fills.append((key, who, bank))

    fill(("cT",), "D")
    for g in range(4):
        fill(("ada", g), "D")
    for n in range(3):
        fill(("gtab", n), "D")
    for n in range(7):
        fill(("stab", n), "A")
    for g in range(4, 8):
        fill(("ada", g), "D")
    for t in range(TILES):
        for h in range(2):
            fill(("hT", t, h), "AD"[h])
        if t < 4:
            fill(("ada", 8 + t), "D")
    fill(("state",), "D")
    for c in range(4):
        for h in range(2):
            fill(("u", c, h), "AD"[h])
    for c in range(6):
        for h in range(2):
            fill(("q", c, h), "AD"[h])
    for g in (0, 1, 2):
        for t in range(TILES):
            fill(("k", g, t), "AD"[t % 2])
    for g in (0, 1):
        for t in range(TILES):
            fill(("v", g, t), "AD"[t % 2])
    for t in range(TILES):
        fill(("v", 2, t), "AD"[t % 2])
    for c in range(6, 10):
        for h in range(2):
            fill(("q", c, h), "AD"[h])
    for t in range(TILES):
        fill(("kvc", t), "AD"[t % 2])
    fill(("uout", 0), "A")
    fill(("uout", 1), "A")
    for m in range(7):
        fill(("kT", m), "AD"[m % 2])
    fill(("kTs",), "D")
    for s in range(len(UNITS) + LAGO):
        if s < len(UNITS):
            fill(("S", s), "D")
        if 0 <= s - LAGT < len(UNITS):
            fill(("T", s - LAGT), "A")
        if 0 <= s - LAGO < len(UNITS):
            fill(("O", s - LAGO), "D")
        for key in after_unit(s - LAGO):
            fill(key, "A")
    ring["set"], ring["n"] = list(range(5)), 0
    fill(("Sn", 0), "A")
    fill(("Sn", 1), "A")
    fill(("SnC",), "A")
    for s in range(NKF + 1):
        if s < NKF:
            fill(("KT", s), "AD"[s % 2])
        if s - 1 == 1:
            fill(("SM", 2), "A", 7)
        if s - 1 == 21:
            fill(("SM", 0), "A", 5)
        if s - 1 == NKF - 1:
            fill(("SM", 1), "A", 6)
    ring["set"], ring["n"] = list(range(8)), 0
    for c in range(4):
        fill(("SRC", c), "D")
    for g in range(3):
        for p in range(2):
            fill(("SR", g, p), "D")
    fill(("PTC",), "A")
    fill(("PTCn",), "D")
    for p in range(2):
        fill(("PT", p), "A")
        fill(("PTn", p), "D")
    fill(("OC",), "D")
    fill(("OB", 0), "D")
    fill(("OB", 1), "D")
    for m in range(KD):
        for h in range(2):
            for what in ("ga", "gb", "gc"):
                fill((what, m, h), "A")
            for what in ("oa", "ob", "oc"):
                fill((what, m, h), "D")
    for h in range(2):
        for t in range(TILES):
            fill(("mix", t, h), "AD"[t % 2])
    for t in range(TILES):
        for h in range(2):
            fill(("h2T", t, h), "AD"[h])
    for t in range(TILES):
        fill(("rt", t), "A")
    for t in range(TILES):
        fill(("sgu", t), "A")
        if t >= 1:
            fill(("saT", t - 1), "A")
            fill(("sy", t - 1, 0), "A")
            fill(("sy", t - 1, 1), "A")
    fill(("saT", TILES - 1), "A")
    fill(("sy", TILES - 1, 0), "A")
    fill(("sy", TILES - 1, 1), "A")
    for t in range(TILES):
        fill(("pos", t), "D")
    fill(("cnt",), "D")
    fill(("rowtok",), "D")
    fill(("bexp",), "D")
    return fills


UNITS = ([(k, t, p) for k in (1, 2) for t in range(4) for p in range(2)]
         + [(0, t, p) for t in range(4) for p in range(2)]
         + [("C", t, p) for t in range(4) for p in range(4)])
LAGT, LAGO = 2, 3
NKF = 54
COMBINE_AT = 27


def heads(unit):
    kind, _, p = unit
    return [2 * p, 2 * p + 1] if kind == "C" else [p, p + 2]


def key_blocks(unit):
    kind, t, _ = unit
    if kind in (1, 2):
        return [(t, 0)]
    return ([(t - 1, 0)] if t else []) + [(t, P)]


def head_cols(unit):
    return P if unit[0] in (1, 2) else 2 * P


def after_unit(u):
    if u < 0 or u >= len(UNITS):
        return []
    out = []
    kind, t, p = UNITS[u]
    if kind == "C" and p == 3:
        out.append(("ocT", t))
    if u == COMBINE_AT + 3:
        out += [("bT", t) for t in range(PT_)]
    return out


def key_fills():
    blocks = [("C", b, 0, 0) for b in range(NB)]
    blocks += [(0, b, 0, p) for b in range(NB) for p in range(2)]
    blocks += [(1, b, r, p) for b in range(NB) for r in range(4) for p in range(2)]
    blocks += [(2, b, r, p) for b in range(NB) for r in range(8) for p in range(2)]
    return [blocks[4 * n:4 * n + 4] for n in range(NKF)]


def loads():
    out = [(("ada", g), g % 4) for g in range(12)]
    out += [(("in", g), g % 4) for g in range(7)]
    n = 7
    for kv in "KV":
        for key in [("c0", 0), ("c1", 0), ("c1", 1)] + [("c2", q) for q in range(4)]:
            out.append(((kv,) + key, n % 4))
            n += 1
    out.append((("wc",), 0))
    for m in range(KD):
        out.append((("gate", m), 1 + m % 3))
    out += [(("wout", 0), 0), (("wout", 1), 1), (("wsgu",), 2), (("wsd",), 3)]
    return out


SLOT = 4096
A_HT = 4 * SLOT
A_QT = A_HT + KD * TOK
A_KT = A_QT + 10 * TOK
A_KTM = A_KT + 7 * TOK
A_VTM = A_KTM + TILES * 896
A_ZT = A_VTM + TILES * 896
A_BT = A_ZT + 4 * TOK
A_OCT = A_BT + 2 * TOK
A_SC = A_OCT + 4 * TOK
ARENA = 52480
UE = 16 + SEQ + NB * (PSTATE + NT)


def consts():
    def bucket(d):
        n = np.asarray(d, np.int64)
        log = np.log(np.maximum(n, 1) / 16) / np.log(2048 / 16)
        return np.where(n < 16, n, np.minimum(16 + (log * 16).astype(np.int64), 31))

    top = np.zeros((BINS, 3, GW), np.float32)
    for x in range(GW):
        d = 255 - x
        for n, (dil, every) in enumerate(((1, 1), (4, 1), (4, 4))):
            ok = 0 <= d <= 128 and d % every == 0
            top[bucket(dil * d) if ok else 32, n, x] = 1
    smp = np.zeros((BINS, 3, NT, NK), np.float32)
    for t in range(NT):
        for k in range(NK):
            new = k - P
            for n, dil in enumerate((1, 4, 16)):
                if dil == 1:
                    j = P + t - k
                    ok = 0 <= j <= 128
                elif k < P:
                    j = P + t // dil - k
                    ok = 0 <= j <= 128
                else:
                    j = (t - new) // dil
                    ok = new <= t and (t - new) % dil == 0
                smp[bucket(dil * j) if ok else 32, n, t, k] = 1
    one = np.zeros((P, 5 * P), np.float32)
    one[:, :P] = np.eye(P)
    one[:, P:2 * P] = np.triu(np.ones((P, P)), 1)
    one[:, 2 * P:3 * P] = np.arange(P)[None]
    rows = np.arange(P)
    for b in range(NB):
        one[:, 3 * P + b] = np.where(rows // 16 == b, 0, MASK)
        for c in range(4):
            one[:, 3 * P + 8 + c * 8 + b] = np.where(2 * c + rows // 64 == b, 0, MASK)
    for t in range(TILES):
        one[:, 3 * P + 40 + t] = t * P + rows
    one[:, 3 * P + 45] = rows
    for g, w in enumerate(POOLW):
        one[:, 4 * P + 16 * g:4 * P + 16 * g + 16] = (1.0 / np.minimum(np.arange(16) + 1, w))[None]
    return top.reshape(BINS, -1), smp.reshape(BINS, -1), one


def build(nc, x_prompt, x_sample, cache_b1, cache_b2, cache_b3, cache_c, state_pool, c_prompt, c_sample,
          rel_bias, w_ada, b_ada, g_pre_mix, g_post_mix, g_pre_ffn, g_post_ffn, w_in, pool_w, pool_scale,
          w_b_up, w_c_up, sinks, w_out, w_router, router_bias, we_gate, we_up, we_down,
          ws_gate, ws_up, ws_down, onehot_top, onehot_smp, const,
          y_p, y_s, b1_p, b2_p, b3_p, c_p, pool_p, b1_s, b2_s, b3_s, c_s, pool_s):
    PLAN = plan()
    INDEX = {key: n for n, (key, _, _) in enumerate(PLAN)}
    RANK = {}
    for n, (key, who, _) in enumerate(PLAN):
        RANK[key] = sum(1 for k in PLAN[:n] if k[1] == who)
    LOADS = loads()
    KEYS = key_fills()
    caches = (cache_b1, cache_b2, cache_b3)
    outs_p, outs_s = (b1_p, b2_p, b3_p), (b1_s, b2_s, b3_s)

    with ExitStack() as ctx:
        def sem(name):
            return ctx.enter_context(nc.semaphore(name))

        def sb(name, shape, dt=F32):
            return ctx.enter_context(nc.sbuf_tensor(name, shape, dt))

        arena = sb("arena", [P, ARENA])

        def at(off, *dims):
            n = int(np.prod(dims))
            v = arena[:, off:off + n]
            if len(dims) == 2:
                v = v.rearrange("p (a b) -> p a b", b=dims[1])
            if len(dims) == 3:
                v = v.rearrange("p (a b c) -> p a b c", b=dims[1], c=dims[2])
            return v

        ident = sb("ident", [P, P])
        misc = sb("misc", [P, P])
        recip = sb("recip", [P, 4, 16])
        mx = sb("mx", [P, 4, 4])
        nmx = sb("nmx", [P, 4, 4])
        den = sb("den", [P, 4, 4])
        dsk = sb("dsk", [P, 4, 4])
        rden = sb("rden", [P, 4, 4])
        cmb = sb("cmb", [P, 8, 16])
        sst = sb("sst", [P, 6, 4])
        sinkr = sb("sinkr", [P, 1])
        sinkb = sb("sinkb", [P, 8])
        pscale = sb("pscale", [P, KD])
        stat = sb("stat", [P, 4, TILES])
        wts = sb("wts", [P, TILES, TOPK])
        icol = sb("icol", [P, 2], U32)
        scol = sb("scol", [P, 2], U32)
        wcol = sb("wcol", [P, 2])
        ints = sb("ints", [P, 2])
        pairs = sb("pairs", [P, 1], I32)
        psb = [ctx.enter_context(nc.psum_tensor(f"bank{n}", [P, 512], F32))[:, :] for n in range(8)]
        bmask_b = misc[:, 0:8]
        bmask_c = misc[:, 8:40].rearrange("p (c b) -> p c b", b=8)
        tokid = misc[:, 40:45]
        pid = misc[:, 45:46]

        toep = nc.dram_tensor("toep", [20, P, GW], F32, kind="Internal").ap()
        sbias = nc.dram_tensor("sbias", [20, NT, NK], F32, kind="Internal").ap()
        mods = nc.dram_tensor("mods", [9, 6, D], F32, kind="Internal").ap()
        fold = nc.dram_tensor("fold", [2, SEQ, 264], F32, kind="Internal").ap()
        h2rows = nc.dram_tensor("h2rows", [TOK, D], F32, kind="Internal").ap()
        yacc = nc.dram_tensor("yacc", [TOK + P, D], F32, kind="Internal").ap()

        slot = [at(n * SLOT, SLOT) for n in range(4)]
        hT = at(A_HT, KD, TOK)
        qT = at(A_QT, 10, TOK)
        kT = at(A_KT, 7, TOK)
        kTM = at(A_KTM, TILES, 896)
        vTM = at(A_VTM, TILES, 896)
        zT = at(A_ZT, 4, TOK)
        bT = at(A_BT, 2, TOK)
        ocT = at(A_OCT, 4, TOK)
        uext = at(A_BT, 4, UE)
        xall = at(A_QT, TILES, D)
        hbuf = at(A_KT, 2, D)
        modb = at(A_KTM, 4, D)
        ada = at(A_VTM, 6 * D)
        gains = at(A_VTM + 6 * D, 4 * D)
        crow = at(A_VTM + 10 * D, 2 * D)
        junk = at(A_VTM + 12 * D, D)
        cT = at(A_VTM + 13 * D, KD, 9)
        relT = at(A_VTM + 13 * D + 80, 20)
        oh_top = at(A_HT, 3 * GW)
        oh_smp = at(A_HT + 3 * GW, 3 * NT * NK)
        gtab = at(A_KT + 2 * D, 3 * GW)
        stab = at(ARENA - 3 * NT * NK, 3 * NT * NK)
        ping = at(A_SC, 2, UE)
        uS = at(A_SC + 2 * UE, 4, NS)
        staterow = at(A_SC + 2 * UE + 4 * NS, 512)
        uouts = at(A_SC + 2 * UE + 4 * NS, 2, 512)
        sbuf_ = at(A_SC, 3, 512)
        pTb = at(A_SC + 1536, 2, 512)
        biasP = at(ARENA - 8 * 512, 8, 512)
        stage = at(2 * SLOT, 3, PT_ * 264)
        octok = at(A_KTM, 2, 512)
        qbd = at(A_SC, 6, P)
        qbdC = at(A_SC + 768, 512)
        biasS = at(A_SC + 1280, 7, SK)
        biasRaw = at(A_SC + 1280 + 7 * SK, 7, NK)
        ktr = at(A_SC + 1280 + 7 * SK + 7 * NK, 4, 512)
        sB = at(A_QT, 2, 3 * SK)
        sC = at(A_QT + 6 * SK, 4, SK)
        stB = at(A_QT + 10 * SK, 6, P)
        stBn = at(A_QT + 10 * SK + 768, 6, P)
        stC = at(A_QT + 10 * SK + 1536, 512)
        stCn = at(A_QT + 10 * SK + 2048, 512)
        pB = at(A_KTM, 6, P)
        pBn = at(A_KTM + 768, 6, P)
        pC = at(A_KTM + 1536, 512)
        pCn = at(A_KTM + 2048, 512)
        mixT = at(A_QT, KD, TOK)
        wb = at(A_KT, 2, D)
        pw = at(A_KT + 2 * D, 4, 256)
        gsig = at(A_KTM, 6, 288)
        msum = at(A_KTM + 6 * 288, 4, 288)
        A_H2 = 24576
        A_SG = 18432
        h2T = at(A_H2, KD, TOK)
        mixed = at(A_H2 + 4608, TILES, D)
        ysh = mixed
        x1 = at(A_H2 + 9728, TILES, D)
        A_M = A_H2 + 14848
        gmod = at(A_M, 2, D)
        modf = at(A_M + 2 * D, 4, D)
        hbuf2 = at(A_M + 6 * D, 2, D)
        junk2 = at(A_M + 8 * D, D)
        A_R = A_M + 9 * D
        assert A_R + 3400 <= ARENA
        const2 = at(A_R, 2, P)
        ones = at(A_R + 256, P)
        rbias = at(A_R + 384, NE)
        scores = at(A_R + 448, TILES, NE)
        sel = at(A_R + 768, TILES, NE)
        maskt = at(A_R + 1088, TILES, NE)
        starts = at(A_R + 1408, 4, NE)
        top8 = at(A_R + 1664, TILES, TOPK)
        idxf = at(A_R + 1704, TILES, TOPK)
        rowk = at(A_R + 1744, TILES, TOPK)
        slotf = at(A_R + 1784, TILES, TOPK)
        blkf = at(A_R + 1824, TILES, TOPK)
        rowi = arena[:, A_R + 1864:A_R + 1904].bitcast(U32)
        sloti = arena[:, A_R + 1904:A_R + 1944].bitcast(I32)
        idxu = arena[:, A_R + 1944:A_R + 1984].bitcast(U32)
        rowtok = arena[:, A_R + 1984:A_R + 1984 + NBLK + 2].bitcast(U32)
        bexp = arena[:, A_R + 2104:A_R + 2232].bitcast(I32)
        bexpf = at(A_R + 2232, 8)
        wr = at(A_R + 2240, KD, NE)
        topm = at(A_M, TILES * TOPK, NE)
        prod = at(A_M + 2560, TOPK * NE)
        ohslot = at(A_M + 3072, TOPK, P)
        ohblk = at(A_M + 4096, 2, TOPK * NBLK)
        sgat = at(A_SG, 3, 256)
        saT = at(A_SG + 768, 2, P)
        wexp = [at(n * 6144, 6144) for n in range(2)]
        xg = at(A_M, 2, D)
        xT = at(A_M + 2048, 2, D)
        act3 = at(A_M + 4096, 6, FF)
        aT = at(A_M + 5632, 2, FF)
        yb = at(A_M + 6144, 2, D)
        g2mod = at(8 * D, 2, D)

        fills_done = sem("fills_done")
        emptied = {"A": sem("emptied_by_act"), "D": sem("emptied_by_dve")}
        slot_in = [sem(f"slot_in{n}") for n in range(4)]
        dve_step, act_step, pool_step = sem("dve_step"), sem("act_step"), sem("pool_step")
        consts_in, x_in, crow_in, gains_in, badd_in = (sem(n) for n in
                                                       ("consts_in", "x_in", "crow_in", "gains_in", "badd_in"))
        onehots_in = sem("onehots_in")
        c_exp, c_silu = sem("c_exp"), sem("c_silu")
        tables_out, mods_out, modb_in = sem("tables_out"), sem("mods_out"), sem("modb_in")
        mods_rows = sem("mods_rows")
        ssq_ready, root_ready, rn_ready, xn_ready, hA_ready, h_ready = (sem(n) for n in (
            "ssq_ready", "root_ready", "rn_ready", "xn_ready", "hA_ready", "h_ready"))
        ms_ready = sem("ms_ready")
        state_in, ubuf_ready, z_ready = sem("state_in"), sem("ubuf_ready"), sem("z_ready")
        kv_out, u_out = sem("kv_out"), sem("u_out")
        biasp_in, biass_in = sem("biasp_in"), sem("biass_in")
        max_ready, probs_ready = sem("max_ready"), sem("probs_ready")
        stage_ready, stage_out, stage_in = sem("stage_ready"), sem("stage_out"), sem("stage_in")
        oc_ready, bsum_ready = sem("oc_ready"), sem("bsum_ready")
        cm_ready, ce_ready = sem("cm_ready"), sem("ce_ready")
        qbd_ready, keys_used = sem("qbd_ready"), sem("keys_used")
        smax_ready, sexp_ready, sprob_ready, biass_ready = (sem(n) for n in (
            "smax_ready", "sexp_ready", "sprob_ready", "biass_ready"))
        merge_in, gate_ready, branch_used, mix_ready = (sem(n) for n in (
            "merge_in", "gate_ready", "branch_used", "mix_ready"))
        gexp_ready = sem("gexp_ready")
        xres_in, gmod_in, modf_in = sem("xres_in"), sem("gmod_in"), sem("modf_in")
        x1_ready, h2_out = sem("x1_ready"), sem("h2_out")
        moe_in, rexp_ready, masks_ready, onehot_ready = (sem(n) for n in (
            "moe_in", "rexp_ready", "masks_ready", "onehot_ready"))
        sexpg, sact_ready = sem("shared_exp"), sem("shared_act")
        ohs_ready, tables_ready, bexp_ready = sem("ohs_ready"), sem("tables_ready"), sem("bexp_ready")
        copies_out = sem("copies_out")
        wgu_in = [sem("wgu_in0"), sem("wgu_in1")]
        wd_in = [sem("wd_in0"), sem("wd_in1")]
        xg_in = [sem("xg_in0"), sem("xg_in1")]
        y_out = [sem("y_out0"), sem("y_out1")]
        icol_ready = sem("icol_ready")
        t_done, xt_act, xt_dve, gu_done, e_ready, a_ready, at_done, at_ready, d_done, y_act, y_dve = (
            sem(n) for n in ("t_done", "xt_act", "xt_dve", "gu_done", "e_ready", "a_ready", "at_done",
                             "at_ready", "d_done", "y_act", "y_dve"))
        added = sem("added")
        yacc_in, cols_ready, g2_in = sem("yacc_in"), sem("cols_ready"), sem("g2_in")
        f_in = [sem(f"f_in{t}") for t in range(TILES)]
        f_ssq, f_root, f_rn, f_out = (sem(n) for n in ("f_ssq", "f_root", "f_rn", "f_out"))

        def wait_fill(eng, key):
            eng.wait_ge(fills_done, INDEX[key] + 1)
            return psb[PLAN[INDEX[key]][2]]

        def wait_emptied(eng, key):
            eng.wait_ge(emptied[PLAN[INDEX[key]][1]], RANK[key] + 1)

        def bank_for(pe, key):
            n = INDEX[key]
            bank = PLAN[n][2]
            for m in range(n - 1, -1, -1):
                if PLAN[m][2] == bank:
                    wait_emptied(pe, PLAN[m][0])
                    break
            return psb[bank]

        def slot_of(key):
            return next(s for k, s in LOADS if k == key)

        def pieces(key):
            n = {"ada": 1, "in": 1, "wc": 1, "gate": 3, "wout": 1, "wsgu": 2, "wsd": 2}.get(key[0])
            if n is None:
                n = {"c0": 2, "c1": 4, "c2": 2}[key[1]]
            return n

        def slot_total(key):
            s = slot_of(key)
            total = 0
            for k, q in LOADS:
                if q == s:
                    total += 16 * pieces(k)
                if k == key:
                    return total

        def wait_load(eng, key):
            eng.wait_ge(slot_in[slot_of(key)], slot_total(key))
            return slot[slot_of(key)]

        LAST = {("ada", g): ("ada", g) for g in range(12)}
        LAST.update({("in", 0): ("u", 3, 1), ("in", 1): ("q", 3, 1), ("in", 2): ("k", 0, 4),
                     ("in", 3): ("k", 2, 4), ("in", 4): ("v", 1, 4), ("in", 5): ("q", 7, 1),
                     ("in", 6): ("kvc", 4), ("K", "c0", 0): ("KT", 5), ("K", "c1", 0): ("KT", 13),
                     ("K", "c1", 1): ("KT", 21)})
        LAST.update({("K", "c2", q): ("KT", 22 + 8 * q + 7) for q in range(4)})
        LAST.update({("V", a, q): ("OB", 1) for a, q in [("c0", 0), ("c1", 0), ("c1", 1), ("c2", 0), ("c2", 1),
                                                         ("c2", 2), ("c2", 3)]})
        LAST.update({("wc",): ("oc", KD - 1, 1)})
        LAST.update({("gate", m): ("gc", m, 1) for m in range(KD)})
        LAST.update({("wout", h): ("mix", TILES - 1, h) for h in range(2)})
        vals_used = sem("vals_used")
        VORD = [("c0", 0), ("c1", 0), ("c1", 1), ("c2", 0), ("c2", 1), ("c2", 2), ("c2", 3)]

        COPY_AT = [("k", 0, 0), ("k", 2, 0), ("v", 0, 0), ("v", 2, 0), ("S", 4), ("S", 16), ("ga", 1, 0), ("ga", 4, 0)]
        U_OUTS = 2
        COPIES = 5 * NB
        KV_OUTS = 2 * (4 * 2 + 2 + 4)
        gather_ticks = sem("gather_ticks")
        ohs_used, dve_loop = sem("ohs_used"), sem("dve_loop")
        sact = at(A_R + 2760, 256)
        wtab = at(A_R + 3020, NBLK)
        addrow = arena[:, A_R + 3124:A_R + 3124 + NBLK].bitcast(U32)
        addf = at(A_R + 3230, NBLK)

        block = ctx.enter_context(nc.Block())

        @block.sync
        def _(sp):
            def load(key):
                s = slot_of(key)
                before = None
                for k, q in LOADS:
                    if k == key:
                        break
                    if q == s:
                        before = k
                if before is not None:
                    if before[0] == "V" and before != ("V", "c2", 3):
                        sp.wait_ge(vals_used, VORD.index(before[1:]) + 1)
                    else:
                        sp.wait_ge(fills_done, INDEX[LAST[before]] + 1)
                if key == ("K", "c2", 0):
                    sp.wait_ge(fills_done, INDEX[("bT", PT_ - 1)] + 1)
                to, done = slot[s], slot_in[s]
                if key[0] == "ada":
                    g = key[1]
                    sp.dma_start(to.rearrange("p (k n) -> p k n", k=KD),
                                 w_ada[0].rearrange("(p k) n -> p k n", k=KD)[:, :, 512 * g:512 * g + 512]
                                 ).then_inc(done, 16)
                elif key[0] == "in":
                    g = key[1]
                    sp.dma_start(to.rearrange("p (k n) -> p k n", k=KD),
                                 w_in[0].rearrange("(p k) n -> p k n", k=KD)[:, :, 512 * g:512 * g + 512]
                                 ).then_inc(done, 16)
                elif key[0] in "KV":
                    kv = "KV".index(key[0])
                    if key[1] == "c0":
                        sp.dma_start(to[:, 0:1024].rearrange("p (b c) -> p b c", b=NB),
                                     cache_c[0, :, :, kv, :, :].rearrange("b i h d -> i b (h d)")).then_inc(done, 16)
                        sp.dma_start(to[:, 1024:3072].rearrange("p (b c) -> p b c", b=NB),
                                     cache_b1[0, :, :, kv, :, :].rearrange("b i h d -> i b (h d)")).then_inc(done, 16)
                    elif key[1] == "c1":
                        for b in range(4):
                            sp.dma_start(to[:, 1024 * b:1024 * b + 1024].rearrange("p (r c) -> p r c", r=4),
                                         cache_b2[0, 4 * key[2] + b, :, kv, :, :].rearrange(
                                             "(i r) h d -> i r (h d)", r=4)).then_inc(done, 16)
                    else:
                        for b in range(2):
                            sp.dma_start(to[:, 2048 * b:2048 * b + 2048].rearrange("p (r c) -> p r c", r=8),
                                         cache_b3[0, 2 * key[2] + b, :, kv, :, :].rearrange(
                                             "(i r) h d -> i r (h d)", r=16)[:, 0:8, :]).then_inc(done, 16)
                elif key[0] == "wc":
                    sp.dma_start(to.rearrange("p (k n) -> p k n", k=4),
                                 w_c_up[0].rearrange("(k p) n -> p k n", p=P)).then_inc(done, 16)
                elif key[0] == "gate":
                    for j in range(3):
                        c = GATE0 + j * D + key[1] * P
                        sp.dma_start(to[:, 1024 * j:1024 * j + 1024].rearrange("p (k n) -> p k n", k=KD),
                                     w_in[0].rearrange("(p k) n -> p k n", k=KD)[:, :, c:c + P]).then_inc(done, 16)
                elif key[0] == "wout":
                    sp.dma_start(to.rearrange("p (k n) -> p k n", k=KD),
                                 w_out[0].rearrange("(k p) n -> p k n", p=P)[:, :, 512 * key[1]:512 * key[1] + 512]
                                 ).then_inc(done, 16)
                elif key[0] == "wsgu":
                    sp.dma_start(to[:, 0:2048], ws_gate[0].rearrange("(p k) n -> p (k n)", k=KD)).then_inc(done, 16)
                    sp.dma_start(to[:, 2048:4096], ws_up[0].rearrange("(p k) n -> p (k n)", k=KD)).then_inc(done, 16)
                elif key[0] == "wsd":
                    sp.dma_start(to[:, 0:2048], ws_down[0].rearrange("(p k) n -> p (k n)", k=2)).then_inc(done, 16)
                    sp.dma_start(to[:, 2048:2560].rearrange("p (k n) -> p k n", k=KD),
                                 w_router[0].rearrange("(p k) n -> p k n", k=KD)).then_inc(done, 16)

            sp.dma_start(crow[0:1, 0:D], c_prompt[:, :]).then_inc(crow_in, 16)
            sp.dma_start(crow[1:9, 0:D], c_sample[:, :]).then_inc(crow_in, 16)
            sp.dma_start(ident[:], const[:, 0:P]).then_inc(consts_in, 16)
            load(("ada", 0))
            sp.dma_start(misc[:], const[:, 3 * P:4 * P]).then_inc(consts_in, 16)
            sp.dma_start(recip[:], const[:, 4 * P:4 * P + 64].rearrange("p (g n) -> p g n", g=4)
                         ).then_inc(consts_in, 16)
            load(("ada", 1))
            sp.dma_start(xall[:, 0:PT_, :], x_prompt[0].rearrange("(t p) d -> p t d", p=P)).then_inc(x_in, 16)
            sp.dma_start(xall[0:NS, PT_, :], x_sample.rearrange("b t d -> (b t) d")).then_inc(x_in, 16)
            load(("ada", 2))
            load(("ada", 3))
            sp.dma_start(oh_top[0:BINS, :], onehot_top).then_inc(onehots_in, 16)
            sp.dma_start(oh_smp[0:BINS, :], onehot_smp).then_inc(onehots_in, 16)
            sp.dma_start(relT[0:32, :], rel_bias).then_inc(onehots_in, 16)
            sp.dma_start(ada[0:9, :], b_ada.broadcast_to([9, 6 * D])).then_inc(badd_in, 16)
            for n, g in enumerate((g_pre_mix, g_post_mix, g_pre_ffn, g_post_ffn)):
                sp.dma_start(gains[0:9, n * D:(n + 1) * D], g.broadcast_to([9, D])).then_inc(gains_in, 16)
            sp.dma_start(sinkb[:], sinks.broadcast_to([P, 8])).then_inc(gains_in, 16)
            for b in range(2):
                sp.dma_start(sinkr[64 * b:64 * b + 64, :],
                             bass.AP(tensor=sinks.tensor, offset=sinks.offset, ap=[[1, 8], [0, 8], [1, 1]])
                             ).then_inc(gains_in, 16)
            sp.dma_start(pscale[:], pool_scale[0].rearrange("(m p) -> p m", p=P), allow_slow_non_contiguous=True).then_inc(gains_in, 16)
            for g in range(4, 7):
                load(("ada", g))
            sp.wait_ge(mods_rows, 1)
            sp.dma_start(mods[:, 0:2, :], ada[0:9, 0:2 * D].rearrange("p (a b) -> p a b", b=D)).then_inc(mods_out, 16)
            sp.wait_ge(mods_out, 16)

            def sample_rows(q):
                return bass.AP(tensor=mods.tensor, offset=(6 + q) * D, ap=[[6 * D, NB], [0, NT], [1, D]])

            def spread(to, rows, done):
                for n, q in enumerate(rows):
                    sp.dma_start(to[:, 2 * n, :], mods[0:1, q, :].broadcast_to([P, D])).then_inc(done, 16)
                    sp.dma_start(to[0:NS, 2 * n + 1, :], sample_rows(q)).then_inc(done, 16)

            spread(modb, (1, 0), modb_in)
            for g in range(7, 12):
                load(("ada", g))
            sp.dma_start(staterow[0:NB * PSTATE, :], state_pool[0].rearrange("b t c -> (b t) c")).then_inc(state_in, 16)
            for g in range(4):
                load(("in", g))
            wait_emptied(sp, ("gtab", 2))
            for n, h0, h1 in ((0, 0, 4), (1, 4, 8), (2, 8, 12), (0, 12, 20)):
                sp.dma_start(toep[h0:h1], gtab[h0:h1, n * GW:(n + 1) * GW].unsqueeze(1).broadcast_to(
                    [h1 - h0, P, GW])).then_inc(tables_out, 16)
            wait_emptied(sp, ("stab", 6))
            for n, h0, h1 in ((0, 0, 4), (1, 4, 8), (2, 8, 12), (0, 12, 20)):
                sp.dma_start(sbias[h0:h1].rearrange("h t k -> h (t k)"),
                             stab[h0:h1, n * NT * NK:(n + 1) * NT * NK]).then_inc(tables_out, 16)
            sp.wait_ge(mods_rows, 2)
            sp.dma_start(mods[:, 2:6, :], ada[0:9, 2 * D:6 * D].rearrange("p (a b) -> p a b", b=D)).then_inc(mods_out, 16)
            for g in range(4, 7):
                load(("in", g))
            sp.wait_ge(tables_out, 16 * 8)
            for n in range(8):
                for j in range(2 if n < 2 or n > 3 else 4):
                    if n < 2:
                        h, off, w, pos = n + 2 * j, 127, 256, 256 * j
                    elif n < 4:
                        h, off, w, pos = 4 * (n - 1) + j // 2 + 2 * (j % 2), 255, 128, 128 * j
                    else:
                        h, off, w, pos = 12 + 2 * (n - 4) + j, 127, 256, 256 * j
                    sp.dma_start(biasP[:, n, pos:pos + w],
                                 bass.AP(tensor=toep.tensor, offset=h * P * GW + off, ap=[[GW - 1, P], [1, w]])
                                 ).then_inc(biasp_in, 16)
            wait_emptied(sp, ("uout", 1))
            sp.dma_start(pool_p[0, 0], uouts[0:PSTATE, 0, :]).then_inc(u_out, 16)
            sp.dma_start(bass.AP(tensor=pool_s.tensor, offset=pool_s.offset + (PSTATE - NT) * 512,
                                 ap=[[PSTATE * 512, NB], [512, NT], [1, 512]]), uouts[0:NS, 1, :]).then_inc(u_out, 16)
            for t in range(TILES):
                for g in range(3):
                    wait_emptied(sp, ("k", g, t))
                    wait_emptied(sp, ("v", g, t))
                wait_emptied(sp, ("kvc", t))
                for kv, src in ((0, kTM), (1, vTM)):
                    if t < PT_:
                        for g in (1, 2):
                            sp.dma_start(outs_p[g][0, 0, :, kv, :, :].rearrange("(i j) h d -> j i (h d)", j=4)[t],
                                         src[:, t, 256 * g:256 * g + 256]).then_inc(kv_out, 16)
                    if t == PT_ - 1:
                        sp.dma_start(b1_p[0, 0, :, kv, :, :].rearrange("i h d -> i (h d)"),
                                     src[:, t, 0:256]).then_inc(kv_out, 16)
                        sp.dma_start(c_p[0, 0, :, kv, :, :].rearrange("i h d -> i (h d)"),
                                     src[:, t, 768:896]).then_inc(kv_out, 16)
                    if t == PT_:
                        for o, n, w, c in [(outs_s[g], CACHE[g], 256, 256 * g) for g in range(3)] + [(c_s, P, 128, 768)]:
                            sp.dma_start(bass.AP(tensor=o.tensor, offset=o.offset + (n - NT) * 2 * w + kv * w,
                                                 ap=[[n * 2 * w, NB], [2 * w, NT], [1, w]]),
                                         src[0:NS, t, c:c + w]).then_inc(kv_out, 16)
            kload = [k for k, _ in LOADS if k[0] == "K"]
            for key in kload[:3]:
                load(key)
            sp.wait_ge(stage_ready, 16)
            for g in (1, 2):
                for t in range(PT_):
                    sp.dma_start(fold[g - 1].rearrange("(i j) c -> j i c", j=4)[t],
                                 stage[:, g, t * 264:(t + 1) * 264]).then_inc(stage_out, 16)
            sp.wait_ge(stage_out, 16 * 8)
            for g in (1, 2):
                sp.dma_start(stage[:, g, :].rearrange("p (t c) -> p t c", t=PT_),
                             fold[g - 1].rearrange("(t p) c -> p t c", p=P)).then_inc(stage_in, 16)
            sp.wait_ge(fills_done, INDEX[("O", len(UNITS) - 1)] + 1)
            wait_emptied(sp, ("O", len(UNITS) - 1))
            for n in range(7):
                reps, rows, h = (NB, 2 * NT, 2 * n) if n < 6 else (2, 8 * NT, 12)
                sp.dma_start(biasRaw[:, n, :],
                             bass.AP(tensor=sbias.tensor, offset=h * NT * NK, ap=[[0, reps], [NK, rows], [1, NK]])
                             ).then_inc(biass_in, 16)
            for key in kload[3:]:
                load(key)
            for key, _ in LOADS:
                if key[0] == "V":
                    load(key)
            sp.wait_ge(fills_done, INDEX[("SnC",)] + 1)
            sp.dma_start(wb, w_b_up[0].rearrange("(k p) n -> p k n", p=P)).then_inc(merge_in, 16)
            sp.dma_start(pw, pool_w[0].rearrange("g c o -> c g o")).then_inc(merge_in, 16)
            load(("wc",))
            for m in range(KD):
                load(("gate", m))
            load(("wout", 0))
            load(("wout", 1))
            sp.wait_ge(mix_ready, 2 * KD)
            sp.dma_start(x1[:, 0:PT_, :], x_prompt[0].rearrange("(t p) d -> p t d", p=P)).then_inc(xres_in, 16)
            sp.dma_start(x1[0:NS, PT_, :], x_sample.rearrange("b t d -> (b t) d")).then_inc(xres_in, 16)
            sp.wait_ge(mods_out, 32)
            spread(gmod, (2,), gmod_in)
            spread(modf, (4, 3), modf_in)
            sp.dma_start(const2, const[:, P:3 * P].rearrange("p (a b) -> p a b", b=P)).then_inc(moe_in, 16)
            sp.dma_start(rbias, router_bias.broadcast_to([P, NE])).then_inc(moe_in, 16)
            load(("wsgu",))
            load(("wsd",))
            for t in range(TILES):
                n = parts(t)
                sp.wait_ge(h_ready, TILES + t + 1)
                sp.dma_start(h2rows[toks(t), :], hbuf2[0:n, t % 2, :]).then_inc(h2_out, 16)
                if t + 1 < TILES:
                    sp.wait_ge(h2_out, 16 * (t + 1))
            for t in range(TILES):
                wait_emptied(sp, ("sy", t, 1))
                sp.dma_start(yacc[toks(t), :], ysh[0:parts(t), t, :]).then_inc(yacc_in, 16)
            sp.dma_start(yacc[TOK:TOK + P, :], ysh[:, 0, :]).then_inc(yacc_in, 16)
            sp.wait_ge(fills_done, INDEX[("sy", TILES - 1, 1)] + 1)
            sp.wait_ge(tables_ready, 1)
            n_pairs = sp.value_load(pairs[0:1, 0:1], min_val=1, max_val=NBLK // 2)
            with sp.Fori(0, n_pairs) as i:
                for j in range(2):
                    e = sp.value_load(bexp[0:1, bass.ds(2 * i + j, 1)], min_val=0, max_val=NE - 1)
                    sp.wait_ge(gu_done, 2 * i + j + 1)
                    sp.dma_start(wexp[j][:, 0:2048],
                                 we_gate[0, bass.ds(e, 1)].rearrange("a (p k) n -> p (a k n)", k=KD)
                                 ).then_inc(wgu_in[j], 16)
                    sp.dma_start(wexp[j][:, 2048:4096],
                                 we_up[0, bass.ds(e, 1)].rearrange("a (p k) n -> p (a k n)", k=KD)
                                 ).then_inc(wgu_in[j], 16)
                    sp.wait_ge(d_done, 2 * i + j + 1)
                    sp.dma_start(wexp[j][:, 4096:6144],
                                 we_down[0, bass.ds(e, 1)].rearrange("a (p k) n -> p (a k n)", k=2)
                                 ).then_inc(wd_in[j], 16)
            sp.wait_ge(d_done, 2 * n_pairs + 2)
            sp.dma_start(g2mod[:, 0, :], mods[0:1, 5, :].broadcast_to([P, D])).then_inc(g2_in, 16)
            sp.dma_start(g2mod[0:NS, 1, :], sample_rows(5)).then_inc(g2_in, 16)
            for j in range(2):
                sp.wait_ge(y_out[j], 16 * n_pairs)
            for t in range(TILES):
                sp.dma_start(ysh[0:parts(t), t, :], yacc[toks(t), :]).then_inc(f_in[t], 16)
            for j in range(2):
                sp.wait_ge(xg_in[j], 16 * n_pairs + 16)
            for t in range(TILES):
                sp.wait_ge(f_out, t + 1)
                if t < PT_:
                    sp.dma_start(y_p[0, toks(t), :], x1[:, t, :]).then_inc(kv_out, 16)
                else:
                    sp.dma_start(y_s.rearrange("b t d -> (b t) d"), x1[0:NS, t, :]).then_inc(kv_out, 16)
            sp.wait_ge(kv_out, 16 * (KV_OUTS + TILES))
            sp.wait_ge(u_out, 16 * U_OUTS)
            sp.wait_ge(copies_out, 16 * COPIES)

        @block.gpsimd
        def _(pool):
            steps = [0]

            def link(ins):
                steps[0] += 1
                ins.then_inc(pool_step, 1)
                pool.wait_ge(pool_step, steps[0])

            for t in range(TILES):
                n = parts(t)
                s = t // PT_
                pool.wait_ge(hA_ready, t + 1)
                if t == 0:
                    pool.wait_ge(modb_in, 16 * 4)
                pool.tensor_tensor(hbuf[0:n, t % 2, :], hbuf[0:n, t % 2, :], modb[0:n, 2 + s, :],
                                   ALU.add).then_inc(h_ready, 1)
            for g, win in enumerate(POOLW):
                for h in range(2):
                    wait_emptied(pool, ("u", g, h))
                if g == 0:
                    wait_emptied(pool, ("state",))
                    pool.wait_ge(ubuf_ready, 1)
                u = uext[:, g, :]
                src = u
                w = 1
                n = 0
                while w < win:
                    dst = ping[:, n % 2, :]
                    lo = 2 * w - 1
                    pool.tensor_tensor(dst[:, lo:528], src[:, lo:528], src[:, lo - w:528 - w], ALU.add)
                    sv = src[:, 528:UE].rearrange("p (b t) -> p b t", b=NB)
                    dv = dst[:, 528:UE].rearrange("p (b t) -> p b t", b=NB)
                    link(pool.tensor_tensor(dv[:, :, lo:], sv[:, :, lo:], sv[:, :, lo - w:PSTATE + NT - w], ALU.add))
                    src = dst
                    w *= 2
                    n += 1
                m = ping[:, n % 2, :]
                pool.wait_ge(consts_in, 48)
                pool.tensor_tensor(m[:, 16:32], src[:, 16:32], recip[:, g, :], ALU.mult)
                pool.tensor_scalar(m[:, 32:528], src[:, 32:528], 1.0 / win, 0.0, ALU.mult, ALU.add)
                mv = m[:, 528:UE].rearrange("p (b t) -> p b t", b=NB)
                sv = src[:, 528:UE].rearrange("p (b t) -> p b t", b=NB)
                link(pool.tensor_scalar(mv[:, :, PSTATE:], sv[:, :, PSTATE:], 1.0 / win, 0.0, ALU.mult, ALU.add))
                pool.wait_ge(mods_out, 32)
                pool.tensor_tensor(zT[:, g, 0:SEQ], m[:, 16:528], u[:, 16:528], ALU.subtract)
                uv = u[:, 528:UE].rearrange("p (b t) -> p b t", b=NB)
                last = pool.tensor_tensor(zT[:, g, SEQ:TOK].rearrange("p (b t) -> p b t", b=NB),
                                          mv[:, :, PSTATE:], uv[:, :, PSTATE:], ALU.subtract)
                if g < 3:
                    link(last)
                else:
                    last.then_inc(z_ready, 1)
            for b in range(NB):
                wait_fill(pool, COPY_AT[b])
                for c, o, n in ((cache_b3, b3_s, CACHE[2]), (cache_b2, b2_s, CACHE[1]),
                                (cache_b1, b1_s, CACHE[0]), (cache_c, c_s, P)):
                    pool.dma_start(o[0, b, 0:n - NT].rearrange("i v h d -> i (v h d)"),
                                   c[0, b, NT:n].rearrange("i v h d -> i (v h d)")).then_inc(copies_out, 16)
                pool.dma_start(pool_s[0, b, 0:PSTATE - NT, :], state_pool[0, b, NT:PSTATE, :]).then_inc(copies_out, 16)
            for t in range(TILES):
                n = parts(t)
                s = t // PT_
                pool.wait_ge(hA_ready, TILES + t + 1)
                pool.tensor_tensor(hbuf2[0:n, t % 2, :], hbuf2[0:n, t % 2, :], modf[0:n, 2 + s, :],
                                   ALU.add).then_inc(h_ready, 1)
            pool.wait_ge(h2_out, 16 * TILES)
            pool.wait_ge(tables_ready, 1)
            pool.wait_ge(yacc_in, 16 * (TILES + 1))
            n_pairs = pool.value_load(pairs[0:1, 0:1], min_val=1, max_val=NBLK // 2)
            pool.sem_inc(added, 2)

            for j in range(2):
                pool.tensor_copy(icol[:, j:j + 1], rowtok[:, j:j + 1]).then_inc(icol_ready, 1)
                pool.wait_ge(icol_ready, j + 1)
                pool.indirect_dma_start(xg[:, j, :], None, h2rows,
                                        bass.IndirectOffsetOnAxis(ap=icol[:, j:j + 1], axis=0)
                                        ).then_inc(xg_in[j], 16)
            with pool.Fori(0, n_pairs) as i:
                for j in range(2):
                    pool.wait_ge(t_done, 2 * i + j + 3)
                    pool.tensor_copy(icol[:, j:j + 1], rowtok[:, bass.ds(2 * i + j + 2, 1)]).then_inc(icol_ready, 1)
                    pool.wait_ge(icol_ready, 2 * i + j + 3)
                    pool.sem_inc(gather_ticks, 1)
                    pool.indirect_dma_start(xg[:, j, :], None, h2rows,
                                            bass.IndirectOffsetOnAxis(ap=icol[:, j:j + 1], axis=0)
                                            ).then_inc(xg_in[j], 16)
                for j in range(2):
                    pool.tensor_copy(scol[:, j:j + 1], addrow[:, bass.ds(2 * i + j, 1)]).then_inc(cols_ready, 1)
                    pool.tensor_copy(wcol[:, j:j + 1], wtab[:, bass.ds(2 * i + j, 1)]).then_inc(cols_ready, 1)
                pool.wait_ge(cols_ready, 4 * i + 4)
                for j in range(2):
                    pool.wait_ge(y_act, 2 * i + j + 2)
                    pool.wait_ge(y_dve, 2 * i + j + 2)
                    pool.sem_inc(gather_ticks, 1)
                    pool.indirect_dma_start(yacc, bass.IndirectOffsetOnAxis(ap=scol[:, j:j + 1], axis=0),
                                            yb[:, j, :], None, compute_op=ALU.add).then_inc(y_out[j], 16)
                    pool.wait_ge(y_out[j], 16 * i + 16)
                    pool.sem_inc(added, 1)

        @block.scalar
        def _(act):
            steps = [0]

            def link(ins):
                steps[0] += 1
                ins.then_inc(act_step, 1)
                act.wait_ge(act_step, steps[0])

            def empty(key, out, pick=lambda b: b):
                bank = wait_fill(act, key)
                act.activation(out, pick(bank), ACT.Copy).then_inc(emptied["A"], 1)

            act.wait_ge(crow_in, 32)
            act.activation(crow[0:9, D:2 * D], crow[0:9, 0:D], ACT.Exp, scale=-1.0).then_inc(c_exp, 1)

            def norm_stats(n, src, junk_to):
                for t in range(TILES):
                    r = parts(t)
                    if t:
                        act.wait_ge(ssq_ready, TILES * n + t)
                    act.activation(junk_to[0:r, :], src[0:r, t, :], ACT.Square,
                                   accum_out=stat[0:r, n, t:t + 1]).then_inc(ssq_ready, 1)
                act.wait_ge(ms_ready, n + 1)
                act.activation(stat[:, n, :], stat[:, n, :], ACT.Sqrt).then_inc(root_ready, 1)

            act.wait_ge(x_in, 32)
            act.wait_ge(ubuf_ready, 1)
            norm_stats(0, xall, junk)
            for n in range(7):
                w = min(480, 3 * NT * NK - 480 * n)
                empty(("stab", n), stab[0:20, 480 * n:480 * n + w], lambda b: b[0:20, 0:w])

            def scaled_rows(first, n, src, hb, keys):
                act.wait_ge(rn_ready, n + 1)
                for t in range(TILES + 1):
                    if t < TILES:
                        r = parts(t)
                        if t >= 2:
                            wait_fill(act, (keys, t - 2, 1))
                            if first:
                                act.wait_ge(h2_out, 16 * (t - 1))
                        act.activation(hb[0:r, t % 2, :], src[0:r, t, :], ACT.Copy,
                                       scale=stat[0:r, n, t:t + 1]).then_inc(xn_ready, 1)
                    if t >= 1:
                        u = t - 1
                        r = parts(u)
                        empty((keys, u, 0), (h2T if first else hT)[:, 0:4, toks(u)],
                              lambda b: b[:, 0:4 * r].rearrange("p (k n) -> p k n", k=4))

            scaled_rows(0, 0, xall, hbuf, "hT")
            act.wait_ge(mods_rows, 2)
            for c in range(4):
                empty(("u", c, 0), uext[:, c, 16:304], lambda b: b[:, 0:288])
            for c in range(6):
                empty(("q", c, 0), qT[:, c, 0:288], lambda b: b[:, 0:288])
            for g in range(3):
                for t in range(0, TILES, 2):
                    r = parts(t)
                    empty(("k", g, t), kTM[0:r, t, 256 * g:256 * g + 256], lambda b: b[0:r, 0:256])
            act.wait_ge(mods_out, 32)
            for g in range(3):
                for t in range(0, TILES, 2):
                    r = parts(t)
                    empty(("v", g, t), vTM[0:r, t, 256 * g:256 * g + 256], lambda b: b[0:r, 0:256])
            for c in range(6, 10):
                bank = wait_fill(act, ("q", c, 0))
                for e in range(2):
                    h = 2 * (c - 6) + e
                    ins = act.activation(qT[64 * (h // 4):64 * (h // 4) + 64, 6 + h % 4, 0:288],
                                         bank[64 * e:64 * e + 64, 0:288], ACT.Copy)
                ins.then_inc(emptied["A"], 1)
            for t in range(0, TILES, 2):
                r = parts(t)
                bank = wait_fill(act, ("kvc", t))
                act.activation(kTM[0:r, t, 768:896], bank[0:r, 0:128], ACT.Copy)
                act.activation(vTM[0:r, t, 768:896], bank[0:r, 128:256], ACT.Copy).then_inc(emptied["A"], 1)
            act.wait_ge(z_ready, 1)
            empty(("uout", 0), uouts[0:PSTATE, 0, :], lambda b: b[0:PSTATE, :])
            empty(("uout", 1), uouts[0:NS, 1, :], lambda b: b[0:NS, :])
            act.wait_ge(tables_out, 16 * 8)
            for m in range(0, 7, 2):
                empty(("kT", m), kT[:, m, 0:SEQ])

            act.wait_ge(u_out, 16 * U_OUTS)
            for s in range(len(UNITS) + LAGO):
                u = s - LAGT
                if 0 <= u < len(UNITS):
                    if u >= 2:
                        wait_fill(act, ("O", u - 2))
                    nb = 2 * len(key_blocks(UNITS[u]))
                    empty(("T", u), pTb[:, u % 2, 0:P * nb], lambda b: b[:, 0:P * nb])
                if s < len(UNITS):
                    kind, t, p = UNITS[s]
                    w = head_cols(UNITS[s])
                    lo = key_blocks(UNITS[s])[0][1]
                    act.wait_ge(max_ready, s + 1)
                    if kind == "C":
                        for h in range(2):
                            act.activation(dsk[:, s % 4, h:h + 1], sinkb[:, 2 * p + h:2 * p + h + 1], ACT.Exp,
                                           scale=-1.0, bias=nmx[:, s % 4, h:h + 1])
                    for h in range(2):
                        v = sbuf_[:, s % 3, h * w + lo:(h + 1) * w]
                        ins = act.activation(v, v, ACT.Exp, bias=nmx[:, s % 4, h:h + 1],
                                             accum_out=den[:, s % 4, h:h + 1])
                    ins.then_inc(probs_ready, 1)
                if s - LAGO == COMBINE_AT:
                    act.wait_ge(cm_ready, 1)
                    act.activation(cmb[:, 1:4, :], cmb[:, 1:4, :], ACT.Exp).then_inc(ce_ready, 1)
                for key in after_unit(s - LAGO):
                    if key[0] == "ocT":
                        empty(key, ocT[:, :, toks(key[1])], lambda b: b[:, :].rearrange("p (c n) -> p c n", c=4))
                    else:
                        empty(key, bT[:, :, toks(key[1])], lambda b: b[:, 0:256].rearrange("p (c n) -> p c n", c=2))

            empty(("Sn", 0), stBn[0:NS, 0:4, :], lambda b: b[0:NS, :].rearrange("p (c n) -> p c n", c=4))
            empty(("Sn", 1), stBn[0:NS, 4:6, :], lambda b: b[0:NS, 0:256].rearrange("p (c n) -> p c n", c=2))
            empty(("SnC",), stCn[0:NS, :], lambda b: b[0:NS, :])
            for s in range(NKF + 1):
                if s < NKF and s % 2 == 0:
                    if s >= 4:
                        act.wait_ge(keys_used, s - 3)
                    empty(("KT", s), ktr[:, s % 4, :])
                if s - 1 == 1:
                    empty(("SM", 2), stC)
                if s - 1 == 21:
                    empty(("SM", 0), stB[:, 0:4, :], lambda b: b[:, :].rearrange("p (c n) -> p c n", c=4))
                if s - 1 == NKF - 1:
                    empty(("SM", 1), stB[:, 4:6, :], lambda b: b[:, 0:256].rearrange("p (c n) -> p c n", c=2))
            act.wait_ge(smax_ready, 1)
            act.activation(sst[:, 2, :], sst[:, 0, :], ACT.Exp, bias=sinkr[:, 0:1])
            for c in range(4):
                act.activation(sC[:, c, :], sC[:, c, :], ACT.Exp, bias=sst[:, 0, c:c + 1],
                               accum_out=sst[:, 1, c:c + 1])
            act.wait_ge(smax_ready, 2)
            for p in range(2):
                ins = act.activation(sB[:, p, :], sB[:, p, :], ACT.Exp, bias=sst[:, 3, p:p + 1],
                                     accum_out=sst[:, 4, p:p + 1])
            ins.then_inc(sexp_ready, 1)
            empty(("PTC",), pC)
            for p in range(2):
                empty(("PT", p), pB[:, 3 * p:3 * p + 3, :],
                      lambda b: b[:, 0:3 * P].rearrange("p (c n) -> p c n", c=3))

            for m in range(KD):
                for h in range(2):
                    n = 2 * m + h
                    for j, what in enumerate(("ga", "gb", "gc")):
                        if j == 0 and n >= 2:
                            act.wait_ge(mix_ready, n - 1)
                        bank = wait_fill(act, (what, m, h))
                        act.activation(gsig[:, 3 * h + j, :], bank[:, 0:288], ACT.Exp,
                                       scale=-1.0).then_inc(emptied["A"], 1)
            for h in range(2):
                for t in range(0, TILES, 2):
                    r = parts(t)
                    empty(("mix", t, h), mixed[0:r, t, 512 * h:512 * h + 512], lambda b: b[0:r, :])
            wait_emptied(act, ("mix", TILES - 1, 1))
            wait_emptied(act, ("mix", TILES - 2, 1))
            norm_stats(1, mixed, junk2)
            act.wait_ge(x1_ready, TILES)
            norm_stats(2, x1, junk2)
            scaled_rows(1, 2, x1, hbuf2, "h2T")

            for t in range(TILES):
                r = parts(t)
                bank = wait_fill(act, ("rt", t))
                act.activation(scores[0:r, t, :], bank[0:r, 0:NE], ACT.Exp, scale=-1.0).then_inc(emptied["A"], 1)

            def shared_rest(t):
                r = parts(t)
                empty(("saT", t), saT[:, :, 0:r], lambda b: b[:, 0:2 * r].rearrange("p (k n) -> p k n", k=2))
                for h in range(2):
                    empty(("sy", t, h), ysh[0:r, t, 512 * h:512 * h + 512], lambda b: b[0:r, :])

            for t in range(TILES):
                r = parts(t)
                bank = wait_fill(act, ("sgu", t))
                if t >= 1:
                    act.wait_ge(sact_ready, t)
                act.activation(sgat[0:r, 0, :], bank[0:r, 0:FF], ACT.Exp, scale=-1.0)
                act.activation(sgat[0:r, 1, :], bank[0:r, 0:FF], ACT.Copy)
                act.activation(sgat[0:r, 2, :], bank[0:r, FF:2 * FF], ACT.Copy).then_inc(emptied["A"], 1)
                if t >= 1:
                    shared_rest(t - 1)
            shared_rest(TILES - 1)

            act.wait_ge(tables_ready, 1)
            n_pairs = act.value_load(pairs[0:1, 0:1], min_val=1, max_val=NBLK // 2)
            with act.Fori(0, n_pairs) as i:
                for j in range(2):
                    act.wait_ge(t_done, 2 * i + j + 3)
                    act.activation(xT[:, j, 0:512], psb[2 * j][:, :], ACT.Copy).then_inc(xt_act, 1)
                for j in range(2):
                    act.wait_ge(gu_done, 2 * i + j + 3)
                    act.activation(act3[:, 3 * j, :], psb[4 + j][:, 0:FF], ACT.Exp, scale=-1.0).then_inc(e_ready, 1)
                for j in range(2):
                    act.wait_ge(at_done, 2 * i + j + 1)
                    act.activation(aT[:, j, :], psb[j][:, 0:2 * P], ACT.Copy).then_inc(at_ready, 1)
                    act.wait_ge(added, 2 * i + j + 1)
                    act.wait_ge(d_done, 2 * i + j + 3)
                    act.wait_ge(cols_ready, 4 * i + 2 * j + 2)
                    act.activation(yb[:, j, 0:512], psb[6 if j == 0 else 2][:, :], ACT.Copy,
                                   scale=wcol[:, j:j + 1]).then_inc(y_act, 1)

            for t in range(TILES):
                r = parts(t)
                act.wait_ge(f_in[t], 16)
                act.activation(junk2[0:r, :], ysh[0:r, t, :], ACT.Square,
                               accum_out=stat[0:r, 3, t:t + 1]).then_inc(f_ssq, 1)
                act.wait_ge(f_root, t + 1)
                act.activation(stat[0:r, 3, t:t + 1], stat[0:r, 3, t:t + 1], ACT.Sqrt).then_inc(f_rn, 1)

        @block.vector
        def _(dve):
            steps = [0]

            def link(ins):
                steps[0] += 1
                ins.then_inc(dve_step, 1)
                dve.wait_ge(dve_step, steps[0])

            def empty(key, out, pick=lambda b: b):
                bank = wait_fill(dve, key)
                dve.tensor_copy(out, pick(bank)).then_inc(emptied["D"], 1)

            dve.memset(relT[32:33, :], MASK).then_inc(onehot_ready, 1)
            dve.memset(stat[:], 1.0).then_inc(ubuf_ready, 1)
            dve.wait_ge(c_exp, 1)
            ce = crow[0:9, D:2 * D]
            link(dve.tensor_scalar(ce, ce, 1.0, None, ALU.add))
            link(dve.reciprocal(ce, ce))
            dve.tensor_tensor(crow[0:9, 0:D], crow[0:9, 0:D], ce, ALU.mult).then_inc(c_silu, 1)
            empty(("cT",), cT, lambda b: b[:, 0:P].rearrange("p (k n) -> p k n", k=KD)[:, :, 0:9])
            dve.wait_ge(gains_in, 16 * 8)
            link(dve.tensor_scalar(sinkb[:], sinkb[:], -1.0, None, ALU.mult))
            dve.wait_ge(badd_in, 16)

            def ada_group(g):
                bank = wait_fill(dve, ("ada", g))
                v = ada[0:9, 512 * g:512 * g + 512]
                dve.tensor_tensor(v, bank[0:9, :], v, ALU.add).then_inc(emptied["D"], 1)

            def ada_row(q, gain, plus, mark):
                v = ada[0:9, q * D:(q + 1) * D]
                wait_emptied(dve, ("ada", 2 * q + 1))
                ins = dve.scalar_tensor_tensor(v, v, plus, gains[0:9, gain * D:(gain + 1) * D], ALU.add, ALU.mult)
                if mark:
                    ins.then_inc(mods_rows, 1)

            def norm_root(n):
                dve.wait_ge(ssq_ready, TILES * (n + 1))
                dve.tensor_scalar(stat[:, n, :], stat[:, n, :], 1.0 / D, EPS, ALU.mult, ALU.add).then_inc(ms_ready, 1)
                dve.wait_ge(root_ready, n + 1)
                dve.reciprocal(stat[:, n, :], stat[:, n, :]).then_inc(rn_ready, 1)

            for g in range(4):
                ada_group(g)
            ada_row(1, 0, 1.0, True)
            norm_root(0)
            for n in range(3):
                empty(("gtab", n), gtab[0:20, n * GW:(n + 1) * GW], lambda b: b[0:20, 0:GW])
            for g in range(4, 8):
                ada_group(g)

            for t in range(TILES):
                r, s = parts(t), t // PT_
                if t == 0:
                    dve.wait_ge(modb_in, 16 * 4)
                dve.wait_ge(xn_ready, t + 1)
                dve.tensor_tensor(hbuf[0:r, t % 2, :], hbuf[0:r, t % 2, :], modb[0:r, s, :],
                                  ALU.mult).then_inc(hA_ready, 1)
                if t >= 1:
                    u = t - 1
                    w = parts(u)
                    empty(("hT", u, 1), hT[:, 4:8, toks(u)], lambda b: b[:, 0:4 * w].rearrange("p (k n) -> p k n", k=4))
                    ada_group(8 + u)
            empty(("hT", PT_, 1), hT[:, 4:8, SEQ:TOK], lambda b: b[:, 0:4 * NS].rearrange("p (k n) -> p k n", k=4))
            ada_row(2, 1, 0.0, False)
            ada_row(4, 2, 1.0, False)
            ada_row(5, 3, 0.0, True)
            dve.wait_ge(mods_rows, 2)
            dve.memset(uext[:, :, 0:16], 0.0)
            bank = wait_fill(dve, ("state",))
            us = uext[:, :, 528:UE].rearrange("p g (b t) -> p g b t", b=NB)
            for g in range(4):
                ins = dve.tensor_copy(us[:, g, :, 0:PSTATE],
                                      bank[:, g * P:g * P + NB * PSTATE].rearrange("p (b t) -> p b t", b=NB))
            ins.then_inc(emptied["D"], 1)
            for c in range(4):
                bank = wait_fill(dve, ("u", c, 1))
                new = bank[:, 224:288]
                dve.tensor_copy(uext[:, c, 304:528], bank[:, 0:224])
                dve.tensor_copy(uS[:, c, :], new)
                dve.tensor_copy(us[:, c, :, PSTATE:], new.rearrange("p (b t) -> p b t", b=NB)).then_inc(emptied["D"], 1)
            for c in range(6):
                empty(("q", c, 1), qT[:, c, 288:TOK], lambda b: b[:, 0:288])
            for g in range(3):
                for t in (1, 3):
                    empty(("k", g, t), kTM[:, t, 256 * g:256 * g + 256], lambda b: b[:, 0:256])
            dve.wait_ge(mods_out, 32)
            for g in range(3):
                for t in (1, 3):
                    empty(("v", g, t), vTM[:, t, 256 * g:256 * g + 256], lambda b: b[:, 0:256])
            for c in range(6, 10):
                bank = wait_fill(dve, ("q", c, 1))
                for e in range(2):
                    h = 2 * (c - 6) + e
                    ins = dve.tensor_copy(qT[64 * (h // 4):64 * (h // 4) + 64, 6 + h % 4, 288:TOK],
                                          bank[64 * e:64 * e + 64, 0:288])
                ins.then_inc(emptied["D"], 1)
            for t in (1, 3):
                bank = wait_fill(dve, ("kvc", t))
                dve.tensor_copy(kTM[:, t, 768:896], bank[:, 0:128])
                dve.tensor_copy(vTM[:, t, 768:896], bank[:, 128:256]).then_inc(emptied["D"], 1)
            dve.wait_ge(tables_out, 16 * 8)
            for m in (1, 3, 5):
                empty(("kT", m), kT[:, m, 0:SEQ])
            empty(("kTs",), kT[:, :, SEQ:TOK], lambda b: b[:, 0:7 * NS].rearrange("p (m n) -> p m n", m=7))

            def outputs(u):
                kind, t, p = UNITS[u]
                bank = wait_fill(dve, ("O", u))
                if kind == "C":
                    if p == 0 and t >= 2:
                        wait_fill(dve, ("ocT", t - 2))
                    link(dve.tensor_tensor(rden[:, u % 4, 0:2], den[:, u % 4, 0:2], dsk[:, u % 4, 0:2], ALU.add))
                    link(dve.reciprocal(rden[:, u % 4, 0:2], rden[:, u % 4, 0:2]))
                    dve.tensor_tensor(octok[:, t % 2, 128 * p:128 * p + 128].rearrange("p (h d) -> p h d", h=2),
                                      bank[:, 0:128].rearrange("p (h d) -> p h d", h=2),
                                      rden[:, u % 4, 0:2].unsqueeze(2).broadcast_to([P, 2, HD]),
                                      ALU.mult).then_inc(emptied["D"], 1)
                else:
                    to = stage[:, kind, t * 264:(t + 1) * 264]
                    dve.tensor_copy(to[:, 256 + p:260:2], nmx[:, u % 4, 0:2])
                    dve.tensor_copy(to[:, 260 + p:264:2], den[:, u % 4, 0:2])
                    dve.tensor_copy(to[:, 0:256].rearrange("p (h g d) -> p h g d", h=2, g=2)[:, :, p, :],
                                    bank[:, 0:128].rearrange("p (h d) -> p h d", h=2)).then_inc(emptied["D"], 1)
                    if kind != 0:
                        wait_emptied(dve, ("O", u))
                        dve.sem_inc(stage_ready, 1)

            def combine():
                dve.wait_ge(stage_in, 32)
                sv = [stage[:, g, :].rearrange("p (t c) -> p t c", t=PT_) for g in range(3)]
                c4 = cmb[:, :, :].rearrange("p n (t h) -> p n t h", t=PT_)
                wait_emptied(dve, ("O", 23))
                link(dve.tensor_tensor(c4[:, 0], sv[0][:, :, 256:260], sv[1][:, :, 256:260], ALU.min))
                link(dve.tensor_tensor(c4[:, 0], c4[:, 0], sv[2][:, :, 256:260], ALU.min))
                for g in range(3):
                    ins = dve.tensor_tensor(c4[:, 1 + g], c4[:, 0], sv[g][:, :, 256:260], ALU.subtract)
                ins.then_inc(cm_ready, 1)
                dve.wait_ge(ce_ready, 1)
                for g in range(3):
                    link(dve.tensor_tensor(c4[:, 4 + g], c4[:, 1 + g], sv[g][:, :, 260:264], ALU.mult))
                link(dve.tensor_tensor(cmb[:, 7, :], cmb[:, 4, :], cmb[:, 5, :], ALU.add))
                link(dve.tensor_tensor(cmb[:, 7, :], cmb[:, 7, :], cmb[:, 6, :], ALU.add))
                link(dve.reciprocal(cmb[:, 7, :], cmb[:, 7, :]))
                for g in range(3):
                    link(dve.tensor_tensor(cmb[:, 4 + g, :], cmb[:, 1 + g, :], cmb[:, 7, :], ALU.mult))
                    for t in range(PT_):
                        v = sv[g][:, t, 0:256].rearrange("p (h d) -> p h d", h=4)
                        ins = dve.tensor_tensor(v, v, c4[:, 4 + g, t].unsqueeze(2).broadcast_to([P, 4, HD]), ALU.mult)
                    link(ins)
                link(dve.tensor_tensor(sv[0][:, :, 0:256], sv[0][:, :, 0:256], sv[1][:, :, 0:256], ALU.add))
                dve.tensor_tensor(sv[0][:, :, 0:256], sv[0][:, :, 0:256], sv[2][:, :, 0:256],
                                  ALU.add).then_inc(bsum_ready, 1)

            dve.wait_ge(biasp_in, 16 * (4 + 8 + 8))
            dve.wait_ge(z_ready, 1)
            for s in range(len(UNITS) + LAGO):
                if s < len(UNITS):
                    kind, t, p = UNITS[s]
                    w = head_cols(UNITS[s])
                    lo = key_blocks(UNITS[s])[0][1]
                    bias = (biasP[:, kind + 1, 2 * P * p:2 * P * (p + 1)] if kind in (1, 2)
                            else biasP[:, p if kind == 0 else 4 + p, :])
                    bank = wait_fill(dve, ("S", s))
                    if s >= 3:
                        wait_fill(dve, ("T", s - 3))

                    def view(x):
                        return x.rearrange("p (h c) -> p h c", h=2)[:, :, lo:]

                    to = sbuf_[:, s % 3, 0:2 * w]
                    dve.scalar_tensor_tensor(view(to), view(bank[:, 0:2 * w]), SCALE, view(bias),
                                             ALU.mult, ALU.add).then_inc(emptied["D"], 1)
                    wait_emptied(dve, ("S", s))
                    nm = nmx[:, s % 4, 0:2]
                    ins = dve.tensor_reduce(nm, view(to), AX, ALU.max, negate=True)
                    if kind == "C":
                        link(ins)
                        ins = dve.tensor_tensor(nm, nm, sinkb[:, 2 * p:2 * p + 2], ALU.min)
                    ins.then_inc(max_ready, 1)
                if s == 24 + LAGO:
                    dve.wait_ge(kv_out, 16 * KV_OUTS)
                if 0 <= s - LAGO < len(UNITS):
                    outputs(s - LAGO)
                    if s - LAGO == COMBINE_AT:
                        combine()

            wait_fill(dve, ("O", len(UNITS) - 1))
            dve.memset(qbd, 0.0)
            link(dve.memset(qbdC, 0.0))
            for g in range(3):
                for p in range(2):
                    for h in range(2):
                        half = slice(64 * h, 64 * h + 64)
                        dve.tensor_copy(
                            qbd[half, 2 * g + p, :].rearrange("p (b h t) -> p b h t", b=NB, h=2)[:, :, h, :],
                            qT[half, 2 * g + p, SEQ:TOK].rearrange("p (b t) -> p b t", b=NB))
            for h in range(8):
                half = slice(64 * (h // 4), 64 * (h // 4) + 64)
                ins = dve.tensor_copy(qbdC[half, :].rearrange("p (b h t) -> p b h t", b=NB, h=8)[:, :, h, :],
                                      qT[half, 6 + h % 4, SEQ:TOK].rearrange("p (b t) -> p b t", b=NB))
            ins.then_inc(qbd_ready, 1)
            for s in range(1, NKF, 2):
                if s >= 4:
                    dve.wait_ge(keys_used, s - 3)
                empty(("KT", s), ktr[:, s % 4, :])
                if s == 21:
                    dve.wait_ge(biass_in, 16 * 7)
                    for n in range(7):
                        dve.tensor_copy(biasS[:, n, 0:P], biasRaw[:, n, 0:P])
                        new = biasRaw[:, n, P:NK].unsqueeze(1).broadcast_to([P, NB, NT])
                        to = biasS[:, n, P:SK].rearrange("p (b t) -> p b t", b=NB)
                        if n < 6:
                            ins = dve.tensor_tensor(to, new, bmask_b.unsqueeze(2).broadcast_to([P, NB, NT]), ALU.add)
                        else:
                            ins = dve.tensor_copy(to, new)
                    link(ins)
            for c in range(4):
                bank = wait_fill(dve, ("SRC", c))
                dve.scalar_tensor_tensor(sC[:, c, :], bank[:, 0:SK], SCALE, biasS[:, 6, :],
                                         ALU.mult, ALU.add).then_inc(emptied["D"], 1)
                wait_emptied(dve, ("SRC", c))
                v = sC[:, c, P:SK].rearrange("p (b t) -> p b t", b=NB)
                ins = dve.tensor_tensor(v, v, bmask_c[:, c, :].unsqueeze(2).broadcast_to([P, NB, NT]), ALU.add)
            link(ins)
            link(dve.tensor_reduce(sst[:, 0, :], sC, AX, ALU.max))
            link(dve.tensor_scalar(sst[:, 0, :], sst[:, 0, :], sinkr[:, 0:1], None, ALU.max))
            dve.tensor_scalar(sst[:, 0, :], sst[:, 0, :], -1.0, None, ALU.mult).then_inc(smax_ready, 1)
            for g in range(3):
                for p in range(2):
                    bank = wait_fill(dve, ("SR", g, p))
                    dve.scalar_tensor_tensor(sB[:, p, g * SK:(g + 1) * SK], bank[:, 0:SK], SCALE,
                                             biasS[:, 2 * g + p, :], ALU.mult, ALU.add).then_inc(emptied["D"], 1)
            wait_emptied(dve, ("SR", 2, 1))
            dve.tensor_reduce(sst[:, 3, 0:2], sB, AX, ALU.max, negate=True).then_inc(smax_ready, 1)
            dve.wait_ge(sexp_ready, 1)
            link(dve.tensor_tensor(sst[:, 1, :], sst[:, 1, :], sst[:, 2, :], ALU.add))
            link(dve.reciprocal(sst[:, 1, :], sst[:, 1, :]))
            link(dve.reciprocal(sst[:, 4, 0:2], sst[:, 4, 0:2]))
            for c in range(4):
                dve.tensor_scalar(sC[:, c, :], sC[:, c, :], sst[:, 1, c:c + 1], None, ALU.mult)
            for p in range(2):
                ins = dve.tensor_scalar(sB[:, p, :], sB[:, p, :], sst[:, 4, p:p + 1], None, ALU.mult)
            ins.then_inc(sprob_ready, 1)
            empty(("PTCn",), pCn[0:NS, :], lambda b: b[0:NS, :])
            for p in range(2):
                empty(("PTn", p), pBn[0:NS, 3 * p:3 * p + 3, :],
                      lambda b: b[0:NS, 0:3 * P].rearrange("p (c n) -> p c n", c=3))
            bank = wait_fill(dve, ("OC",))
            for h in range(8):
                src = bank[64 * (h // 4):64 * (h // 4) + 64, :].rearrange("p (b h t) -> p b h t", b=NB, h=8)[:, :, h, :]
                ins = dve.tensor_copy(ocT[64 * (h % 2):64 * (h % 2) + 64, h // 2, SEQ:TOK].rearrange(
                    "p (b t) -> p b t", b=NB), src)
            ins.then_inc(emptied["D"], 1)
            for p in range(2):
                bank = wait_fill(dve, ("OB", p))
                for h in range(2):
                    half = slice(64 * h, 64 * h + 64)
                    ins = dve.tensor_copy(
                        bT[half, p, SEQ:TOK].rearrange("p (b t) -> p b t", b=NB),
                        bank[half, 0:P].rearrange("p (b h t) -> p b h t", b=NB, h=2)[:, :, h, :])
                ins.then_inc(emptied["D"], 1)

            for m in range(KD):
                for h in range(2):
                    gs = gsig[:, 3 * h:3 * h + 3, :]
                    wait_emptied(dve, ("gc", m, h))
                    link(dve.tensor_scalar(gs, gs, 1.0, None, ALU.add))
                    link(dve.reciprocal(gs, gs))
                    bank = wait_fill(dve, ("oa", m, h))
                    dve.scalar_tensor_tensor(msum[:, 0, :], bank[:, 0:288], pscale[:, m:m + 1], gs[:, 0, :],
                                             ALU.mult, ALU.mult).then_inc(emptied["D"], 1)
                    bank = wait_fill(dve, ("ob", m, h))
                    dve.tensor_tensor(msum[:, 1, :], bank[:, 0:288], gs[:, 1, :], ALU.mult).then_inc(emptied["D"], 1)
                    bank = wait_fill(dve, ("oc", m, h))
                    dve.tensor_tensor(msum[:, 2, :], bank[:, 0:288], gs[:, 2, :], ALU.mult).then_inc(emptied["D"], 1)
                    wait_emptied(dve, ("oc", m, h))
                    link(dve.tensor_tensor(msum[:, 3, :], msum[:, 0, :], msum[:, 1, :], ALU.add))
                    dve.tensor_tensor(mixT[:, m, 288 * h:288 * h + 288], msum[:, 3, :], msum[:, 2, :],
                                      ALU.add).then_inc(mix_ready, 1)
            for h in range(2):
                for t in (1, 3):
                    empty(("mix", t, h), mixed[:, t, 512 * h:512 * h + 512])
            norm_root(1)
            dve.wait_ge(rn_ready, 2)
            dve.wait_ge(gmod_in, 16 * 2)
            dve.wait_ge(xres_in, 32)
            for t in range(TILES):
                r, s = parts(t), t // PT_
                link(dve.scalar_tensor_tensor(mixed[0:r, t, :], mixed[0:r, t, :], stat[0:r, 1, t:t + 1],
                                              gmod[0:r, s, :], ALU.mult, ALU.mult))
                dve.tensor_tensor(x1[0:r, t, :], x1[0:r, t, :], mixed[0:r, t, :], ALU.add).then_inc(x1_ready, 1)
            norm_root(2)
            dve.wait_ge(modf_in, 16 * 4)
            for t in range(TILES + 1):
                if t < TILES:
                    r, s = parts(t), t // PT_
                    dve.wait_ge(xn_ready, TILES + t + 1)
                    dve.tensor_tensor(hbuf2[0:r, t % 2, :], hbuf2[0:r, t % 2, :], modf[0:r, s, :],
                                      ALU.mult).then_inc(hA_ready, 1)
                if t >= 1:
                    u = t - 1
                    w = parts(u)
                    empty(("h2T", u, 1), h2T[:, 4:8, toks(u)],
                          lambda b: b[:, 0:4 * w].rearrange("p (k n) -> p k n", k=4))

            dve.wait_ge(moe_in, 32)
            iota = const2[:, 1, :]
            dve.memset(ones, 1.0)
            for t in range(TILES):
                r = parts(t)
                sc, se = scores[0:r, t, :], sel[0:r, t, :]
                wait_emptied(dve, ("rt", t))
                link(dve.tensor_scalar(sc, sc, 1.0, None, ALU.add))
                link(dve.reciprocal(sc, sc))
                link(dve.tensor_tensor(se, sc, rbias[0:r, :], ALU.add))
                link(dve.max(top8[0:r, t, :], se))
                link(dve.max_index(idxu[0:r, TOPK * t:TOPK * t + TOPK], top8[0:r, t, :], se))
                link(dve.tensor_copy(idxf[0:r, t, :], idxu[0:r, TOPK * t:TOPK * t + TOPK]))
                tm = topm[0:r, TOPK * t:TOPK * t + TOPK, :]
                link(dve.tensor_tensor(tm, iota[0:r, 0:NE].unsqueeze(1).broadcast_to([r, TOPK, NE]),
                                       idxf[0:r, t, :].unsqueeze(2).broadcast_to([r, TOPK, NE]), ALU.is_equal))
                dve.tensor_reduce(maskt[0:r, t, :], tm.rearrange("p k e -> p e k"), AX, ALU.add).then_inc(masks_ready, 1)

            def shared_act(t):
                r = parts(t)
                wait_emptied(dve, ("sgu", t))
                e, g, u = (sgat[0:r, n, :] for n in range(3))
                link(dve.tensor_scalar(e, e, 1.0, None, ALU.add))
                link(dve.reciprocal(e, e))
                link(dve.tensor_tensor(g, g, e, ALU.mult))
                if t >= 1:
                    wait_fill(dve, ("saT", t - 1))
                dve.tensor_tensor(sact[0:r, :], g, u, ALU.mult).then_inc(sact_ready, 1)

            for t in range(TILES):
                shared_act(t)
            total, nblk, ends, r0 = (starts[:, n, :] for n in range(4))
            bank = wait_fill(dve, ("cnt",))
            link(dve.tensor_copy(total, bank[:, 0:NE]))
            link(dve.tensor_scalar(nblk, total, 0.0, None, ALU.is_gt))
            for j in range(1, -(-TOK // P)):
                link(dve.scalar_tensor_tensor(nblk, total, float(P * j), nblk, ALU.is_gt, ALU.add))
            link(dve.tensor_tensor_scan(ends, ones[:, 0:NE], nblk, 0.0, ALU.mult, ALU.add))
            link(dve.tensor_tensor(r0, ends, nblk, ALU.subtract))
            link(dve.tensor_scalar(r0, r0, float(P), None, ALU.mult))
            for t in range(TILES):
                r = parts(t)
                bank = wait_fill(dve, ("pos", t))
                dve.tensor_tensor(sel[0:r, t, :], bank[0:r, 0:NE], r0[0:r, :], ALU.add).then_inc(emptied["D"], 1)
            dve.tensor_copy(nblk[0:1, 0:1], wait_fill(dve, ("cnt",))[0:1, 0:1]).then_inc(emptied["D"], 1)
            wait_emptied(dve, ("cnt",))
            for t in range(TILES):
                r = parts(t)
                tm = topm[0:r, TOPK * t:TOPK * t + TOPK, :]
                pr = prod[0:r, :].rearrange("p (k e) -> p k e", k=TOPK)
                link(dve.tensor_tensor(pr, tm, sel[0:r, t, :].unsqueeze(1).broadcast_to([r, TOPK, NE]), ALU.mult))
                link(dve.tensor_reduce(rowk[0:r, t, :], pr, AX, ALU.add))
                link(dve.tensor_tensor(pr, tm, scores[0:r, t, :].unsqueeze(1).broadcast_to([r, TOPK, NE]), ALU.mult))
                link(dve.tensor_reduce(wts[0:r, t, :], pr, AX, ALU.add))
                link(dve.tensor_reduce(bexpf[0:r, 1:2], wts[0:r, t, :], AX, ALU.add))
                link(dve.reciprocal(bexpf[0:r, 1:2], bexpf[0:r, 1:2]))
                link(dve.tensor_scalar(wts[0:r, t, :], wts[0:r, t, :], bexpf[0:r, 1:2], RSCALE, ALU.mult, ALU.mult))
                cols = slice(TOPK * t, TOPK * t + TOPK)
                link(dve.tensor_copy(rowi[0:r, cols], rowk[0:r, t, :]))
                ri = rowi[0:r, cols].bitcast(I32)
                link(dve.tensor_scalar(sloti[0:r, cols], ri, P - 1, None, ALU.bitwise_and))
                link(dve.tensor_copy(slotf[0:r, t, :], sloti[0:r, cols]))
                link(dve.tensor_tensor(blkf[0:r, t, :], rowk[0:r, t, :], slotf[0:r, t, :], ALU.subtract))
                link(dve.tensor_scalar(blkf[0:r, t, :], blkf[0:r, t, :], 1.0 / P, None, ALU.mult))
                if t >= 1:
                    dve.wait_ge(ohs_used, t)
                dve.tensor_tensor(ohslot[0:r], iota[0:r, :].unsqueeze(1).broadcast_to([r, TOPK, P]),
                                  slotf[0:r, t, :].unsqueeze(2).broadcast_to([r, TOPK, P]), ALU.is_equal)
                ob = [ohblk[0:r, n, :].rearrange("p (k n) -> p k n", k=TOPK) for n in range(2)]
                link(dve.tensor_tensor(ob[0], iota[0:r, 0:NBLK].unsqueeze(1).broadcast_to([r, TOPK, NBLK]),
                                       blkf[0:r, t, :].unsqueeze(2).broadcast_to([r, TOPK, NBLK]), ALU.is_equal))
                link(dve.tensor_tensor(ob[1], ob[0], wts[0:r, t, :].unsqueeze(2).broadcast_to([r, TOPK, NBLK]),
                                       ALU.mult))
                dve.tensor_scalar(ob[0], ob[0], tokid[0:r, t:t + 1], None, ALU.mult).then_inc(ohs_ready, 1)
            link(dve.tensor_scalar(prod[:, 0:NE], ends, pid, None, ALU.is_le, ALU.add, accum_out=bexpf[:, 0:1]))
            dve.tensor_scalar(bexpf[:, 0:1], bexpf[:, 0:1], float(NE - 1), None, ALU.min).then_inc(bexp_ready, 1)
            link(dve.tensor_scalar(prod[:, 0:NE], iota[:, 0:NE], 2.0, None, ALU.mult))
            link(dve.tensor_scalar(prod[:, 0:NE], prod[:, 0:NE], ends[:, NE - 1:NE], None, ALU.is_lt, ALU.add,
                                   accum_out=bexpf[:, 2:3]))
            dve.memset(rowtok[:, NBLK:NBLK + 2], 0)
            bank = wait_fill(dve, ("rowtok",))
            dve.tensor_copy(rowtok[:, 0:NBLK], bank[:, 0:NBLK])
            link(dve.tensor_copy(wtab, bank[:, NBLK:2 * NBLK]))
            link(dve.tensor_scalar(prod[:, NBLK:NBLK + 1], pid, float(TOK), None, ALU.add))
            link(dve.tensor_scalar(addf, wtab, 0.0, None, ALU.is_gt))
            link(dve.tensor_tensor(addf, bank[:, 0:NBLK], addf, ALU.mult))
            link(dve.tensor_scalar(prod[:, 0:NBLK], wtab, 0.0, prod[:, NBLK:NBLK + 1], ALU.is_le, ALU.mult))
            link(dve.tensor_tensor(addf, addf, prod[:, 0:NBLK], ALU.add))
            dve.tensor_copy(addrow, addf).then_inc(emptied["D"], 1)
            empty(("bexp",), bexp[0:1, :], lambda b: b[0:1, 0:P])
            wait_emptied(dve, ("bexp",))
            dve.tensor_copy(pairs[:], bexpf[:, 2:3]).then_inc(tables_ready, 1)
            dve.wait_ge(tables_ready, 1)

            n_pairs = dve.value_load(pairs[0:1, 0:1], min_val=1, max_val=NBLK // 2)
            with dve.Fori(0, n_pairs) as i:
                for j in range(2):
                    dve.wait_ge(t_done, 2 * i + j + 3)
                    dve.tensor_copy(xT[:, j, 512:1024], psb[2 * j + 1][:, :]).then_inc(xt_dve, 1)
                for j in range(2):
                    e, g, a = (act3[:, 3 * j + n, :] for n in range(3))
                    dve.wait_ge(e_ready, 2 * i + j + 1)
                    dve.tensor_scalar(e, e, 1.0, None, ALU.add).then_inc(dve_loop, 1)
                    dve.wait_ge(dve_loop, 6 * i + 3 * j + 1)
                    dve.reciprocal(e, e).then_inc(dve_loop, 1)
                    dve.wait_ge(dve_loop, 6 * i + 3 * j + 2)
                    dve.tensor_tensor(g, psb[4 + j][:, 0:FF], e, ALU.mult).then_inc(dve_loop, 1)
                    dve.wait_ge(dve_loop, 6 * i + 3 * j + 3)
                    dve.tensor_tensor(a, psb[4 + j][:, FF:2 * FF], g, ALU.mult).then_inc(a_ready, 1)
                for j in range(2):
                    dve.wait_ge(added, 2 * i + j + 1)
                    dve.wait_ge(d_done, 2 * i + j + 3)
                    dve.wait_ge(cols_ready, 4 * i + 2 * j + 2)
                    dve.tensor_scalar(yb[:, j, 512:1024], psb[7 if j == 0 else 3][:, :], wcol[:, j:j + 1], None,
                                      ALU.mult).then_inc(y_dve, 1)

            for t in range(TILES):
                r, s = parts(t), t // PT_
                y = ysh[0:r, t, :]
                dve.wait_ge(f_ssq, t + 1)
                st = stat[0:r, 3, t:t + 1]
                dve.tensor_scalar(st, st, 1.0 / D, EPS, ALU.mult, ALU.add).then_inc(f_root, 1)
                dve.wait_ge(f_rn, t + 1)
                link(dve.reciprocal(st, st))
                if t == 0:
                    dve.wait_ge(g2_in, 16 * 2)
                link(dve.scalar_tensor_tensor(y, y, st, g2mod[0:r, s, :], ALU.mult, ALU.mult))
                dve.tensor_tensor(x1[0:r, t, :], x1[0:r, t, :], y, ALU.add).then_inc(f_out, 1)

        @block.tensor
        def _(pe):
            def close(ins):
                ins.then_inc(fills_done, 1)

            def mm(out, lhsT, rhs, first, last):
                return pe.matmul(out, lhsT, rhs, start=first, stop=last)

            pe.wait_ge(consts_in, 48)
            pe.wait_ge(c_silu, 1)
            bank = bank_for(pe, ("cT",))
            for k in range(KD):
                ins = pe.transpose(bank[:, 16 * k:16 * k + 9], crow[0:9, k:D:KD], ident[0:9, 0:9])
            close(ins)

            def ada_group(g):
                bank = bank_for(pe, ("ada", g))
                w = wait_load(pe, ("ada", g))
                if g == 0:
                    wait_emptied(pe, ("cT",))
                for k in range(KD):
                    ins = mm(bank[0:9, :], cT[:, k, :], w[:, 512 * k:512 * k + 512], k == 0, k == KD - 1)
                close(ins)

            def transposed_rows(key, t, src):
                r = parts(t)
                for h in range(2):
                    bank = bank_for(pe, (key, t, h))
                    for k in range(4):
                        ins = pe.transpose(bank[:, k * r:(k + 1) * r], src[0:r, 4 * h + k:D:KD], ident[0:r, 0:r])
                    close(ins)

            for g in range(4):
                ada_group(g)
            pe.wait_ge(onehots_in, 48)
            pe.wait_ge(onehot_ready, 1)
            for n in range(3):
                bank = bank_for(pe, ("gtab", n))
                close(mm(bank[0:20, 0:GW], relT[0:BINS, :], oh_top[0:BINS, n * GW:(n + 1) * GW], True, True))
            for n in range(7):
                w = min(480, 3 * NT * NK - 480 * n)
                bank = bank_for(pe, ("stab", n))
                close(mm(bank[0:20, 0:w], relT[0:BINS, :], oh_smp[0:BINS, 480 * n:480 * n + w], True, True))
            for g in range(4, 8):
                ada_group(g)
            for t in range(TILES):
                pe.wait_ge(h_ready, t + 1)
                transposed_rows("hT", t, hbuf[:, t % 2, :])
                if t < 4:
                    ada_group(8 + t)
            pe.wait_ge(state_in, 16)
            bank = bank_for(pe, ("state",))
            n = NB * PSTATE
            for g in range(4):
                ins = pe.transpose(bank[:, g * P:g * P + n], staterow[0:n, g * P:(g + 1) * P], ident[0:n, 0:n])
            close(ins)

            def by_channel(key, w, col):
                for h in range(2):
                    bank = bank_for(pe, key + (h,))
                    for k in range(KD):
                        ins = mm(bank[:, 0:288], w[:, 512 * k + col:512 * k + col + P],
                                 hT[:, k, 288 * h:288 * h + 288], k == 0, k == KD - 1)
                    close(ins)

            def by_token(key, w, col, t, folded):
                bank = bank_for(pe, key)
                r = parts(t)
                for k in range(KD):
                    x = hT[:, k, t:SEQ:4] if folded and t < PT_ else hT[:, k, toks(t)]
                    ins = mm(bank[0:r, 0:256], x, w[:, 512 * k + col:512 * k + col + 256], k == 0, k == KD - 1)
                close(ins)

            for t in range(TILES):
                for h in range(2):
                    wait_emptied(pe, ("hT", t, h))
            w = wait_load(pe, ("in", 0))
            for c in range(4):
                by_channel(("u", c), w, c * P)
            w = wait_load(pe, ("in", 1))
            for c in range(4):
                by_channel(("q", c), w, c * P)
            w = wait_load(pe, ("in", 2))
            for c in range(4, 6):
                by_channel(("q", c), w, (c - 4) * P)
            for g in range(3):
                if g == 1:
                    w = wait_load(pe, ("in", 3))
                for t in range(TILES):
                    by_token(("k", g, t), w, (256, 0, 256)[g], t, g > 0)
            for g in range(3):
                if g != 1:
                    w = wait_load(pe, ("in", 4 + g // 2))
                for t in range(TILES):
                    by_token(("v", g, t), w, (0, 256, 0)[g], t, g > 0)
            for c in range(6, 8):
                by_channel(("q", c), w, 256 + (c - 6) * P)
            w = wait_load(pe, ("in", 6))
            for c in range(8, 10):
                by_channel(("q", c), w, (c - 8) * P)
            for t in range(TILES):
                by_token(("kvc", t), w, 256, t, False)
            bank = bank_for(pe, ("uout", 0))
            for c in range(4):
                ins = pe.transpose(bank[0:PSTATE, c * P:(c + 1) * P], uext[:, c, 528 - PSTATE:528], ident[:, :])
            close(ins)
            bank = bank_for(pe, ("uout", 1))
            for c in range(4):
                ins = pe.transpose(bank[0:NS, c * P:(c + 1) * P], uS[:, c, :], ident[:, :])
            close(ins)
            for t in range(TILES):
                for g in range(3):
                    wait_emptied(pe, ("k", g, t))
                wait_emptied(pe, ("kvc", t))
            for m in range(7):
                bank = bank_for(pe, ("kT", m))
                for t in range(PT_):
                    ins = pe.transpose(bank[:, t * P:(t + 1) * P], kTM[:, t, m * P:(m + 1) * P], ident[:, :])
                close(ins)
            bank = bank_for(pe, ("kTs",))
            for m in range(7):
                ins = pe.transpose(bank[:, m * NS:(m + 1) * NS], kTM[0:NS, PT_, m * P:(m + 1) * P], ident[0:NS, 0:NS])
            close(ins)

            for m in range(7):
                wait_emptied(pe, ("kT", m))
            wait_emptied(pe, ("v", 2, 4))
            wait_emptied(pe, ("v", 2, 3))
            for h in range(2):
                wait_emptied(pe, ("q", 9, h))
            for s in range(len(UNITS) + LAGO):
                if s < len(UNITS):
                    kind, t, p = UNITS[s]
                    bank = bank_for(pe, ("S", s))
                    w = head_cols(UNITS[s])
                    for h, hd in enumerate(heads(UNITS[s])):
                        if kind == "C":
                            half, cq, ck = 64 * (hd // 4), 6 + hd % 4, 6
                        else:
                            half, cq, ck = 64 * (hd % 2), 2 * kind + hd // 2, 2 * kind + hd // 2
                        rows = slice(half, half + 64)
                        q = qT[rows, cq, t:SEQ:4] if kind in (1, 2) else qT[rows, cq, toks(t)]
                        blocks = key_blocks(UNITS[s])
                        lo, k0 = blocks[0][1], blocks[0][0] * P
                        width = P * len(blocks)
                        ins = mm(bank[:, h * w + lo:h * w + lo + width], q, kT[rows, ck, k0:k0 + width], True, True)
                    close(ins)
                u = s - LAGT
                if 0 <= u < len(UNITS):
                    bank = bank_for(pe, ("T", u))
                    pe.wait_ge(probs_ready, u + 1)
                    w = head_cols(UNITS[u])
                    n = 0
                    for h in range(2):
                        for _, pos in key_blocks(UNITS[u]):
                            ins = pe.transpose(bank[:, n * P:(n + 1) * P],
                                               sbuf_[:, u % 3, h * w + pos:h * w + pos + P], ident[:, :])
                            n += 1
                    close(ins)
                u = s - LAGO
                if 0 <= u < len(UNITS):
                    kind, t, p = UNITS[u]
                    bank = bank_for(pe, ("O", u))
                    wait_emptied(pe, ("T", u))
                    n = 0
                    blocks = key_blocks(UNITS[u])
                    for h, hd in enumerate(heads(UNITS[u])):
                        col = 768 + 64 * (hd // 4) if kind == "C" else 256 * kind + 64 * hd
                        for i, (kt, _) in enumerate(blocks):
                            ins = mm(bank[:, 64 * h:64 * h + 64], pTb[:, u % 2, n * P:(n + 1) * P],
                                     vTM[:, kt, col:col + 64], i == 0, i == len(blocks) - 1)
                            n += 1
                    close(ins)
                for key in after_unit(u):
                    bank = bank_for(pe, key)
                    t = key[1]
                    if key[0] == "ocT":
                        wait_emptied(pe, ("O", u))
                        for c in range(4):
                            ins = pe.transpose(bank[:, c * P:(c + 1) * P], octok[:, t % 2, c * P:(c + 1) * P], ident[:, :])
                    else:
                        pe.wait_ge(bsum_ready, 1)
                        for c in range(2):
                            ins = pe.transpose(bank[:, c * P:(c + 1) * P],
                                               stage[:, 0, t * 264 + c * P:t * 264 + (c + 1) * P], ident[:, :])
                    close(ins)

            pe.wait_ge(qbd_ready, 1)
            wait_emptied(pe, ("kTs",))
            for n in range(2):
                bank = bank_for(pe, ("Sn", n))
                for m in range(4 * n, min(4 * n + 4, 6)):
                    ins = mm(bank[0:NS, (m % 4) * P:(m % 4 + 1) * P], kT[:, m, SEQ:TOK], qbd[:, m, :], True, True)
                close(ins)
            bank = bank_for(pe, ("SnC",))
            close(mm(bank[0:NS, :], kT[:, 6, SEQ:TOK], qbdC, True, True))

            def cached(kv, kind, b, r, p):
                if kind == "C":
                    return slot[slot_of((kv, "c0", 0))][:, 128 * b:128 * b + 128]
                if kind == 0:
                    c = 1024 + 256 * b + 128 * p
                    return slot[slot_of((kv, "c0", 0))][:, c:c + 128]
                if kind == 1:
                    c = 1024 * (b % 4) + 256 * r + 128 * p
                    return slot[slot_of((kv, "c1", b // 4))][:, c:c + 128]
                c = 2048 * (b % 2) + 256 * r + 128 * p
                return slot[slot_of((kv, "c2", b // 2))][:, c:c + 128]

            def load_of(kv, kind, b):
                return (kv, "c0", 0) if kind in ("C", 0) else (kv, "c1", b // 4) if kind == 1 else (kv, "c2", b // 2)

            def row_cols(x, kind, b, r):
                if kind == "C":
                    return x[:, 64 * b:64 * b + 64]
                v = x.rearrange("p (b h t) -> p b h t", b=NB, h=2)[:, b]
                if kind == 0:
                    return x[:, 16 * b:16 * b + 16]
                if kind == 1:
                    return v[:, :, r::4]
                return v[:, :, r]

            for s in range(NKF + 1):
                if s < NKF:
                    bank = bank_for(pe, ("KT", s))
                    for n, (kind, b, r, p) in enumerate(KEYS[s]):
                        wait_load(pe, load_of("K", kind, b))
                        ins = pe.transpose(bank[:, n * P:(n + 1) * P], cached("K", kind, b, r, p), ident[:, :])
                    close(ins)
                if s >= 1:
                    if s == 1:
                        sm = [bank_for(pe, ("SM", n)) for n in range(3)]
                    wait_emptied(pe, ("KT", s - 1))
                    for n, (kind, b, r, p) in enumerate(KEYS[s - 1]):
                        if kind == "C":
                            to, q = sm[2][:, :], qbdC
                        elif kind == 2:
                            to, q = sm[1][:, p * P:(p + 1) * P], qbd[:, 4 + p, :]
                        else:
                            to, q = sm[0][:, (2 * kind + p) * P:(2 * kind + p + 1) * P], qbd[:, 2 * kind + p, :]
                        ins = mm(row_cols(to, kind, b, r), ktr[:, (s - 1) % 4, n * P:(n + 1) * P],
                                 row_cols(q, kind, b, r), True, True)
                    if s - 1 in (1, 21, NKF - 1):
                        close(ins)
                        pe.wait_ge(fills_done, INDEX[("SM", {1: 2, 21: 0, NKF - 1: 1}[s - 1])] + 1)
                        pe.sem_inc(keys_used, 1)
                    else:
                        ins.then_inc(keys_used, 1)
            for c in range(4):
                bank = bank_for(pe, ("SRC", c))
                wait_emptied(pe, ("SM", 2))
                wait_emptied(pe, ("SnC",))
                pe.transpose(bank[:, 0:P], stC[:, c * P:(c + 1) * P], ident[:, :])
                close(pe.transpose(bank[:, P:SK], stCn[0:NS, c * P:(c + 1) * P], ident[0:NS, 0:NS]))
            for g in range(3):
                for p in range(2):
                    m = 2 * g + p
                    bank = bank_for(pe, ("SR", g, p))
                    wait_emptied(pe, ("SM", g // 2))
                    wait_emptied(pe, ("Sn", m // 4))
                    pe.transpose(bank[:, 0:P], stB[:, m, :], ident[:, :])
                    close(pe.transpose(bank[:, P:SK], stBn[0:NS, m, :], ident[0:NS, 0:NS]))
            pe.wait_ge(sprob_ready, 1)
            bank = bank_for(pe, ("PTC",))
            for c in range(4):
                ins = pe.transpose(bank[:, c * P:(c + 1) * P], sC[:, c, 0:P], ident[:, :])
            close(ins)
            bank = bank_for(pe, ("PTCn",))
            for c in range(4):
                ins = pe.transpose(bank[0:NS, c * P:(c + 1) * P], sC[:, c, P:SK], ident[:, :])
            close(ins)
            for p in range(2):
                bank = bank_for(pe, ("PT", p))
                for g in range(3):
                    ins = pe.transpose(bank[:, g * P:(g + 1) * P], sB[:, p, g * SK:g * SK + P], ident[:, :])
                close(ins)
                bank = bank_for(pe, ("PTn", p))
                for g in range(3):
                    ins = pe.transpose(bank[0:NS, g * P:(g + 1) * P], sB[:, p, g * SK + P:(g + 1) * SK], ident[:, :])
                close(ins)
            oc, ob = bank_for(pe, ("OC",)), [bank_for(pe, ("OB", p)) for p in range(2)]
            for key in (("PTC",), ("PTCn",), ("PT", 0), ("PTn", 0), ("PT", 1), ("PTn", 1)):
                wait_emptied(pe, key)
            mm(oc[:, :], vTM[0:NS, PT_, 768:896], pCn[0:NS, :], True, False)
            for p in range(2):
                for g in range(3):
                    c = 256 * g + P * p
                    mm(ob[p][:, 0:P], vTM[0:NS, PT_, c:c + P], pBn[0:NS, 3 * p + g, :], g == 0, False)
            wait_load(pe, ("V", "c0", 0))
            for b in range(NB):
                ins = mm(row_cols(oc[:, :], "C", b, 0), cached("V", "C", b, 0, 0), row_cols(pC, "C", b, 0),
                         False, b == NB - 1)
            close(ins)
            for vs, (kind, bs, res) in enumerate([(0, range(8), 1)] + [(1, range(4 * q, 4 * q + 4), 4) for q in range(2)]
                                                 + [(2, range(2 * q, 2 * q + 2), 8) for q in range(4)]):
                wait_load(pe, load_of("V", kind, bs[0]))
                for p in range(2):
                    for b in bs:
                        for r in range(res):
                            last = vs == 6 and b == bs[-1] and r == res - 1
                            ins = mm(row_cols(ob[p][:, 0:P], kind, b, r), cached("V", kind, b, r, p),
                                     row_cols(pB[:, 3 * p + kind, :], kind, b, r), False, last)
                    if vs == 6:
                        close(ins)
                if vs < 6:
                    ins.then_inc(vals_used, 1)

            for m in range(KD):
                wc = wait_load(pe, ("wc",))
                wg = wait_load(pe, ("gate", m))
                for h in range(2):
                    cols = slice(288 * h, 288 * h + 288)
                    for j, what in enumerate(("ga", "gb", "gc")):
                        bank = bank_for(pe, (what, m, h))
                        for k in range(KD):
                            c = 1024 * j + P * k
                            ins = mm(bank[:, 0:288], wg[:, c:c + P], hT[:, k, cols], k == 0, k == KD - 1)
                        close(ins)
                    if m == 0 and h == 0:
                        wait_emptied(pe, ("OC",))
                        wait_emptied(pe, ("OB", 1))
                        pe.wait_ge(merge_in, 32)
                        pe.wait_ge(z_ready, 1)
                    bank = bank_for(pe, ("oa", m, h))
                    close(mm(bank[:, 0:288], pw[:, m // 2, (m % 2) * P:(m % 2 + 1) * P], zT[:, m // 2, cols], True, True))
                    bank = bank_for(pe, ("ob", m, h))
                    for c in range(2):
                        ins = mm(bank[:, 0:288], wb[:, c, m * P:(m + 1) * P], bT[:, c, cols], c == 0, c == 1)
                    close(ins)
                    bank = bank_for(pe, ("oc", m, h))
                    for c in range(4):
                        ins = mm(bank[:, 0:288], wc[:, D * c + m * P:D * c + (m + 1) * P], ocT[:, c, cols], c == 0, c == 3)
                    close(ins)
            pe.wait_ge(mix_ready, 2 * KD)
            for h in range(2):
                w = wait_load(pe, ("wout", h))
                for t in range(TILES):
                    r = parts(t)
                    bank = bank_for(pe, ("mix", t, h))
                    for m in range(KD):
                        ins = mm(bank[0:r, :], mixT[:, m, toks(t)], w[:, 512 * m:512 * m + 512], m == 0, m == KD - 1)
                    close(ins)
            for t in range(TILES):
                pe.wait_ge(h_ready, TILES + t + 1)
                transposed_rows("h2T", t, hbuf2[:, t % 2, :])

            w = wait_load(pe, ("wsd",))
            for t in range(TILES):
                for h in range(2):
                    wait_emptied(pe, ("h2T", t, h))
            for t in range(TILES):
                r = parts(t)
                bank = bank_for(pe, ("rt", t))
                for k in range(KD):
                    ins = mm(bank[0:r, 0:NE], h2T[:, k, toks(t)], w[:, 2048 + NE * k:2048 + NE * (k + 1)],
                             k == 0, k == KD - 1)
                close(ins)
            wgu = wait_load(pe, ("wsgu",)).rearrange("p (j k n) -> p k j n", j=2, k=KD)

            def shared_down(t):
                r = parts(t)
                bank = bank_for(pe, ("saT", t))
                pe.wait_ge(sact_ready, t + 1)
                for k in range(2):
                    ins = pe.transpose(bank[:, k * r:(k + 1) * r], sact[0:r, k:FF:2], ident[0:r, 0:r])
                close(ins)
                for h in range(2):
                    bank = bank_for(pe, ("sy", t, h))
                    wait_emptied(pe, ("saT", t))
                    for k in range(2):
                        c = D * k + 512 * h
                        ins = mm(bank[0:r, :], saT[:, k, 0:r], w[:, c:c + 512], k == 0, k == 1)
                    close(ins)

            for t in range(TILES):
                r = parts(t)
                bank = bank_for(pe, ("sgu", t))
                for k in range(KD):
                    ins = mm(bank[0:r, :], h2T[:, k, toks(t)], wgu[:, k], k == 0, k == KD - 1)
                close(ins)
                if t >= 1:
                    shared_down(t - 1)
            shared_down(TILES - 1)

            pe.wait_ge(moe_in, 32)
            pe.wait_ge(masks_ready, TILES)
            tri = const2[:, 0, :]
            for t in range(TILES):
                r = parts(t)
                bank = bank_for(pe, ("pos", t))
                for u in range(t + 1):
                    n = parts(u)
                    ins = mm(bank[0:r, 0:NE], tri[0:n, 0:r] if u == t else ones[0:n, 0:r], maskt[0:n, u, :],
                             u == 0, u == t)
                close(ins)
            bank = bank_for(pe, ("cnt",))
            for u in range(TILES):
                n = parts(u)
                ins = mm(bank[:, 0:NE], ones[0:n, :], maskt[0:n, u, :], u == 0, u == TILES - 1)
            close(ins)
            bank = bank_for(pe, ("rowtok",))
            for t in range(TILES):
                r = parts(t)
                pe.wait_ge(ohs_ready, t + 1)
                for k in range(TOPK):
                    ins = mm(bank[:, 0:2 * NBLK], ohslot[0:r, k, :], ohblk[0:r, :, k * NBLK:(k + 1) * NBLK], t == 0 and k == 0,
                             t == TILES - 1 and k == TOPK - 1)
                if t < TILES - 1:
                    ins.then_inc(ohs_used, 1)
                else:
                    close(ins)
            bank = bank_for(pe, ("bexp",))
            pe.wait_ge(bexp_ready, 1)
            close(mm(bank[0:1, 0:P], bexpf[:, 0:1], ident[:, :], True, True))

            pe.wait_ge(tables_ready, 1)
            n_pairs = pe.value_load(pairs[0:1, 0:1], min_val=1, max_val=NBLK // 2)
            pe.sem_inc(t_done, 2)
            pe.sem_inc(gu_done, 2)
            pe.sem_inc(d_done, 2)
            pe.sem_inc(y_act, 1)
            pe.sem_inc(y_dve, 1)
            with pe.Fori(0, n_pairs) as i:
                for j in range(2):
                    if j == 1:
                        pe.wait_ge(y_act, 2 * i + 1)
                        pe.wait_ge(y_dve, 2 * i + 1)
                    pe.wait_ge(xg_in[j], 16 * i + 16)
                    for k in range(KD):
                        ins = pe.transpose(psb[2 * j + k // 4][:, P * (k % 4):P * (k % 4 + 1)], xg[:, j, k:D:KD],
                                           ident[:, :])
                    ins.then_inc(t_done, 1)
                for j in range(2):
                    pe.wait_ge(xt_act, 2 * i + j + 1)
                    pe.wait_ge(xt_dve, 2 * i + j + 1)
                    pe.wait_ge(wgu_in[j], 32 * i + 32)
                    wv = wexp[j][:, 0:4096].rearrange("p (j k n) -> p k j n", j=2, k=KD)
                    for k in range(KD):
                        ins = mm(psb[4 + j][:, :], xT[:, j, P * k:P * (k + 1)], wv[:, k], k == 0, k == KD - 1)
                    ins.then_inc(gu_done, 1)
                for j in range(2):
                    pe.wait_ge(a_ready, 2 * i + j + 1)
                    for k in range(2):
                        ins = pe.transpose(psb[j][:, k * P:(k + 1) * P], act3[:, 3 * j + 2, k:FF:2], ident[:, :])
                    ins.then_inc(at_done, 1)
                    pe.wait_ge(at_ready, 2 * i + j + 1)
                    pe.wait_ge(wd_in[j], 16 * i + 16)
                    for h in range(2):
                        to = psb[(6 if j == 0 else 2) + h]
                        for k in range(2):
                            c = 4096 + D * k + 512 * h
                            ins = mm(to[:, :], aT[:, j, k * P:(k + 1) * P], wexp[j][:, c:c + 512], k == 0, k == 1)
                    ins.then_inc(d_done, 1)


_INS = ['x_prompt', 'x_sample', 'cache_b1', 'cache_b2', 'cache_b3', 'cache_c', 'state_pool', 'c_prompt',
        'c_sample', 'rel_bias', 'w_ada', 'b_ada', 'g_pre_mix', 'g_post_mix', 'g_pre_ffn', 'g_post_ffn',
        'w_in', 'pool_w', 'pool_scale', 'w_b_up', 'w_c_up', 'sinks', 'w_out', 'w_router', 'router_bias',
        'we_gate', 'we_up', 'we_down', 'ws_gate', 'ws_up', 'ws_down']
_OUTS = ([(1, SEQ, D), (NB, NT, D)]
         + [(1, 1, min(n, SEQ), 2, 4, HD) for n in CACHE] + [(1, 1, P, 2, 2, HD), (1, 1, PSTATE, 512)]
         + [(1, NB, n, 2, 4, HD) for n in CACHE] + [(1, NB, P, 2, 2, HD), (1, NB, PSTATE, 512)])


def kernel(**inputs):
    import concourse.bacc as bacc
    from concourse.bass_utils import run_bass_kernel_spmd

    nc = bacc.Bacc("TRN2", target_bir_lowering=False, num_devices=1)
    arrays, args = {}, []
    named = [(name, np.ascontiguousarray(inputs[name])) for name in _INS]
    named += list(zip(("onehot_top", "onehot_smp", "const"), consts()))
    for name, a in named:
        arrays["in_" + name] = a
        args.append(nc.dram_tensor("in_" + name, a.shape, mybir.dt.from_np(a.dtype), kind="ExternalInput").ap())
    for i, shape in enumerate(_OUTS):
        args.append(nc.dram_tensor(f"out_{i}", shape, F32, kind="ExternalOutput").ap())
    build(nc, *args)
    r = run_bass_kernel_spmd(nc, [arrays], core_ids=[0])
    return tuple(r.results[0][f"out_{i}"] for i in range(len(_OUTS)))
```

```python
from contextlib import ExitStack

import numpy as np
import concourse.bass as bass
from concourse import mybir

F32 = mybir.dt.float32
I32 = mybir.dt.int32
U32 = mybir.dt.uint32
ACT = mybir.ActivationFunctionType
ALU = mybir.AluOpType
AX = mybir.AxisListType.X

P = 128
D = 1024
KD = D // P
SEQ = 512
NB, NT = 8, 8
NS = NB * NT
TOK = SEQ + NS
PT_ = SEQ // P
TILES = PT_ + 1
HD = 64
SCALE = HD ** -0.5
POOLW = (2, 4, 8, 16)
PSTATE = 15
GATE0 = 3584
NE, TOPK, FF = 64, 8, 256
RSCALE = 2.5
EPS = 1e-6
MASK = -1e30
NBLK = (TOK * TOPK + NE * (P - 1)) // P // 2 * 2 + 2
CACHE = (128, 512, 2048)
BINS = 33
GW = 384
NK = 136
SK = P + NS


def parts(t):
    return P if t < PT_ else NS


def toks(t):
    return slice(t * P, t * P + parts(t))


def plan():
    fills = []
    ring = {"set": list(range(8)), "n": 0}

    def fill(key, who, bank=None):
        if bank is None:
            bank = ring["set"][ring["n"] % len(ring["set"])]
            ring["n"] += 1
        fills.append((key, who, bank))

    fill(("cT",), "D")
    for g in range(4):
        fill(("ada", g), "D")
    for n in range(3):
        fill(("gtab", n), "D")
    for n in range(7):
        fill(("stab", n), "A")
    for g in range(4, 8):
        fill(("ada", g), "D")
    for t in range(TILES):
        for h in range(2):
            fill(("hT", t, h), "AD"[h])
        if t < 4:
            fill(("ada", 8 + t), "D")
    fill(("state",), "D")
    for c in range(4):
        for h in range(2):
            fill(("u", c, h), "AD"[h])
    for c in range(6):
        for h in range(2):
            fill(("q", c, h), "AD"[h])
    for g in (0, 1, 2):
        for t in range(TILES):
            fill(("k", g, t), "AD"[t % 2])
    for g in (0, 1):
        for t in range(TILES):
            fill(("v", g, t), "AD"[t % 2])
    for t in range(TILES):
        fill(("v", 2, t), "AD"[t % 2])
    for c in range(6, 10):
        for h in range(2):
            fill(("q", c, h), "AD"[h])
    for t in range(TILES):
        fill(("kvc", t), "AD"[t % 2])
    fill(("uout", 0), "A")
    fill(("uout", 1), "A")
    for m in range(7):
        fill(("kT", m), "AD"[m % 2])
    fill(("kTs",), "D")
    for s in range(len(UNITS) + LAGO):
        if s < len(UNITS):
            fill(("S", s), "D")
        if 0 <= s - LAGT < len(UNITS):
            fill(("T", s - LAGT), "A")
        if 0 <= s - LAGO < len(UNITS):
            fill(("O", s - LAGO), "D")
        for key in after_unit(s - LAGO):
            fill(key, "A")
    ring["set"], ring["n"] = list(range(8)), 0
    fill(("Sn", 0), "A")
    fill(("Sn", 1), "A")
    fill(("SnC",), "A")
    for s in range(NKF + 1):
        if s < NKF:
            fill(("KT", s), "AD"[s % 2])
        if s >= 1:
            fill(("SM", s - 1), "AD"[s % 2])
    for c in range(4):
        fill(("SRC", c), "D")
    for g in range(3):
        for p in range(2):
            fill(("SR", g, p), "D")
    fill(("PTC",), "A")
    fill(("PTCn",), "D")
    for p in range(2):
        fill(("PT", p), "A")
        fill(("PTn", p), "D")
    fill(("OC",), "D")
    fill(("OB", 0), "D")
    fill(("OB", 1), "D")
    for s in range(NKF):
        fill(("VO", s), "AD"[s % 2])
    for m in range(KD):
        for h in range(2):
            for what in ("ga", "gb", "gc"):
                fill((what, m, h), "A")
            for what in ("oa", "ob", "oc"):
                fill((what, m, h), "D")
    def routed(t):
        fill(("h2T", t, 0), "A")
        fill(("h2T", t, 1), "D")
        fill(("rt", t), "A")

    def shared_down(t):
        fill(("saT", t), "A")
        fill(("sy", t, 0), "A")
        fill(("sy", t, 1), "A")

    for t in range(TILES):
        fill(("mix", t, 0), "A")
        fill(("mix", t, 1), "D")
        if t >= 2:
            routed(t - 2)
    routed(TILES - 2)
    fill(("sgu", 0), "A")
    routed(TILES - 1)
    fill(("sgu", 1), "A")
    shared_down(0)
    for t in range(TILES):
        fill(("pos", t), "D")
    fill(("cnt",), "D")
    ring["set"], ring["n"] = list(range(7)), 0
    for t in range(2, TILES):
        fill(("sgu", t), "A")
        shared_down(t - 1)
    shared_down(TILES - 1)
    fill(("rowtok",), "D", 7)
    fill(("bexp",), "D")
    return fills


UNITS = ([(k, t, p) for k in (1, 2) for t in range(4) for p in range(2)]
         + [(0, t, p) for t in range(4) for p in range(2)]
         + [("C", t, p) for t in range(4) for p in range(4)])
LAGT, LAGO = 2, 3
NKF = 54
COMBINE_AT = 27


def heads(unit):
    kind, _, p = unit
    return [2 * p, 2 * p + 1] if kind == "C" else [p, p + 2]


def key_blocks(unit):
    kind, t, _ = unit
    if kind in (1, 2):
        return [(t, 0)]
    return ([(t - 1, 0)] if t else []) + [(t, P)]


def head_cols(unit):
    return P if unit[0] in (1, 2) else 2 * P


def after_unit(u):
    if u < 0 or u >= len(UNITS):
        return []
    out = []
    kind, t, p = UNITS[u]
    if kind == "C" and p == 3:
        out.append(("ocT", t))
    if u == COMBINE_AT + 7:
        out += [("bT", t) for t in range(PT_)]
    return out


def key_fills():
    blocks = [("C", b, 0, 0) for b in range(NB)]
    blocks += [(0, b, 0, p) for b in range(NB) for p in range(2)]
    blocks += [(1, b, r, p) for b in range(NB) for r in range(4) for p in range(2)]
    blocks += [(2, b, r, p) for b in range(NB) for r in range(8) for p in range(2)]
    return [blocks[4 * n:4 * n + 4] for n in range(NKF)]


def loads():
    out = [(("ada", g), g % 4) for g in range(12)]
    out += [(("in", g), g % 4) for g in range(7)]
    n = 7
    for kv in "KV":
        for key in [("c0", 0), ("c1", 0), ("c1", 1)] + [("c2", q) for q in range(4)]:
            out.append(((kv,) + key, n % 4))
            n += 1
    out.append((("wc",), 1))
    out += [(("gate", m), (2, 3, 0, 2, 3, 0, 2, 0)[m]) for m in range(KD)]
    out += [(("wout", 0), 3), (("wout", 1), 2), (("wsd",), 0), (("wsgu",), 1)]
    return out


SLOT = 4096
A_HT = 4 * SLOT
A_QT = A_HT + KD * TOK
A_KT = A_QT + 10 * TOK
A_KTM = A_KT + 7 * TOK
A_VTM = A_KTM + TILES * 896
A_ZT = A_VTM + TILES * 896
A_BT = A_ZT + 4 * TOK
A_OCT = A_BT + 2 * TOK
A_SC = A_OCT + 4 * TOK
ARENA = 52480
UE = 16 + SEQ + NB * (PSTATE + NT)


def consts():
    def bucket(d):
        n = np.asarray(d, np.int64)
        log = np.log(np.maximum(n, 1) / 16) / np.log(2048 / 16)
        return np.where(n < 16, n, np.minimum(16 + (log * 16).astype(np.int64), 31))

    top = np.zeros((BINS, 3, GW), np.float32)
    for x in range(GW):
        d = 255 - x
        for n, (dil, every) in enumerate(((1, 1), (4, 1), (4, 4))):
            ok = 0 <= d <= 128 and d % every == 0
            top[bucket(dil * d) if ok else 32, n, x] = 1
    smp = np.zeros((BINS, 3, NT, NK), np.float32)
    for t in range(NT):
        for k in range(NK):
            new = k - P
            for n, dil in enumerate((1, 4, 16)):
                if dil == 1:
                    j = P + t - k
                    ok = 0 <= j <= 128
                elif k < P:
                    j = P + t // dil - k
                    ok = 0 <= j <= 128
                else:
                    j = (t - new) // dil
                    ok = new <= t and (t - new) % dil == 0
                smp[bucket(dil * j) if ok else 32, n, t, k] = 1
    one = np.zeros((P, 5 * P), np.float32)
    one[:, :P] = np.eye(P)
    one[:, P:2 * P] = np.triu(np.ones((P, P)), 1)
    one[:, 2 * P:3 * P] = np.arange(P)[None]
    rows = np.arange(P)
    for b in range(NB):
        one[:, 3 * P + b] = np.where(rows // 16 == b, 0, MASK)
        for c in range(4):
            one[:, 3 * P + 8 + c * 8 + b] = np.where(2 * c + rows // 64 == b, 0, MASK)
    for t in range(TILES):
        one[:, 3 * P + 40 + t] = t * P + rows
    one[:, 3 * P + 45] = rows
    for g, w in enumerate(POOLW):
        one[:, 4 * P + 16 * g:4 * P + 16 * g + 16] = (1.0 / np.minimum(np.arange(16) + 1, w))[None]
    return top.reshape(BINS, -1), smp.reshape(BINS, -1), one


def build(nc, x_prompt, x_sample, cache_b1, cache_b2, cache_b3, cache_c, state_pool, c_prompt, c_sample,
          rel_bias, w_ada, b_ada, g_pre_mix, g_post_mix, g_pre_ffn, g_post_ffn, w_in, pool_w, pool_scale,
          w_b_up, w_c_up, sinks, w_out, w_router, router_bias, we_gate, we_up, we_down,
          ws_gate, ws_up, ws_down, onehot_top, onehot_smp, const,
          y_p, y_s, b1_p, b2_p, b3_p, c_p, pool_p, b1_s, b2_s, b3_s, c_s, pool_s):
    PLAN = plan()
    INDEX = {key: n for n, (key, _, _) in enumerate(PLAN)}
    RANK = {}
    for n, (key, who, _) in enumerate(PLAN):
        RANK[key] = sum(1 for k in PLAN[:n] if k[1] == who)
    LOADS = loads()
    KEYS = key_fills()
    caches = (cache_b1, cache_b2, cache_b3)
    outs_p, outs_s = (b1_p, b2_p, b3_p), (b1_s, b2_s, b3_s)

    with ExitStack() as ctx:
        def sem(name):
            return ctx.enter_context(nc.semaphore(name))

        def sb(name, shape, dt=F32):
            return ctx.enter_context(nc.sbuf_tensor(name, shape, dt))

        arena = sb("arena", [P, ARENA])

        def at(off, *dims):
            n = int(np.prod(dims))
            v = arena[:, off:off + n]
            if len(dims) == 2:
                v = v.rearrange("p (a b) -> p a b", b=dims[1])
            if len(dims) == 3:
                v = v.rearrange("p (a b c) -> p a b c", b=dims[1], c=dims[2])
            return v

        ident = sb("ident", [P, P])
        misc = sb("misc", [P, P])
        recip = sb("recip", [P, 4, 16])
        mx = sb("mx", [P, 4, 4])
        nmx = sb("nmx", [P, 4, 4])
        den = sb("den", [P, 4, 4])
        dsk = sb("dsk", [P, 4, 4])
        rden = sb("rden", [P, 4, 4])
        cmb = sb("cmb", [P, 8, 16])
        sst = sb("sst", [P, 6, 4])
        sinkr = sb("sinkr", [P, 1])
        sinkb = sb("sinkb", [P, 8])
        pscale = sb("pscale", [P, KD])
        stat = sb("stat", [P, 4, TILES])
        wts = sb("wts", [P, TILES, TOPK])
        icol = sb("icol", [P, 2], U32)
        scol = sb("scol", [P, 2], U32)
        wcol = sb("wcol", [P, 2])
        ints = sb("ints", [P, 2])
        pairs = sb("pairs", [P, 2], I32)
        psb = [ctx.enter_context(nc.psum_tensor(f"bank{n}", [P, 512], F32))[:, :] for n in range(8)]
        bmask_b = misc[:, 0:8]
        bmask_c = misc[:, 8:40].rearrange("p (c b) -> p c b", b=8)
        tokid = misc[:, 40:45]
        pid = misc[:, 45:46]

        toep = nc.dram_tensor("toep", [20, P, GW], F32, kind="Internal").ap()
        sbias = nc.dram_tensor("sbias", [20, NT, NK], F32, kind="Internal").ap()
        mods = nc.dram_tensor("mods", [9, 6, D], F32, kind="Internal").ap()
        fold = nc.dram_tensor("fold", [2, SEQ, 264], F32, kind="Internal").ap()
        h2rows = nc.dram_tensor("h2rows", [TOK, D], F32, kind="Internal").ap()
        yacc = nc.dram_tensor("yacc", [TOK + P, D], F32, kind="Internal").ap()

        slot = [at(n * SLOT, SLOT) for n in range(4)]
        hT = at(A_HT, KD, TOK)
        qT = at(A_QT, 10, TOK)
        kT = at(A_KT, 7, TOK)
        kTM = at(A_KTM, TILES, 896)
        vTM = at(A_VTM, TILES, 896)
        zT = at(A_ZT, 4, TOK)
        bT = at(A_BT, 2, TOK)
        ocT = at(A_OCT, 4, TOK)
        uext = at(A_BT, 4, UE)
        xall = at(A_QT, TILES, D)
        hbuf = at(A_KT, 2, D)
        modb = at(A_KTM, 4, D)
        ada = at(A_VTM, 6 * D)
        gains = at(A_VTM + 6 * D, 4 * D)
        crow = at(A_VTM + 10 * D, 2 * D)
        junk = at(A_VTM + 12 * D, D)
        cT = at(A_VTM + 13 * D, KD, 9)
        relT = at(A_VTM + 13 * D + 80, 20)
        oh_top = at(A_HT, 3 * GW)
        oh_smp = at(A_HT + 3 * GW, 3 * NT * NK)
        gtab = at(A_KT + 2 * D, 3 * GW)
        stab = at(ARENA - 3 * NT * NK, 3 * NT * NK)
        ping = at(A_SC, 2, UE)
        uS = at(A_SC + 2 * UE, 4, NS)
        staterow = at(A_SC + 2 * UE + 4 * NS, 512)
        uouts = at(A_SC + 2 * UE + 4 * NS, 2, 512)
        sbuf_ = at(A_SC, 3, 512)
        pTb = at(A_SC + 1536, 2, 512)
        biasP = at(ARENA - 8 * 512, 8, 512)
        stage = at(2 * SLOT, 3, PT_ * 264)
        octok = at(A_KTM, 2, 512)
        qbd = at(A_SC, 6, P)
        qbdC = at(A_SC + 768, 512)
        biasS = at(A_SC + 1280, 7, SK)
        biasRaw = at(A_SC + 1280 + 7 * SK, 7, NK)
        ktr = at(A_SC + 1280 + 7 * SK + 7 * NK, 4, 512)
        sB = at(A_QT, 2, 3 * SK)
        sC = at(A_QT + 6 * SK, 4, SK)
        stB = at(A_QT + 10 * SK, 6, P)
        stBn = at(A_QT + 10 * SK + 768, 6, P)
        stC = at(A_QT + 10 * SK + 1536, 512)
        stCn = at(A_QT + 10 * SK + 2048, 512)
        pB = at(A_KTM, 6, P)
        pBn = at(A_KTM + 768, 6, P)
        pC = at(A_KTM + 1536, 512)
        pCn = at(A_KTM + 2048, 512)
        mixT = at(A_QT, KD, TOK)
        wb = at(A_KT, 2, D)
        pw = at(A_KT + 2 * D, 4, 256)
        gsig = at(A_KTM, 6, 288)
        msum = at(A_KTM + 6 * 288, 4, 288)
        A_H2 = 24576
        A_W0 = 2 * SLOT
        A_W1 = A_QT
        h2T = at(A_HT, KD, TOK)
        mixed = at(A_H2 + 4608, TILES, D)
        ysh = mixed
        x1 = at(A_H2 + 9728, TILES, D)
        A_M = A_H2 + 14848
        gmod = at(A_M, 2, D)
        modf = at(A_M + 2 * D, 4, D)
        hbuf2 = at(A_M + 6 * D, 2, D)
        junk2 = at(A_M + 8 * D, D)
        A_R = A_M + 9 * D
        assert A_R + 3400 <= ARENA and A_W1 + 6144 + 512 * PT_ <= A_H2 + 4608
        const2 = at(A_R, 2, P)
        ones = at(A_R + 256, P)
        rbias = at(A_R + 384, NE)
        scores = at(A_R + 448, TILES, NE)
        sel = at(A_R + 768, TILES, NE)
        maskt = at(A_R + 1088, TILES, NE)
        starts = at(A_R + 1408, 4, NE)
        top8 = at(A_R + 1664, TILES, TOPK)
        idxf = at(A_R + 1704, TILES, TOPK)
        rowk = at(A_R + 1744, TILES, TOPK)
        slotf = at(A_R + 1784, TILES, TOPK)
        blkf = at(A_R + 1824, TILES, TOPK)
        rowi = arena[:, A_R + 1864:A_R + 1904].bitcast(U32)
        sloti = arena[:, A_R + 1904:A_R + 1944].bitcast(I32)
        idxu = arena[:, A_R + 1944:A_R + 1984].bitcast(U32)
        rowtok = arena[:, A_R + 1984:A_R + 1984 + NBLK + 2].bitcast(U32)
        bexpf = at(A_R + 2104, 10)
        topm = [at(A_W1 + 6144 + 512 * t, TOPK, NE) for t in range(PT_)] + [at(A_W0 + 7168, TOPK, NE)]
        prod = at(A_M + 2560, TOPK * NE)
        ohslot = at(A_M + 3072, TOPK, P)
        ohblk = at(A_M + 4096, 2, TOPK * NBLK)
        sgat = at(A_W0 + 6144, 3, 256)
        saT = at(A_W0 + 6912, 2, P)
        wexp = [at(n, 6144) for n in (A_W0, A_W1)]
        xg = at(A_M, 2, D)
        xT = at(A_M + 2048, 2, D)
        act3 = at(A_M + 4096, 6, FF)
        aT = at(A_M + 5632, 2, FF)
        yb = at(A_M + 6144, 2, D)
        g2mod = at(8 * D, 2, D)

        fills_done = sem("fills_done")
        emptied = {"A": sem("emptied_by_act"), "D": sem("emptied_by_dve")}
        slot_in = [sem(f"slot_in{n}") for n in range(4)]
        dve_step, act_step, pool_step = sem("dve_step"), sem("act_step"), sem("pool_step")
        consts_in, x_in, crow_in, gains_in, badd_in = (sem(n) for n in
                                                       ("consts_in", "x_in", "crow_in", "gains_in", "badd_in"))
        onehots_in = sem("onehots_in")
        c_exp, c_silu = sem("c_exp"), sem("c_silu")
        tables_out, mods_out, modb_in = sem("tables_out"), sem("mods_out"), sem("modb_in")
        mods_rows = sem("mods_rows")
        ssq_ready, root_ready, rn_ready, xn_ready, hA_ready, h_ready = (sem(n) for n in (
            "ssq_ready", "root_ready", "rn_ready", "xn_ready", "hA_ready", "h_ready"))
        ms_ready = sem("ms_ready")
        state_in, ubuf_ready, z_ready = sem("state_in"), sem("ubuf_ready"), sem("z_ready")
        kv_out, u_out = sem("kv_out"), sem("u_out")
        biasp_in, biass_in = sem("biasp_in"), sem("biass_in")
        max_ready, probs_ready = sem("max_ready"), sem("probs_ready")
        stage_ready, stage_out, stage_in = sem("stage_ready"), sem("stage_out"), sem("stage_in")
        oc_ready, bsum_ready = sem("oc_ready"), sem("bsum_ready")
        cm_ready, ce_ready, cw_ready = sem("cm_ready"), sem("ce_ready"), sem("cw_ready")
        qbd_ready = sem("qbd_ready")
        smax_ready, sexp_ready, sprob_ready, biass_ready = (sem(n) for n in (
            "smax_ready", "sexp_ready", "sprob_ready", "biass_ready"))
        merge_in, branches_ready, mix_ready = (sem(n) for n in ("merge_in", "branches_ready", "mix_ready"))
        xres_in, gmod_in, modf_in = sem("xres_in"), sem("gmod_in"), sem("modf_in")
        x1_ready, h2_out = sem("x1_ready"), sem("h2_out")
        moe_in, rexp_ready, masks_ready, onehot_ready = (sem(n) for n in (
            "moe_in", "rexp_ready", "masks_ready", "onehot_ready"))
        sact_ready = sem("shared_act")
        ohs_ready, tables_ready, bexp_ready = sem("ohs_ready"), sem("tables_ready"), sem("bexp_ready")
        copies_out = sem("copies_out")
        wgu_in = [sem("wgu_in0"), sem("wgu_in1")]
        wd_in = [sem("wd_in0"), sem("wd_in1")]
        xg_in = [sem("xg_in0"), sem("xg_in1")]
        y_out = [sem("y_out0"), sem("y_out1")]
        icol_ready = sem("icol_ready")
        t_done, xt_act, xt_dve, gu_done, e_ready, a_ready, at_done, at_ready, d_done, y_act, y_dve = (
            sem(n) for n in ("t_done", "xt_act", "xt_dve", "gu_done", "e_ready", "a_ready", "at_done",
                             "at_ready", "d_done", "y_act", "y_dve"))
        added, weights_in = sem("added"), sem("weights_in")
        yacc_in, cols_ready, g2_in = sem("yacc_in"), sem("cols_ready"), sem("g2_in")
        f_in = [sem(f"f_in{t}") for t in range(TILES)]
        f_ssq, f_root, f_rn, f_out = (sem(n) for n in ("f_ssq", "f_root", "f_rn", "f_out"))

        def wait_fill(eng, key):
            eng.wait_ge(fills_done, INDEX[key] + 1)
            return psb[PLAN[INDEX[key]][2]]

        def wait_emptied(eng, key):
            eng.wait_ge(emptied[PLAN[INDEX[key]][1]], RANK[key] + 1)

        def bank_for(pe, key):
            n = INDEX[key]
            bank = PLAN[n][2]
            for m in range(n - 1, -1, -1):
                if PLAN[m][2] == bank:
                    wait_emptied(pe, PLAN[m][0])
                    break
            return psb[bank]

        def slot_of(key):
            return next(s for k, s in LOADS if k == key)

        def pieces(key):
            n = {"ada": 1, "in": 1, "wc": 1, "gate": 3, "wout": 1, "wsgu": 2, "wsd": 2}.get(key[0])
            if n is None:
                n = {"c0": 2, "c1": 4, "c2": 2}[key[1]]
            return n

        def slot_total(key):
            s = slot_of(key)
            total = 0
            for k, q in LOADS:
                if q == s:
                    total += 16 * pieces(k)
                if k == key:
                    return total

        def wait_load(eng, key):
            eng.wait_ge(slot_in[slot_of(key)], slot_total(key))
            return slot[slot_of(key)]

        LAST = {("ada", g): ("ada", g) for g in range(12)}
        LAST.update({("in", 0): ("u", 3, 1), ("in", 1): ("q", 3, 1), ("in", 2): ("k", 0, 4),
                     ("in", 3): ("k", 2, 4), ("in", 4): ("v", 1, 4), ("in", 5): ("q", 7, 1),
                     ("in", 6): ("kvc", 4), ("K", "c0", 0): ("KT", 5), ("K", "c1", 0): ("KT", 13),
                     ("K", "c1", 1): ("KT", 21)})
        LAST.update({("K", "c2", q): ("KT", 22 + 8 * q + 7) for q in range(4)})
        LAST.update({("V",) + key[1:]: ("VO", last[1]) for key, last in LAST.items() if key[0] == "K"})
        LAST.update({("wc",): ("oc", KD - 1, 1)})
        LAST.update({("gate", m): ("gc", m, 1) for m in range(KD)})
        LAST.update({("wout", h): ("mix", TILES - 1, h) for h in range(2)})
        COPY_AT = [("k", 0, 0), ("k", 2, 0), ("v", 0, 0), ("v", 2, 0), ("KT", 24), ("ga", 1, 0), ("ga", 3, 0), ("ga", 5, 0)]
        U_OUTS = 2
        COPIES = 5 * NB
        KV_OUTS = 2 * (4 * 2 + 2 + 4)
        gather_ticks = sem("gather_ticks")
        ohs_used, dve_loop = sem("ohs_used"), sem("dve_loop")
        sact = at(A_R + 2760, 256)
        wtab = at(A_R + 3020, NBLK)
        addrow = arena[:, A_R + 3124:A_R + 3124 + NBLK].bitcast(U32)
        addf = at(A_R + 3230, NBLK)
        blocki = at(A_R + 2240, 4, P).bitcast(I32)

        def row_cols(x, kind, b, r):
            if kind == "C":
                return x[:, 64 * b:64 * b + 64]
            v = x.rearrange("p (b h t) -> p b h t", b=NB, h=2)[:, b]
            if kind == 0:
                return x[:, 16 * b:16 * b + 16]
            if kind == 1:
                return v[:, :, r::4]
            return v[:, :, r]

        def own_rows(step, bank, to):
            for n, (kind, b, r, p) in enumerate(KEYS[step]):
                if kind == "C":
                    yield to[1][:, 64 * b:64 * b + 64], bank[:, P * n + 64 * (b % 2):P * n + 64 * (b % 2) + 64]
                else:
                    yield (row_cols(to[0][:, 2 * kind + p, :], kind, b, r),
                           row_cols(bank[:, P * n:P * n + P], kind, b, r))

        block = ctx.enter_context(nc.Block())

        @block.sync
        def _(sp):
            def load(key):
                s = slot_of(key)
                before = None
                for k, q in LOADS:
                    if k == key:
                        break
                    if q == s:
                        before = k
                if before is not None:
                    sp.wait_ge(fills_done, INDEX[LAST[before]] + 1)
                if key == ("K", "c2", 0):
                    sp.wait_ge(fills_done, INDEX[("bT", PT_ - 1)] + 1)
                to, done = slot[s], slot_in[s]
                if key[0] == "ada":
                    g = key[1]
                    sp.dma_start(to.rearrange("p (k n) -> p k n", k=KD),
                                 w_ada[0].rearrange("(p k) n -> p k n", k=KD)[:, :, 512 * g:512 * g + 512]
                                 ).then_inc(done, 16)
                elif key[0] == "in":
                    g = key[1]
                    sp.dma_start(to.rearrange("p (k n) -> p k n", k=KD),
                                 w_in[0].rearrange("(p k) n -> p k n", k=KD)[:, :, 512 * g:512 * g + 512]
                                 ).then_inc(done, 16)
                elif key[0] in "KV":
                    kv = "KV".index(key[0])
                    if key[1] == "c0":
                        sp.dma_start(to[:, 0:1024].rearrange("p (b c) -> p b c", b=NB),
                                     cache_c[0, :, :, kv, :, :].rearrange("b i h d -> i b (h d)")).then_inc(done, 16)
                        sp.dma_start(to[:, 1024:3072].rearrange("p (b c) -> p b c", b=NB),
                                     cache_b1[0, :, :, kv, :, :].rearrange("b i h d -> i b (h d)")).then_inc(done, 16)
                    elif key[1] == "c1":
                        for b in range(4):
                            sp.dma_start(to[:, 1024 * b:1024 * b + 1024].rearrange("p (r c) -> p r c", r=4),
                                         cache_b2[0, 4 * key[2] + b, :, kv, :, :].rearrange(
                                             "(i r) h d -> i r (h d)", r=4)).then_inc(done, 16)
                    else:
                        for b in range(2):
                            sp.dma_start(to[:, 2048 * b:2048 * b + 2048].rearrange("p (r c) -> p r c", r=8),
                                         cache_b3[0, 2 * key[2] + b, :, kv, :, :].rearrange(
                                             "(i r) h d -> i r (h d)", r=16)[:, 0:8, :]).then_inc(done, 16)
                elif key[0] == "wc":
                    sp.dma_start(to.rearrange("p (k n) -> p k n", k=4),
                                 w_c_up[0].rearrange("(k p) n -> p k n", p=P)).then_inc(done, 16)
                elif key[0] == "gate":
                    for j in range(3):
                        c = GATE0 + j * D + key[1] * P
                        sp.dma_start(to[:, 1024 * j:1024 * j + 1024].rearrange("p (k n) -> p k n", k=KD),
                                     w_in[0].rearrange("(p k) n -> p k n", k=KD)[:, :, c:c + P]).then_inc(done, 16)
                elif key[0] == "wout":
                    sp.dma_start(to.rearrange("p (k n) -> p k n", k=KD),
                                 w_out[0].rearrange("(k p) n -> p k n", p=P)[:, :, 512 * key[1]:512 * key[1] + 512]
                                 ).then_inc(done, 16)
                elif key[0] == "wsgu":
                    sp.dma_start(to[:, 0:2048], ws_gate[0].rearrange("(p k) n -> p (k n)", k=KD)).then_inc(done, 16)
                    sp.dma_start(to[:, 2048:4096], ws_up[0].rearrange("(p k) n -> p (k n)", k=KD)).then_inc(done, 16)
                elif key[0] == "wsd":
                    sp.dma_start(to[:, 0:2048], ws_down[0].rearrange("(p k) n -> p (k n)", k=2)).then_inc(done, 16)
                    sp.dma_start(to[:, 2048:2560].rearrange("p (k n) -> p k n", k=KD),
                                 w_router[0].rearrange("(p k) n -> p k n", k=KD)).then_inc(done, 16)

            sp.dma_start(crow[0:1, 0:D], c_prompt[:, :]).then_inc(crow_in, 16)
            sp.dma_start(crow[1:9, 0:D], c_sample[:, :]).then_inc(crow_in, 16)
            sp.dma_start(ident[:], const[:, 0:P]).then_inc(consts_in, 16)
            load(("ada", 0))
            sp.dma_start(misc[:], const[:, 3 * P:4 * P]).then_inc(consts_in, 16)
            sp.dma_start(recip[:], const[:, 4 * P:4 * P + 64].rearrange("p (g n) -> p g n", g=4)
                         ).then_inc(consts_in, 16)
            load(("ada", 1))
            sp.dma_start(xall[:, 0:PT_, :], x_prompt[0].rearrange("(t p) d -> p t d", p=P)).then_inc(x_in, 16)
            sp.dma_start(xall[0:NS, PT_, :], x_sample.rearrange("b t d -> (b t) d")).then_inc(x_in, 16)
            load(("ada", 2))
            load(("ada", 3))
            sp.dma_start(oh_top[0:BINS, :], onehot_top).then_inc(onehots_in, 16)
            sp.dma_start(oh_smp[0:BINS, :], onehot_smp).then_inc(onehots_in, 16)
            sp.dma_start(relT[0:32, :], rel_bias).then_inc(onehots_in, 16)
            sp.dma_start(ada[0:9, :], b_ada.broadcast_to([9, 6 * D])).then_inc(badd_in, 16)
            for n, g in enumerate((g_pre_mix, g_post_mix, g_pre_ffn, g_post_ffn)):
                sp.dma_start(gains[0:9, n * D:(n + 1) * D], g.broadcast_to([9, D])).then_inc(gains_in, 16)
            sp.dma_start(sinkb[:], sinks.broadcast_to([P, 8])).then_inc(gains_in, 16)
            for b in range(2):
                sp.dma_start(sinkr[64 * b:64 * b + 64, :],
                             bass.AP(tensor=sinks.tensor, offset=sinks.offset, ap=[[1, 8], [0, 8], [1, 1]])
                             ).then_inc(gains_in, 16)
            sp.dma_start(pscale[:], pool_scale[0].rearrange("(m p) -> p m", p=P), allow_slow_non_contiguous=True).then_inc(gains_in, 16)
            for g in range(4, 7):
                load(("ada", g))
            sp.wait_ge(mods_rows, 1)
            sp.dma_start(mods[:, 0:2, :], ada[0:9, 0:2 * D].rearrange("p (a b) -> p a b", b=D)).then_inc(mods_out, 16)
            sp.wait_ge(mods_out, 16)

            def sample_rows(q):
                return bass.AP(tensor=mods.tensor, offset=(6 + q) * D, ap=[[6 * D, NB], [0, NT], [1, D]])

            def spread(to, rows, done):
                for n, q in enumerate(rows):
                    sp.dma_start(to[:, 2 * n, :], mods[0:1, q, :].broadcast_to([P, D])).then_inc(done, 16)
                    sp.dma_start(to[0:NS, 2 * n + 1, :], sample_rows(q)).then_inc(done, 16)

            spread(modb, (1, 0), modb_in)
            for g in range(7, 12):
                load(("ada", g))
            sp.dma_start(staterow[0:NB * PSTATE, :], state_pool[0].rearrange("b t c -> (b t) c")).then_inc(state_in, 16)
            for g in range(4):
                load(("in", g))
            wait_emptied(sp, ("gtab", 2))
            for n, h0, h1 in ((0, 0, 4), (1, 4, 8), (2, 8, 12), (0, 12, 20)):
                sp.dma_start(toep[h0:h1], gtab[h0:h1, n * GW:(n + 1) * GW].unsqueeze(1).broadcast_to(
                    [h1 - h0, P, GW])).then_inc(tables_out, 16)
            wait_emptied(sp, ("stab", 6))
            for n, h0, h1 in ((0, 0, 4), (1, 4, 8), (2, 8, 12), (0, 12, 20)):
                sp.dma_start(sbias[h0:h1].rearrange("h t k -> h (t k)"),
                             stab[h0:h1, n * NT * NK:(n + 1) * NT * NK]).then_inc(tables_out, 16)
            sp.wait_ge(mods_rows, 2)
            sp.dma_start(mods[:, 2:6, :], ada[0:9, 2 * D:6 * D].rearrange("p (a b) -> p a b", b=D)).then_inc(mods_out, 16)
            for g in range(4, 7):
                load(("in", g))
            sp.wait_ge(tables_out, 16 * 8)
            for n in range(8):
                for j in range(2 if n < 2 or n > 3 else 4):
                    if n < 2:
                        h, off, w, pos = n + 2 * j, 127, 256, 256 * j
                    elif n < 4:
                        h, off, w, pos = 4 * (n - 1) + j // 2 + 2 * (j % 2), 255, 128, 128 * j
                    else:
                        h, off, w, pos = 12 + 2 * (n - 4) + j, 127, 256, 256 * j
                    sp.dma_start(biasP[:, n, pos:pos + w],
                                 bass.AP(tensor=toep.tensor, offset=h * P * GW + off, ap=[[GW - 1, P], [1, w]])
                                 ).then_inc(biasp_in, 16)
            wait_emptied(sp, ("uout", 1))
            sp.dma_start(pool_p[0, 0], uouts[0:PSTATE, 0, :]).then_inc(u_out, 16)
            sp.dma_start(bass.AP(tensor=pool_s.tensor, offset=pool_s.offset + (PSTATE - NT) * 512,
                                 ap=[[PSTATE * 512, NB], [512, NT], [1, 512]]), uouts[0:NS, 1, :]).then_inc(u_out, 16)
            for t in range(TILES):
                for g in range(3):
                    wait_emptied(sp, ("k", g, t))
                    wait_emptied(sp, ("v", g, t))
                wait_emptied(sp, ("kvc", t))
                for kv, src in ((0, kTM), (1, vTM)):
                    if t < PT_:
                        for g in (1, 2):
                            sp.dma_start(outs_p[g][0, 0, :, kv, :, :].rearrange("(i j) h d -> j i (h d)", j=4)[t],
                                         src[:, t, 256 * g:256 * g + 256]).then_inc(kv_out, 16)
                    if t == PT_ - 1:
                        sp.dma_start(b1_p[0, 0, :, kv, :, :].rearrange("i h d -> i (h d)"),
                                     src[:, t, 0:256]).then_inc(kv_out, 16)
                        sp.dma_start(c_p[0, 0, :, kv, :, :].rearrange("i h d -> i (h d)"),
                                     src[:, t, 768:896]).then_inc(kv_out, 16)
                    if t == PT_:
                        for o, n, w, c in [(outs_s[g], CACHE[g], 256, 256 * g) for g in range(3)] + [(c_s, P, 128, 768)]:
                            sp.dma_start(bass.AP(tensor=o.tensor, offset=o.offset + (n - NT) * 2 * w + kv * w,
                                                 ap=[[n * 2 * w, NB], [2 * w, NT], [1, w]]),
                                         src[0:NS, t, c:c + w]).then_inc(kv_out, 16)
            kload = [k for k, _ in LOADS if k[0] == "K"]
            for key in kload[:3]:
                load(key)
            sp.wait_ge(stage_ready, 16)
            for g in (1, 2):
                for t in range(PT_):
                    sp.dma_start(fold[g - 1].rearrange("(i j) c -> j i c", j=4)[t],
                                 stage[:, g, t * 264:(t + 1) * 264]).then_inc(stage_out, 16)
            sp.wait_ge(stage_out, 16 * 8)
            for g in (1, 2):
                sp.dma_start(stage[:, g, :].rearrange("p (t c) -> p t c", t=PT_),
                             fold[g - 1].rearrange("(t p) c -> p t c", p=P)).then_inc(stage_in, 16)
            sp.wait_ge(fills_done, INDEX[("O", len(UNITS) - 1)] + 1)
            wait_emptied(sp, ("O", len(UNITS) - 1))
            for n in range(7):
                reps, rows, h = (NB, 2 * NT, 2 * n) if n < 6 else (2, 8 * NT, 12)
                sp.dma_start(biasRaw[:, n, :],
                             bass.AP(tensor=sbias.tensor, offset=h * NT * NK, ap=[[0, reps], [NK, rows], [1, NK]])
                             ).then_inc(biass_in, 16)
            for key in kload[3:]:
                load(key)
            for key, _ in LOADS:
                if key[0] == "V":
                    load(key)
            sp.wait_ge(fills_done, INDEX[("SnC",)] + 1)
            sp.dma_start(wb, w_b_up[0].rearrange("(k p) n -> p k n", p=P)).then_inc(merge_in, 16)
            sp.dma_start(pw, pool_w[0].rearrange("g c o -> c g o")).then_inc(merge_in, 16)
            load(("wc",))
            for m in range(3):
                load(("gate", m))
            sp.dma_start(x1[:, 0:PT_, :], x_prompt[0].rearrange("(t p) d -> p t d", p=P)).then_inc(xres_in, 16)
            sp.dma_start(x1[0:NS, PT_, :], x_sample.rearrange("b t d -> (b t) d")).then_inc(xres_in, 16)
            for m in range(3, KD - 1):
                load(("gate", m))
            load(("wout", 0))
            load(("gate", KD - 1))
            load(("wout", 1))
            load(("wsd",))
            sp.wait_ge(mix_ready, 2 * KD)
            sp.wait_ge(mods_out, 32)
            spread(gmod, (2,), gmod_in)
            spread(modf, (4, 3), modf_in)
            sp.dma_start(const2, const[:, P:3 * P].rearrange("p (a b) -> p a b", b=P)).then_inc(moe_in, 16)
            sp.dma_start(rbias, router_bias.broadcast_to([P, NE])).then_inc(moe_in, 16)
            load(("wsgu",))
            for t in range(TILES):
                n = parts(t)
                sp.wait_ge(h_ready, TILES + t + 1)
                sp.dma_start(h2rows[toks(t), :], hbuf2[0:n, t % 2, :]).then_inc(h2_out, 16)
                if t + 1 < TILES:
                    sp.wait_ge(h2_out, 16 * (t + 1))
            def expert_weights(j, e, done):
                if done is not None:
                    sp.wait_ge(gu_done, done)
                sp.dma_start(wexp[j][:, 0:2048],
                             we_gate[0, e].rearrange("a (p k) n -> p (a k n)", k=KD)).then_inc(wgu_in[j], 16)
                sp.dma_start(wexp[j][:, 2048:4096],
                             we_up[0, e].rearrange("a (p k) n -> p (a k n)", k=KD)).then_inc(wgu_in[j], 16)
                if done is not None:
                    sp.wait_ge(d_done, done)
                sp.dma_start(wexp[j][:, 4096:6144],
                             we_down[0, e].rearrange("a (p k) n -> p (a k n)", k=2)).then_inc(wd_in[j], 16)

            for t in range(TILES):
                wait_emptied(sp, ("sy", t, 1))
                sp.dma_start(yacc[toks(t), :], ysh[0:parts(t), t, :]).then_inc(yacc_in, 16)
            sp.dma_start(yacc[TOK:TOK + P, :], ysh[:, 0, :]).then_inc(yacc_in, 16)
            sp.wait_ge(tables_ready, 1)
            for j in range(2):
                expert = sp.value_load(blocki[0:1, 3, j:j + 1], min_val=0, max_val=NE - 1)
                expert_weights(j, bass.ds(expert, 1), None)
            more = sp.value_load(pairs[0:1, 1:2], min_val=1, max_val=NE // 2 - 1)
            with sp.Fori(0, more) as i:
                for j in range(2):
                    expert = sp.value_load(blocki[0:1, 3, bass.ds(2 * i + (j + 2), 1)], min_val=0, max_val=NE - 1)
                    done = sp.value_load(blocki[0:1, 3, bass.ds(2 * i + (j + NE), 1)], min_val=2, max_val=NBLK + 2)
                    expert_weights(j, bass.ds(expert, 1), done)
            n_pairs = sp.value_load(pairs[0:1, 0:1], min_val=1, max_val=NBLK // 2)
            sp.wait_ge(d_done, 2 * n_pairs + 2)
            sp.wait_ge(wgu_in[1], 32 * more + 64)
            sp.wait_ge(wd_in[1], 16 * more + 32)
            sp.dma_start(g2mod[:, 0, :], mods[0:1, 5, :].broadcast_to([P, D])).then_inc(g2_in, 16)
            sp.dma_start(g2mod[0:NS, 1, :], sample_rows(5)).then_inc(g2_in, 16)
            for j in range(2):
                sp.wait_ge(y_out[j], 16 * n_pairs)
            for t in range(TILES):
                sp.dma_start(ysh[0:parts(t), t, :], yacc[toks(t), :]).then_inc(f_in[t], 16)
            for j in range(2):
                sp.wait_ge(xg_in[j], 16 * n_pairs + 16)
            for t in range(TILES):
                sp.wait_ge(f_out, t + 1)
                if t < PT_:
                    sp.dma_start(y_p[0, toks(t), :], x1[:, t, :]).then_inc(kv_out, 16)
                else:
                    sp.dma_start(y_s.rearrange("b t d -> (b t) d"), x1[0:NS, t, :]).then_inc(kv_out, 16)
            sp.wait_ge(kv_out, 16 * (KV_OUTS + TILES))
            sp.wait_ge(u_out, 16 * U_OUTS)
            sp.wait_ge(copies_out, 16 * COPIES)

        @block.gpsimd
        def _(pool):
            steps = [0]

            def link(ins):
                steps[0] += 1
                ins.then_inc(pool_step, 1)
                pool.wait_ge(pool_step, steps[0])

            for t in range(TILES):
                n = parts(t)
                s = t // PT_
                pool.wait_ge(hA_ready, t + 1)
                if t == 0:
                    pool.wait_ge(modb_in, 16 * 4)
                pool.tensor_tensor(hbuf[0:n, t % 2, :], hbuf[0:n, t % 2, :], modb[0:n, 2 + s, :],
                                   ALU.add).then_inc(h_ready, 1)
            for g, win in enumerate(POOLW):
                for h in range(2):
                    wait_emptied(pool, ("u", g, h))
                if g == 0:
                    wait_emptied(pool, ("state",))
                    pool.wait_ge(ubuf_ready, 1)
                u = uext[:, g, :]
                src = u
                w = 1
                n = 0
                while w < win:
                    dst = ping[:, n % 2, :]
                    lo = 2 * w - 1
                    pool.tensor_tensor(dst[:, lo:528], src[:, lo:528], src[:, lo - w:528 - w], ALU.add)
                    sv = src[:, 528:UE].rearrange("p (b t) -> p b t", b=NB)
                    dv = dst[:, 528:UE].rearrange("p (b t) -> p b t", b=NB)
                    link(pool.tensor_tensor(dv[:, :, lo:], sv[:, :, lo:], sv[:, :, lo - w:PSTATE + NT - w], ALU.add))
                    src = dst
                    w *= 2
                    n += 1
                m = ping[:, n % 2, :]
                pool.wait_ge(consts_in, 48)
                pool.tensor_tensor(m[:, 16:32], src[:, 16:32], recip[:, g, :], ALU.mult)
                pool.tensor_scalar(m[:, 32:528], src[:, 32:528], 1.0 / win, 0.0, ALU.mult, ALU.add)
                mv = m[:, 528:UE].rearrange("p (b t) -> p b t", b=NB)
                sv = src[:, 528:UE].rearrange("p (b t) -> p b t", b=NB)
                link(pool.tensor_scalar(mv[:, :, PSTATE:], sv[:, :, PSTATE:], 1.0 / win, 0.0, ALU.mult, ALU.add))
                pool.wait_ge(mods_out, 32)
                pool.tensor_tensor(zT[:, g, 0:SEQ], m[:, 16:528], u[:, 16:528], ALU.subtract)
                uv = u[:, 528:UE].rearrange("p (b t) -> p b t", b=NB)
                last = pool.tensor_tensor(zT[:, g, SEQ:TOK].rearrange("p (b t) -> p b t", b=NB),
                                          mv[:, :, PSTATE:], uv[:, :, PSTATE:], ALU.subtract)
                if g < 3:
                    link(last)
                else:
                    last.then_inc(z_ready, 1)
            for b in range(NB):
                if b == 4:
                    pool.wait_ge(cw_ready, 1)
                    sv = [stage[:, g, :].rearrange("p (t c) -> p t c", t=PT_) for g in range(3)]
                    c4 = cmb[:, :, :].rearrange("p n (t h) -> p n t h", t=PT_)
                    for g in range(3):
                        for t in range(PT_):
                            v = sv[g][:, t, 0:256].rearrange("p (h d) -> p h d", h=4)
                            ins = pool.tensor_tensor(v, v, c4[:, 4 + g, t].unsqueeze(2).broadcast_to([P, 4, HD]),
                                                     ALU.mult)
                    link(ins)
                    link(pool.tensor_tensor(sv[0][:, :, 0:256], sv[0][:, :, 0:256], sv[1][:, :, 0:256], ALU.add))
                    pool.tensor_tensor(sv[0][:, :, 0:256], sv[0][:, :, 0:256], sv[2][:, :, 0:256],
                                       ALU.add).then_inc(bsum_ready, 1)
                wait_fill(pool, COPY_AT[b])
                for c, o, n in ((cache_b3, b3_s, CACHE[2]), (cache_b2, b2_s, CACHE[1]),
                                (cache_b1, b1_s, CACHE[0]), (cache_c, c_s, P)):
                    pool.dma_start(o[0, b, 0:n - NT].rearrange("i v h d -> i (v h d)"),
                                   c[0, b, NT:n].rearrange("i v h d -> i (v h d)")).then_inc(copies_out, 16)
                pool.dma_start(pool_s[0, b, 0:PSTATE - NT, :], state_pool[0, b, NT:PSTATE, :]).then_inc(copies_out, 16)
            for t in range(TILES):
                n = parts(t)
                s = t // PT_
                pool.wait_ge(hA_ready, TILES + t + 1)
                pool.tensor_tensor(hbuf2[0:n, t % 2, :], hbuf2[0:n, t % 2, :], modf[0:n, 2 + s, :],
                                   ALU.add).then_inc(h_ready, 1)
            pool.wait_ge(h2_out, 16 * TILES)
            pool.wait_ge(tables_ready, 1)
            n_pairs = pool.value_load(pairs[0:1, 0:1], min_val=1, max_val=NBLK // 2)
            pool.sem_inc(added, 2)

            for j in range(2):
                pool.tensor_copy(icol[:, j:j + 1], rowtok[:, j:j + 1]).then_inc(icol_ready, 1)
                pool.wait_ge(icol_ready, j + 1)
                pool.indirect_dma_start(xg[:, j, :], None, h2rows,
                                        bass.IndirectOffsetOnAxis(ap=icol[:, j:j + 1], axis=0)
                                        ).then_inc(xg_in[j], 16)
            pool.wait_ge(yacc_in, 16 * (TILES + 1))
            with pool.Fori(0, n_pairs) as i:
                for j in range(2):
                    pool.wait_ge(t_done, 2 * i + j + 3)
                    pool.tensor_copy(icol[:, j:j + 1], rowtok[:, bass.ds(2 * i + j + 2, 1)]).then_inc(icol_ready, 1)
                    pool.wait_ge(icol_ready, 2 * i + j + 3)
                    pool.sem_inc(gather_ticks, 1)
                    pool.indirect_dma_start(xg[:, j, :], None, h2rows,
                                            bass.IndirectOffsetOnAxis(ap=icol[:, j:j + 1], axis=0)
                                            ).then_inc(xg_in[j], 16)
                for j in range(2):
                    pool.tensor_copy(scol[:, j:j + 1], addrow[:, bass.ds(2 * i + j, 1)]).then_inc(cols_ready, 1)
                    pool.tensor_copy(wcol[:, j:j + 1], wtab[:, bass.ds(2 * i + j, 1)]).then_inc(cols_ready, 1)
                pool.wait_ge(cols_ready, 4 * i + 4)
                for j in range(2):
                    pool.wait_ge(y_act, 2 * i + j + 2)
                    pool.wait_ge(y_dve, 2 * i + j + 2)
                    pool.sem_inc(gather_ticks, 1)
                    pool.indirect_dma_start(yacc, bass.IndirectOffsetOnAxis(ap=scol[:, j:j + 1], axis=0),
                                            yb[:, j, :], None, compute_op=ALU.add).then_inc(y_out[j], 16)
                    pool.wait_ge(y_out[j], 16 * i + 16)
                    pool.sem_inc(added, 1)

        @block.scalar
        def _(act):
            steps = [0]

            def link(ins):
                steps[0] += 1
                ins.then_inc(act_step, 1)
                act.wait_ge(act_step, steps[0])

            def empty(key, out, pick=lambda b: b):
                bank = wait_fill(act, key)
                act.activation(out, pick(bank), ACT.Copy).then_inc(emptied["A"], 1)

            act.wait_ge(crow_in, 32)
            act.activation(crow[0:9, D:2 * D], crow[0:9, 0:D], ACT.Exp, scale=-1.0).then_inc(c_exp, 1)

            act.wait_ge(x_in, 32)
            act.wait_ge(ubuf_ready, 1)
            for t in range(TILES):
                r = parts(t)
                if t:
                    act.wait_ge(ssq_ready, t)
                act.activation(junk[0:r, :], xall[0:r, t, :], ACT.Square,
                               accum_out=stat[0:r, 0, t:t + 1]).then_inc(ssq_ready, 1)
            act.wait_ge(ms_ready, 1)
            act.activation(stat[:, 0, :], stat[:, 0, :], ACT.Sqrt).then_inc(root_ready, 1)
            for n in range(7):
                w = min(480, 3 * NT * NK - 480 * n)
                empty(("stab", n), stab[0:20, 480 * n:480 * n + w], lambda b: b[0:20, 0:w])

            act.wait_ge(rn_ready, 1)
            for t in range(TILES + 1):
                if t < TILES:
                    r = parts(t)
                    if t >= 2:
                        wait_fill(act, ("hT", t - 2, 1))
                    act.activation(hbuf[0:r, t % 2, :], xall[0:r, t, :], ACT.Copy,
                                   scale=stat[0:r, 0, t:t + 1]).then_inc(xn_ready, 1)
                if t >= 1:
                    u = t - 1
                    r = parts(u)
                    empty(("hT", u, 0), hT[:, 0:4, toks(u)],
                          lambda b: b[:, 0:4 * r].rearrange("p (k n) -> p k n", k=4))
            act.wait_ge(mods_rows, 2)
            for c in range(4):
                empty(("u", c, 0), uext[:, c, 16:304], lambda b: b[:, 0:288])
            for c in range(6):
                empty(("q", c, 0), qT[:, c, 0:288], lambda b: b[:, 0:288])
            for g in range(3):
                for t in range(0, TILES, 2):
                    r = parts(t)
                    empty(("k", g, t), kTM[0:r, t, 256 * g:256 * g + 256], lambda b: b[0:r, 0:256])
            act.wait_ge(mods_out, 32)
            for g in range(3):
                for t in range(0, TILES, 2):
                    r = parts(t)
                    empty(("v", g, t), vTM[0:r, t, 256 * g:256 * g + 256], lambda b: b[0:r, 0:256])
            for c in range(6, 10):
                bank = wait_fill(act, ("q", c, 0))
                for e in range(2):
                    h = 2 * (c - 6) + e
                    ins = act.activation(qT[64 * (h // 4):64 * (h // 4) + 64, 6 + h % 4, 0:288],
                                         bank[64 * e:64 * e + 64, 0:288], ACT.Copy)
                ins.then_inc(emptied["A"], 1)
            for t in range(0, TILES, 2):
                r = parts(t)
                bank = wait_fill(act, ("kvc", t))
                act.activation(kTM[0:r, t, 768:896], bank[0:r, 0:128], ACT.Copy)
                act.activation(vTM[0:r, t, 768:896], bank[0:r, 128:256], ACT.Copy).then_inc(emptied["A"], 1)
            act.wait_ge(z_ready, 1)
            empty(("uout", 0), uouts[0:PSTATE, 0, :], lambda b: b[0:PSTATE, :])
            empty(("uout", 1), uouts[0:NS, 1, :], lambda b: b[0:NS, :])
            act.wait_ge(tables_out, 16 * 8)
            for m in range(0, 7, 2):
                empty(("kT", m), kT[:, m, 0:SEQ])

            act.wait_ge(u_out, 16 * U_OUTS)
            for s in range(len(UNITS) + LAGO):
                u = s - LAGT
                if 0 <= u < len(UNITS):
                    if u >= 2:
                        wait_fill(act, ("O", u - 2))
                    nb = 2 * len(key_blocks(UNITS[u]))
                    empty(("T", u), pTb[:, u % 2, 0:P * nb], lambda b: b[:, 0:P * nb])
                if s < len(UNITS):
                    kind, t, p = UNITS[s]
                    w = head_cols(UNITS[s])
                    lo = key_blocks(UNITS[s])[0][1]
                    act.wait_ge(max_ready, s + 1)
                    if kind == "C":
                        for h in range(2):
                            act.activation(dsk[:, s % 4, h:h + 1], sinkb[:, 2 * p + h:2 * p + h + 1], ACT.Exp,
                                           scale=-1.0, bias=nmx[:, s % 4, h:h + 1])
                    for h in range(2):
                        v = sbuf_[:, s % 3, h * w + lo:(h + 1) * w]
                        ins = act.activation(v, v, ACT.Exp, bias=nmx[:, s % 4, h:h + 1],
                                             accum_out=den[:, s % 4, h:h + 1])
                    ins.then_inc(probs_ready, 1)
                if s - LAGO == COMBINE_AT:
                    act.wait_ge(cm_ready, 1)
                    act.activation(cmb[:, 1:4, :], cmb[:, 1:4, :], ACT.Exp).then_inc(ce_ready, 1)
                for key in after_unit(s - LAGO):
                    if key[0] == "ocT":
                        empty(key, ocT[:, :, toks(key[1])], lambda b: b[:, :].rearrange("p (c n) -> p c n", c=4))
                    else:
                        empty(key, bT[:, :, toks(key[1])], lambda b: b[:, 0:256].rearrange("p (c n) -> p c n", c=2))

            empty(("Sn", 0), stBn[0:NS, 0:4, :], lambda b: b[0:NS, :].rearrange("p (c n) -> p c n", c=4))
            empty(("Sn", 1), stBn[0:NS, 4:6, :], lambda b: b[0:NS, 0:256].rearrange("p (c n) -> p c n", c=2))
            empty(("SnC",), stCn[0:NS, :], lambda b: b[0:NS, :])
            for s in range(NKF + 1):
                if s % 2 == 0:
                    if s < NKF:
                        if s >= 4:
                            wait_fill(act, ("SM", s - 4))
                        empty(("KT", s), ktr[:, s % 4, :])
                    if s >= 1:
                        bank = wait_fill(act, ("SM", s - 1))
                        for to, src in own_rows(s - 1, bank, (stB, stC)):
                            ins = act.activation(to, src, ACT.Copy)
                        ins.then_inc(emptied["A"], 1)
            act.wait_ge(smax_ready, 1)
            act.activation(sst[:, 2, :], sst[:, 0, :], ACT.Exp, bias=sinkr[:, 0:1])
            for c in range(4):
                act.activation(sC[:, c, :], sC[:, c, :], ACT.Exp, bias=sst[:, 0, c:c + 1],
                               accum_out=sst[:, 1, c:c + 1])
            act.wait_ge(smax_ready, 2)
            for p in range(2):
                ins = act.activation(sB[:, p, :], sB[:, p, :], ACT.Exp, bias=sst[:, 3, p:p + 1],
                                     accum_out=sst[:, 4, p:p + 1])
            ins.then_inc(sexp_ready, 1)
            empty(("PTC",), pC)
            for p in range(2):
                empty(("PT", p), pB[:, 3 * p:3 * p + 3, :],
                      lambda b: b[:, 0:3 * P].rearrange("p (c n) -> p c n", c=3))

            for s in range(0, NKF, 2):
                bank = wait_fill(act, ("VO", s))
                for to, src in own_rows(s, bank, (stB, stC)):
                    ins = act.activation(to, src, ACT.Copy)
                ins.then_inc(emptied["A"], 1)
            for m in range(KD):
                for h in range(2):
                    n = 2 * m + h
                    for j, what in enumerate(("ga", "gb", "gc")):
                        if j == 0 and n >= 2:
                            act.wait_ge(mix_ready, n - 1)
                        bank = wait_fill(act, (what, m, h))
                        act.activation(gsig[:, 3 * h + j, :], bank[:, 0:288], ACT.Sigmoid).then_inc(emptied["A"], 1)

            def norm_tile(n, t, src):
                r = parts(t)
                k = 2 * t + n
                act.wait_ge(ssq_ready, TILES + k - 1)
                act.activation(junk2[0:r, :], src[0:r, t, :], ACT.Square,
                               accum_out=stat[0:r, n, t:t + 1]).then_inc(ssq_ready, 1)
                act.wait_ge(ms_ready, k + 1)
                act.activation(stat[0:r, n, t:t + 1], stat[0:r, n, t:t + 1], ACT.Sqrt).then_inc(root_ready, 1)

            def rows_in(t):
                r = parts(t)
                empty(("h2T", t, 0), h2T[:, 0:4, toks(t)],
                      lambda b: b[:, 0:4 * r].rearrange("p (k n) -> p k n", k=4))

            def routed(t):
                r = parts(t)
                bank = wait_fill(act, ("rt", t))
                act.activation(scores[0:r, t, :], bank[0:r, 0:NE], ACT.Exp, scale=-1.0).then_inc(emptied["A"], 1)

            for t in range(TILES):
                r = parts(t)
                empty(("mix", t, 0), mixed[0:r, t, 0:512], lambda b: b[0:r, :])
                wait_emptied(act, ("mix", t, 0))
                wait_emptied(act, ("mix", t, 1))
                norm_tile(1, t, mixed)
                if t >= 2:
                    rows_in(t - 2)
                act.wait_ge(x1_ready, t + 1)
                norm_tile(2, t, x1)
                act.wait_ge(rn_ready, 2 * t + 3)
                if t >= 2:
                    wait_fill(act, ("h2T", t - 2, 1))
                    act.wait_ge(h2_out, 16 * (t - 1))
                act.activation(hbuf2[0:r, t % 2, :], x1[0:r, t, :], ACT.Copy,
                               scale=stat[0:r, 2, t:t + 1]).then_inc(xn_ready, 1)
                if t >= 2:
                    routed(t - 2)

            def shared_rest(t):
                r = parts(t)
                empty(("saT", t), saT[:, :, 0:r], lambda b: b[:, 0:2 * r].rearrange("p (k n) -> p k n", k=2))
                for h in range(2):
                    empty(("sy", t, h), ysh[0:r, t, 512 * h:512 * h + 512], lambda b: b[0:r, :])

            def shared_in(t):
                r = parts(t)
                bank = wait_fill(act, ("sgu", t))
                if t >= 1:
                    act.wait_ge(sact_ready, t)
                act.activation(sgat[0:r, 0, :], bank[0:r, 0:FF], ACT.Silu)
                act.activation(sgat[0:r, 1, :], bank[0:r, FF:2 * FF], ACT.Copy).then_inc(emptied["A"], 1)

            rows_in(TILES - 2)
            routed(TILES - 2)
            shared_in(0)
            rows_in(TILES - 1)
            routed(TILES - 1)
            for t in range(1, TILES):
                shared_in(t)
                shared_rest(t - 1)
            shared_rest(TILES - 1)

            act.wait_ge(tables_ready, 1)
            n_pairs = act.value_load(pairs[0:1, 0:1], min_val=1, max_val=NBLK // 2)
            act.sem_inc(wgu_in[1], 32)
            act.sem_inc(wd_in[1], 16)

            def loads_due(n):
                return [act.value_load(blocki[0:1, side, bass.ds(n, 1)], min_val=1, max_val=NE // 2 + 1)
                        for side in range(2)]

            def weights_wait(due):
                for side in range(2):
                    act.wait_ge(wgu_in[side], 32 * due[side])
                act.sem_inc(weights_in, 1)

            weights_wait(loads_due(0))
            with act.Fori(0, n_pairs) as i:
                for j in range(2):
                    act.wait_ge(t_done, 2 * i + j + 3)
                    act.activation(xT[:, j, 0:512], psb[2 * j][:, :], ACT.Copy).then_inc(xt_act, 1)
                second = loads_due(2 * i + 1)
                weights_wait(second)
                first = loads_due(2 * i)

                def turned(j, due):
                    for side in range(2):
                        act.wait_ge(wd_in[side], 16 * due[side])
                    act.wait_ge(at_done, 2 * i + j + 1)
                    act.activation(aT[:, j, :], psb[j][:, 0:2 * P], ACT.Copy).then_inc(at_ready, 1)

                def result(j):
                    act.wait_ge(added, 2 * i + j + 1)
                    act.wait_ge(d_done, 2 * i + j + 3)
                    act.wait_ge(cols_ready, 4 * i + 2 * j + 2)
                    act.activation(yb[:, j, 0:512], psb[6 if j == 0 else 2][:, :], ACT.Copy,
                                   scale=wcol[:, j:j + 1]).then_inc(y_act, 1)

                def exps(j):
                    act.wait_ge(gu_done, 2 * i + j + 3)
                    act.activation(act3[:, 3 * j, :], psb[4 + j][:, 0:FF], ACT.Silu).then_inc(e_ready, 1)

                exps(0)
                turned(0, first)
                exps(1)
                turned(1, second)
                result(0)
                following = loads_due(2 * i + 2)
                result(1)
                weights_wait(following)

            for t in range(TILES + 1):
                if t < TILES:
                    r = parts(t)
                    act.wait_ge(f_in[t], 16)
                    if t:
                        act.wait_ge(f_ssq, t)
                    act.activation(junk2[0:r, :], ysh[0:r, t, :], ACT.Square,
                                   accum_out=stat[0:r, 3, t:t + 1]).then_inc(f_ssq, 1)
                if t >= 1:
                    r = parts(t - 1)
                    act.wait_ge(f_root, t)
                    act.activation(stat[0:r, 3, t - 1:t], stat[0:r, 3, t - 1:t], ACT.Sqrt).then_inc(f_rn, 1)

        @block.vector
        def _(dve):
            steps = [0]

            def link(ins):
                steps[0] += 1
                ins.then_inc(dve_step, 1)
                dve.wait_ge(dve_step, steps[0])

            def empty(key, out, pick=lambda b: b):
                bank = wait_fill(dve, key)
                dve.tensor_copy(out, pick(bank)).then_inc(emptied["D"], 1)

            dve.memset(relT[32:33, :], MASK).then_inc(onehot_ready, 1)
            dve.memset(stat[:], 1.0).then_inc(ubuf_ready, 1)
            dve.wait_ge(c_exp, 1)
            ce = crow[0:9, D:2 * D]
            link(dve.tensor_scalar(ce, ce, 1.0, None, ALU.add))
            link(dve.reciprocal(ce, ce))
            dve.tensor_tensor(crow[0:9, 0:D], crow[0:9, 0:D], ce, ALU.mult).then_inc(c_silu, 1)
            empty(("cT",), cT, lambda b: b[:, 0:P].rearrange("p (k n) -> p k n", k=KD)[:, :, 0:9])
            dve.wait_ge(gains_in, 16 * 8)
            link(dve.tensor_scalar(sinkb[:], sinkb[:], -1.0, None, ALU.mult))
            dve.wait_ge(badd_in, 16)

            def ada_group(g):
                bank = wait_fill(dve, ("ada", g))
                v = ada[0:9, 512 * g:512 * g + 512]
                dve.tensor_tensor(v, bank[0:9, :], v, ALU.add).then_inc(emptied["D"], 1)

            def ada_row(q, gain, plus, mark):
                v = ada[0:9, q * D:(q + 1) * D]
                wait_emptied(dve, ("ada", 2 * q + 1))
                ins = dve.scalar_tensor_tensor(v, v, plus, gains[0:9, gain * D:(gain + 1) * D], ALU.add, ALU.mult)
                if mark:
                    ins.then_inc(mods_rows, 1)

            def norm_root(st, sums, roots):
                dve.wait_ge(ssq_ready, sums)
                dve.tensor_scalar(st, st, 1.0 / D, EPS, ALU.mult, ALU.add).then_inc(ms_ready, 1)
                dve.wait_ge(root_ready, roots)
                dve.reciprocal(st, st).then_inc(rn_ready, 1)
                dve.wait_ge(rn_ready, roots)

            for g in range(4):
                ada_group(g)
            ada_row(1, 0, 1.0, True)
            norm_root(stat[:, 0, :], TILES, 1)
            for n in range(3):
                empty(("gtab", n), gtab[0:20, n * GW:(n + 1) * GW], lambda b: b[0:20, 0:GW])
            for g in range(4, 8):
                ada_group(g)

            for t in range(TILES):
                r, s = parts(t), t // PT_
                if t == 0:
                    dve.wait_ge(modb_in, 16 * 4)
                dve.wait_ge(xn_ready, t + 1)
                dve.tensor_tensor(hbuf[0:r, t % 2, :], hbuf[0:r, t % 2, :], modb[0:r, s, :],
                                  ALU.mult).then_inc(hA_ready, 1)
                if t >= 1:
                    u = t - 1
                    w = parts(u)
                    empty(("hT", u, 1), hT[:, 4:8, toks(u)], lambda b: b[:, 0:4 * w].rearrange("p (k n) -> p k n", k=4))
                    ada_group(8 + u)
            empty(("hT", PT_, 1), hT[:, 4:8, SEQ:TOK], lambda b: b[:, 0:4 * NS].rearrange("p (k n) -> p k n", k=4))
            ada_row(2, 1, 0.0, False)
            ada_row(4, 2, 1.0, False)
            ada_row(5, 3, 0.0, True)
            dve.wait_ge(mods_rows, 2)
            dve.memset(uext[:, :, 0:16], 0.0)
            bank = wait_fill(dve, ("state",))
            us = uext[:, :, 528:UE].rearrange("p g (b t) -> p g b t", b=NB)
            for g in range(4):
                ins = dve.tensor_copy(us[:, g, :, 0:PSTATE],
                                      bank[:, g * P:g * P + NB * PSTATE].rearrange("p (b t) -> p b t", b=NB))
            ins.then_inc(emptied["D"], 1)
            for c in range(4):
                bank = wait_fill(dve, ("u", c, 1))
                new = bank[:, 224:288]
                dve.tensor_copy(uext[:, c, 304:528], bank[:, 0:224])
                dve.tensor_copy(uS[:, c, :], new)
                dve.tensor_copy(us[:, c, :, PSTATE:], new.rearrange("p (b t) -> p b t", b=NB)).then_inc(emptied["D"], 1)
            for c in range(6):
                empty(("q", c, 1), qT[:, c, 288:TOK], lambda b: b[:, 0:288])
            for g in range(3):
                for t in (1, 3):
                    empty(("k", g, t), kTM[:, t, 256 * g:256 * g + 256], lambda b: b[:, 0:256])
            dve.wait_ge(mods_out, 32)
            for g in range(3):
                for t in (1, 3):
                    empty(("v", g, t), vTM[:, t, 256 * g:256 * g + 256], lambda b: b[:, 0:256])
            for c in range(6, 10):
                bank = wait_fill(dve, ("q", c, 1))
                for e in range(2):
                    h = 2 * (c - 6) + e
                    ins = dve.tensor_copy(qT[64 * (h // 4):64 * (h // 4) + 64, 6 + h % 4, 288:TOK],
                                          bank[64 * e:64 * e + 64, 0:288])
                ins.then_inc(emptied["D"], 1)
            for t in (1, 3):
                bank = wait_fill(dve, ("kvc", t))
                dve.tensor_copy(kTM[:, t, 768:896], bank[:, 0:128])
                dve.tensor_copy(vTM[:, t, 768:896], bank[:, 128:256]).then_inc(emptied["D"], 1)
            dve.wait_ge(tables_out, 16 * 8)
            for m in (1, 3, 5):
                empty(("kT", m), kT[:, m, 0:SEQ])
            empty(("kTs",), kT[:, :, SEQ:TOK], lambda b: b[:, 0:7 * NS].rearrange("p (m n) -> p m n", m=7))

            def outputs(u):
                kind, t, p = UNITS[u]
                bank = wait_fill(dve, ("O", u))
                own = 64 * (p // 2) if kind == "C" else 64 * p
                own = bank[:, 0:2 * P].rearrange("p (h d) -> p h d", h=2)[:, :, own:own + HD]
                if kind == "C":
                    if p == 0 and t >= 2:
                        wait_fill(dve, ("ocT", t - 2))
                    link(dve.tensor_tensor(rden[:, u % 4, 0:2], den[:, u % 4, 0:2], dsk[:, u % 4, 0:2], ALU.add))
                    link(dve.reciprocal(rden[:, u % 4, 0:2], rden[:, u % 4, 0:2]))
                    dve.tensor_tensor(octok[:, t % 2, 128 * p:128 * p + 128].rearrange("p (h d) -> p h d", h=2),
                                      own,
                                      rden[:, u % 4, 0:2].unsqueeze(2).broadcast_to([P, 2, HD]),
                                      ALU.mult).then_inc(emptied["D"], 1)
                else:
                    to = stage[:, kind, t * 264:(t + 1) * 264]
                    dve.tensor_copy(to[:, 256 + p:260:2], nmx[:, u % 4, 0:2])
                    dve.tensor_copy(to[:, 260 + p:264:2], den[:, u % 4, 0:2])
                    dve.tensor_copy(to[:, 0:256].rearrange("p (h g d) -> p h g d", h=2, g=2)[:, :, p, :],
                                    own).then_inc(emptied["D"], 1)
                    if kind != 0:
                        wait_emptied(dve, ("O", u))
                        dve.sem_inc(stage_ready, 1)

            def combine():
                dve.wait_ge(stage_in, 32)
                sv = [stage[:, g, :].rearrange("p (t c) -> p t c", t=PT_) for g in range(3)]
                c4 = cmb[:, :, :].rearrange("p n (t h) -> p n t h", t=PT_)
                wait_emptied(dve, ("O", 23))
                link(dve.tensor_tensor(c4[:, 0], sv[0][:, :, 256:260], sv[1][:, :, 256:260], ALU.min))
                link(dve.tensor_tensor(c4[:, 0], c4[:, 0], sv[2][:, :, 256:260], ALU.min))
                for g in range(3):
                    ins = dve.tensor_tensor(c4[:, 1 + g], c4[:, 0], sv[g][:, :, 256:260], ALU.subtract)
                ins.then_inc(cm_ready, 1)
                dve.wait_ge(ce_ready, 1)
                for g in range(3):
                    ins = dve.tensor_tensor(c4[:, 4 + g], c4[:, 1 + g], sv[g][:, :, 260:264], ALU.mult)
                link(ins)
                link(dve.tensor_tensor(cmb[:, 7, :], cmb[:, 4, :], cmb[:, 5, :], ALU.add))
                link(dve.tensor_tensor(cmb[:, 7, :], cmb[:, 7, :], cmb[:, 6, :], ALU.add))
                link(dve.reciprocal(cmb[:, 7, :], cmb[:, 7, :]))
                for g in range(3):
                    ins = dve.tensor_tensor(cmb[:, 4 + g, :], cmb[:, 1 + g, :], cmb[:, 7, :], ALU.mult)
                ins.then_inc(cw_ready, 1)

            dve.wait_ge(biasp_in, 16 * (4 + 8 + 8))
            dve.wait_ge(z_ready, 1)
            for s in range(len(UNITS) + LAGO):
                if s < len(UNITS):
                    kind, t, p = UNITS[s]
                    w = head_cols(UNITS[s])
                    lo = key_blocks(UNITS[s])[0][1]
                    bias = (biasP[:, kind + 1, 2 * P * p:2 * P * (p + 1)] if kind in (1, 2)
                            else biasP[:, p if kind == 0 else 4 + p, :])
                    bank = wait_fill(dve, ("S", s))
                    if s >= 3:
                        wait_fill(dve, ("T", s - 3))

                    def view(x):
                        return x.rearrange("p (h c) -> p h c", h=2)[:, :, lo:]

                    to = sbuf_[:, s % 3, 0:2 * w]
                    dve.scalar_tensor_tensor(view(to), view(bank[:, 0:2 * w]), SCALE, view(bias),
                                             ALU.mult, ALU.add).then_inc(emptied["D"], 1)
                    wait_emptied(dve, ("S", s))
                    nm = nmx[:, s % 4, 0:2]
                    ins = dve.tensor_reduce(nm, view(to), AX, ALU.max, negate=True)
                    if kind == "C":
                        link(ins)
                        ins = dve.tensor_tensor(nm, nm, sinkb[:, 2 * p:2 * p + 2], ALU.min)
                    ins.then_inc(max_ready, 1)
                if s == 24 + LAGO:
                    dve.wait_ge(kv_out, 16 * KV_OUTS)
                if 0 <= s - LAGO < len(UNITS):
                    outputs(s - LAGO)
                    if s - LAGO == COMBINE_AT:
                        combine()

            wait_fill(dve, ("O", len(UNITS) - 1))
            dve.memset(qbd, 0.0)
            link(dve.memset(qbdC, 0.0))
            for g in range(3):
                for p in range(2):
                    for h in range(2):
                        half = slice(64 * h, 64 * h + 64)
                        dve.tensor_copy(
                            qbd[half, 2 * g + p, :].rearrange("p (b h t) -> p b h t", b=NB, h=2)[:, :, h, :],
                            qT[half, 2 * g + p, SEQ:TOK].rearrange("p (b t) -> p b t", b=NB))
            for h in range(8):
                half = slice(64 * (h // 4), 64 * (h // 4) + 64)
                ins = dve.tensor_copy(qbdC[half, :].rearrange("p (b h t) -> p b h t", b=NB, h=8)[:, :, h, :],
                                      qT[half, 6 + h % 4, SEQ:TOK].rearrange("p (b t) -> p b t", b=NB))
            ins.then_inc(qbd_ready, 1)
            for s in range(1, NKF, 2):
                if s >= 4:
                    wait_fill(dve, ("SM", s - 4))
                empty(("KT", s), ktr[:, s % 4, :])
                bank = wait_fill(dve, ("SM", s - 1))
                for to, src in own_rows(s - 1, bank, (stB, stC)):
                    ins = dve.tensor_copy(to, src)
                ins.then_inc(emptied["D"], 1)
                if s == 21:
                    dve.wait_ge(biass_in, 16 * 7)
                    for n in range(7):
                        dve.tensor_copy(biasS[:, n, 0:P], biasRaw[:, n, 0:P])
                        new = biasRaw[:, n, P:NK].unsqueeze(1).broadcast_to([P, NB, NT])
                        to = biasS[:, n, P:SK].rearrange("p (b t) -> p b t", b=NB)
                        if n < 6:
                            ins = dve.tensor_tensor(to, new, bmask_b.unsqueeze(2).broadcast_to([P, NB, NT]), ALU.add)
                        else:
                            ins = dve.tensor_copy(to, new)
                    link(ins)
            for c in range(4):
                bank = wait_fill(dve, ("SRC", c))
                dve.scalar_tensor_tensor(sC[:, c, :], bank[:, 0:SK], SCALE, biasS[:, 6, :],
                                         ALU.mult, ALU.add).then_inc(emptied["D"], 1)
                wait_emptied(dve, ("SRC", c))
                v = sC[:, c, P:SK].rearrange("p (b t) -> p b t", b=NB)
                ins = dve.tensor_tensor(v, v, bmask_c[:, c, :].unsqueeze(2).broadcast_to([P, NB, NT]), ALU.add)
            link(ins)
            link(dve.tensor_reduce(sst[:, 0, :], sC, AX, ALU.max))
            link(dve.tensor_scalar(sst[:, 0, :], sst[:, 0, :], sinkr[:, 0:1], None, ALU.max))
            dve.tensor_scalar(sst[:, 0, :], sst[:, 0, :], -1.0, None, ALU.mult).then_inc(smax_ready, 1)
            for g in range(3):
                for p in range(2):
                    bank = wait_fill(dve, ("SR", g, p))
                    dve.scalar_tensor_tensor(sB[:, p, g * SK:(g + 1) * SK], bank[:, 0:SK], SCALE,
                                             biasS[:, 2 * g + p, :], ALU.mult, ALU.add).then_inc(emptied["D"], 1)
            wait_emptied(dve, ("SR", 2, 1))
            dve.tensor_reduce(sst[:, 3, 0:2], sB, AX, ALU.max, negate=True).then_inc(smax_ready, 1)
            dve.wait_ge(sexp_ready, 1)
            link(dve.tensor_tensor(sst[:, 1, :], sst[:, 1, :], sst[:, 2, :], ALU.add))
            link(dve.reciprocal(sst[:, 1, :], sst[:, 1, :]))
            link(dve.reciprocal(sst[:, 4, 0:2], sst[:, 4, 0:2]))
            for c in range(4):
                dve.tensor_scalar(sC[:, c, :], sC[:, c, :], sst[:, 1, c:c + 1], None, ALU.mult)
            for p in range(2):
                ins = dve.tensor_scalar(sB[:, p, :], sB[:, p, :], sst[:, 4, p:p + 1], None, ALU.mult)
            ins.then_inc(sprob_ready, 1)
            empty(("PTCn",), pCn[0:NS, :], lambda b: b[0:NS, :])
            for p in range(2):
                empty(("PTn", p), pBn[0:NS, 3 * p:3 * p + 3, :],
                      lambda b: b[0:NS, 0:3 * P].rearrange("p (c n) -> p c n", c=3))
            empty(("OC",), stCn)
            for p in range(2):
                empty(("OB", p), stBn[:, p, :], lambda b: b[:, 0:P])
            for s in range(1, NKF, 2):
                bank = wait_fill(dve, ("VO", s))
                for to, src in own_rows(s, bank, (stB, stC)):
                    ins = dve.tensor_copy(to, src)
                ins.then_inc(emptied["D"], 1)
            wait_emptied(dve, ("OB", 1))
            for n in range(NKF - 2, NKF):
                wait_emptied(dve, ("VO", n))
            dve.tensor_tensor(stCn, stCn, stC, ALU.add)
            for g in range(3):
                link(dve.tensor_tensor(stBn[:, 0:2, :], stBn[:, 0:2, :], stB[:, 2 * g:2 * g + 2, :], ALU.add))
            for h in range(8):
                src = stCn[64 * (h // 4):64 * (h // 4) + 64, :].rearrange("p (b h t) -> p b h t", b=NB, h=8)[:, :, h, :]
                dve.tensor_copy(ocT[64 * (h % 2):64 * (h % 2) + 64, h // 2, SEQ:TOK].rearrange(
                    "p (b t) -> p b t", b=NB), src)
            for p in range(2):
                for h in range(2):
                    half = slice(64 * h, 64 * h + 64)
                    ins = dve.tensor_copy(
                        bT[half, p, SEQ:TOK].rearrange("p (b t) -> p b t", b=NB),
                        stBn[half, p, :].rearrange("p (b h t) -> p b h t", b=NB, h=2)[:, :, h, :])
            ins.then_inc(branches_ready, 1)

            for m in range(KD):
                for h in range(2):
                    gs = gsig[:, 3 * h:3 * h + 3, :]
                    wait_emptied(dve, ("gc", m, h))
                    if m or h:
                        dve.wait_ge(mix_ready, 2 * m + h)
                    bank = wait_fill(dve, ("oa", m, h))
                    dve.scalar_tensor_tensor(msum[:, 0, :], bank[:, 0:288], pscale[:, m:m + 1], gs[:, 0, :],
                                             ALU.mult, ALU.mult).then_inc(emptied["D"], 1)
                    bank = wait_fill(dve, ("ob", m, h))
                    dve.tensor_tensor(msum[:, 1, :], bank[:, 0:288], gs[:, 1, :], ALU.mult).then_inc(emptied["D"], 1)
                    bank = wait_fill(dve, ("oc", m, h))
                    dve.tensor_tensor(msum[:, 2, :], bank[:, 0:288], gs[:, 2, :], ALU.mult).then_inc(emptied["D"], 1)
                    wait_emptied(dve, ("oc", m, h))
                    link(dve.tensor_tensor(msum[:, 3, :], msum[:, 0, :], msum[:, 1, :], ALU.add))
                    dve.tensor_tensor(mixT[:, m, 288 * h:288 * h + 288], msum[:, 3, :], msum[:, 2, :],
                                      ALU.add).then_inc(mix_ready, 1)

            iota = const2[:, 1, :]

            def rows_in(t):
                r = parts(t)
                empty(("h2T", t, 1), h2T[:, 4:8, toks(t)],
                      lambda b: b[:, 0:4 * r].rearrange("p (k n) -> p k n", k=4))

            def routed(t):
                r = parts(t)
                if t == 0:
                    dve.wait_ge(moe_in, 32)
                    dve.memset(ones, 1.0)
                sc, se = scores[0:r, t, :], sel[0:r, t, :]
                wait_emptied(dve, ("rt", t))
                link(dve.tensor_scalar(sc, sc, 1.0, None, ALU.add))
                link(dve.reciprocal(sc, sc))
                link(dve.tensor_tensor(se, sc, rbias[0:r, :], ALU.add))
                link(dve.max(top8[0:r, t, :], se))
                link(dve.max_index(idxu[0:r, TOPK * t:TOPK * t + TOPK], top8[0:r, t, :], se))
                link(dve.tensor_copy(idxf[0:r, t, :], idxu[0:r, TOPK * t:TOPK * t + TOPK]))
                tm = topm[t][0:r]
                link(dve.tensor_tensor(tm, iota[0:r, 0:NE].unsqueeze(1).broadcast_to([r, TOPK, NE]),
                                       idxf[0:r, t, :].unsqueeze(2).broadcast_to([r, TOPK, NE]), ALU.is_equal))
                dve.tensor_reduce(maskt[0:r, t, :], tm.rearrange("p k e -> p e k"), AX, ALU.add).then_inc(masks_ready, 1)

            for t in range(TILES):
                r, s = parts(t), t // PT_
                empty(("mix", t, 1), mixed[0:r, t, 512:1024], lambda b: b[0:r, :])
                if t >= 2:
                    rows_in(t - 2)
                norm_root(stat[0:r, 1, t:t + 1], TILES + 2 * t + 1, 2 * t + 2)
                if t == 0:
                    dve.wait_ge(gmod_in, 16 * 2)
                    dve.wait_ge(xres_in, 32)
                link(dve.scalar_tensor_tensor(mixed[0:r, t, :], mixed[0:r, t, :], stat[0:r, 1, t:t + 1],
                                              gmod[0:r, s, :], ALU.mult, ALU.mult))
                dve.tensor_tensor(x1[0:r, t, :], x1[0:r, t, :], mixed[0:r, t, :], ALU.add).then_inc(x1_ready, 1)
                norm_root(stat[0:r, 2, t:t + 1], TILES + 2 * t + 2, 2 * t + 3)
                if t == 0:
                    dve.wait_ge(modf_in, 16 * 4)
                dve.wait_ge(xn_ready, TILES + t + 1)
                dve.tensor_tensor(hbuf2[0:r, t % 2, :], hbuf2[0:r, t % 2, :], modf[0:r, s, :],
                                  ALU.mult).then_inc(hA_ready, 1)
                if t >= 2:
                    routed(t - 2)

            def shared_act(t):
                r = parts(t)
                wait_emptied(dve, ("sgu", t))
                g, u = sgat[0:r, 0, :], sgat[0:r, 1, :]
                if t >= 1:
                    wait_fill(dve, ("saT", t - 1))
                dve.tensor_tensor(sact[0:r, :], g, u, ALU.mult).then_inc(sact_ready, 1)

            rows_in(TILES - 2)
            routed(TILES - 2)
            rows_in(TILES - 1)
            shared_act(0)
            routed(TILES - 1)
            shared_act(1)
            total, nblk, ends, r0 = (starts[:, n, :] for n in range(4))
            bank = wait_fill(dve, ("cnt",))
            link(dve.tensor_copy(total, bank[:, 0:NE]))
            link(dve.tensor_scalar(nblk, total, 0.0, None, ALU.is_gt))
            for j in range(1, -(-TOK // P)):
                link(dve.scalar_tensor_tensor(nblk, total, float(P * j), nblk, ALU.is_gt, ALU.add))
            link(dve.tensor_tensor_scan(ends, ones[:, 0:NE], nblk, 0.0, ALU.mult, ALU.add))
            used, count, mine = total, prod[:, 0:NE], prod[:, NE:2 * NE]
            link(dve.tensor_scalar(used, nblk, 0.0, None, ALU.is_gt))
            link(dve.tensor_tensor_scan(count, ones[:, 0:NE], used, 0.0, ALU.mult, ALU.add))
            link(dve.tensor_copy(bexpf[:, 8:9], count[:, NE - 1:NE]))
            link(dve.tensor_scalar(mine, count, pid, 1.0, ALU.subtract, ALU.is_equal))
            link(dve.tensor_tensor(mine, mine, used, ALU.mult))
            link(dve.tensor_tensor(count, mine, iota[:, 0:NE], ALU.mult))
            link(dve.tensor_reduce(bexpf[:, 6:7], count, AX, ALU.add))
            link(dve.tensor_tensor(count, mine, ends, ALU.mult))
            link(dve.tensor_reduce(bexpf[:, 7:8], count, AX, ALU.add))
            link(dve.tensor_scalar(bexpf[:, 7:8], bexpf[:, 7:8], 2.0, None, ALU.add))
            link(dve.tensor_tensor(r0, ends, nblk, ALU.subtract))
            link(dve.tensor_scalar(r0, r0, float(P), None, ALU.mult))
            for t in range(TILES):
                r = parts(t)
                bank = wait_fill(dve, ("pos", t))
                dve.tensor_tensor(sel[0:r, t, :], bank[0:r, 0:NE], r0[0:r, :], ALU.add).then_inc(emptied["D"], 1)
            dve.tensor_copy(nblk[0:1, 0:1], wait_fill(dve, ("cnt",))[0:1, 0:1]).then_inc(emptied["D"], 1)
            wait_emptied(dve, ("cnt",))
            for t in range(TILES):
                r = parts(t)
                tm = topm[t][0:r]
                pr = prod[0:r, :].rearrange("p (k e) -> p k e", k=TOPK)
                link(dve.tensor_tensor(pr, tm, sel[0:r, t, :].unsqueeze(1).broadcast_to([r, TOPK, NE]), ALU.mult))
                link(dve.tensor_reduce(rowk[0:r, t, :], pr, AX, ALU.add))
                link(dve.tensor_tensor(pr, tm, scores[0:r, t, :].unsqueeze(1).broadcast_to([r, TOPK, NE]), ALU.mult))
                link(dve.tensor_reduce(wts[0:r, t, :], pr, AX, ALU.add))
                link(dve.tensor_reduce(bexpf[0:r, 1:2], wts[0:r, t, :], AX, ALU.add))
                link(dve.reciprocal(bexpf[0:r, 1:2], bexpf[0:r, 1:2]))
                link(dve.tensor_scalar(wts[0:r, t, :], wts[0:r, t, :], bexpf[0:r, 1:2], RSCALE, ALU.mult, ALU.mult))
                cols = slice(TOPK * t, TOPK * t + TOPK)
                link(dve.tensor_copy(rowi[0:r, cols], rowk[0:r, t, :]))
                ri = rowi[0:r, cols].bitcast(I32)
                link(dve.tensor_scalar(sloti[0:r, cols], ri, P - 1, None, ALU.bitwise_and))
                link(dve.tensor_copy(slotf[0:r, t, :], sloti[0:r, cols]))
                link(dve.tensor_tensor(blkf[0:r, t, :], rowk[0:r, t, :], slotf[0:r, t, :], ALU.subtract))
                link(dve.tensor_scalar(blkf[0:r, t, :], blkf[0:r, t, :], 1.0 / P, None, ALU.mult))
                if t >= 1:
                    dve.wait_ge(ohs_used, t)
                dve.tensor_tensor(ohslot[0:r], iota[0:r, :].unsqueeze(1).broadcast_to([r, TOPK, P]),
                                  slotf[0:r, t, :].unsqueeze(2).broadcast_to([r, TOPK, P]), ALU.is_equal)
                ob = [ohblk[0:r, n, :].rearrange("p (k n) -> p k n", k=TOPK) for n in range(2)]
                link(dve.tensor_tensor(ob[0], iota[0:r, 0:NBLK].unsqueeze(1).broadcast_to([r, TOPK, NBLK]),
                                       blkf[0:r, t, :].unsqueeze(2).broadcast_to([r, TOPK, NBLK]), ALU.is_equal))
                link(dve.tensor_tensor(ob[1], ob[0], wts[0:r, t, :].unsqueeze(2).broadcast_to([r, TOPK, NBLK]),
                                       ALU.mult))
                dve.tensor_scalar(ob[0], ob[0], tokid[0:r, t:t + 1], None, ALU.mult).then_inc(ohs_ready, 1)
                if t + 2 < TILES:
                    shared_act(t + 2)
            link(dve.tensor_scalar(prod[:, 0:NE], ends, pid, None, ALU.is_le))
            link(dve.tensor_tensor(prod[:, 0:NE], prod[:, 0:NE], used, ALU.mult))
            link(dve.tensor_reduce(bexpf[:, 0:1], prod[:, 0:NE], AX, ALU.add))
            link(dve.tensor_scalar(bexpf[:, 1:2], bexpf[:, 8:9], -1.0, None, ALU.add))
            link(dve.tensor_tensor(bexpf[:, 0:1], bexpf[:, 0:1], bexpf[:, 1:2], ALU.min))
            link(dve.tensor_copy(rowi[:, 0:1], bexpf[:, 0:1]))
            link(dve.tensor_scalar(sloti[:, 0:1], rowi[:, 0:1].bitcast(I32), 1, None, ALU.bitwise_and))
            link(dve.tensor_copy(bexpf[:, 5:6], sloti[:, 0:1]))
            link(dve.tensor_tensor(bexpf[:, 3:4], bexpf[:, 0:1], bexpf[:, 5:6], ALU.subtract))
            link(dve.tensor_tensor(bexpf[:, 4:5], bexpf[:, 0:1], bexpf[:, 5:6], ALU.add))
            dve.tensor_scalar(bexpf[:, 3:5], bexpf[:, 3:5], 0.5, 1.0, ALU.mult, ALU.add).then_inc(bexp_ready, 1)
            link(dve.tensor_scalar(prod[:, 0:NE], iota[:, 0:NE], 2.0, None, ALU.mult))
            link(dve.tensor_scalar(prod[:, 0:NE], prod[:, 0:NE], ends[:, NE - 1:NE], None, ALU.is_lt, ALU.add,
                                   accum_out=bexpf[:, 2:3]))
            link(dve.tensor_scalar(prod[:, 0:NE], iota[:, 0:NE], 2.0, None, ALU.mult))
            link(dve.tensor_scalar(prod[:, 0:NE], prod[:, 0:NE], bexpf[:, 8:9], None, ALU.is_lt, ALU.add,
                                   accum_out=bexpf[:, 9:10]))
            link(dve.tensor_scalar(bexpf[:, 9:10], bexpf[:, 9:10], -1.0, None, ALU.add))
            dve.memset(rowtok[:, NBLK:NBLK + 2], 0)
            bank = wait_fill(dve, ("rowtok",))
            dve.tensor_copy(rowtok[:, 0:NBLK], bank[:, 0:NBLK])
            link(dve.tensor_copy(wtab, bank[:, NBLK:2 * NBLK]))
            link(dve.tensor_scalar(prod[:, NBLK:NBLK + 1], pid, float(TOK), None, ALU.add))
            link(dve.tensor_scalar(addf, wtab, 0.0, None, ALU.is_gt))
            link(dve.tensor_tensor(addf, bank[:, 0:NBLK], addf, ALU.mult))
            link(dve.tensor_scalar(prod[:, 0:NBLK], wtab, 0.0, prod[:, NBLK:NBLK + 1], ALU.is_le, ALU.mult))
            link(dve.tensor_tensor(addf, addf, prod[:, 0:NBLK], ALU.add))
            dve.tensor_copy(addrow, addf).then_inc(emptied["D"], 1)
            empty(("bexp",), blocki[0:1], lambda b: b[0:1, :].rearrange("p (n b) -> p n b", n=4))
            wait_emptied(dve, ("bexp",))
            dve.tensor_copy(pairs[:, 1:2], bexpf[:, 9:10])
            dve.tensor_copy(pairs[:, 0:1], bexpf[:, 2:3]).then_inc(tables_ready, 1)
            dve.wait_ge(tables_ready, 1)

            n_pairs = dve.value_load(pairs[0:1, 0:1], min_val=1, max_val=NBLK // 2)
            with dve.Fori(0, n_pairs) as i:
                for j in range(2):
                    dve.wait_ge(t_done, 2 * i + j + 3)
                    dve.tensor_copy(xT[:, j, 512:1024], psb[2 * j + 1][:, :]).then_inc(xt_dve, 1)
                for j in range(2):
                    e, a = (act3[:, 3 * j + n, :] for n in (0, 2))
                    dve.wait_ge(e_ready, 2 * i + j + 1)
                    dve.tensor_tensor(a, psb[4 + j][:, FF:2 * FF], e, ALU.mult).then_inc(a_ready, 1)
                for j in range(2):
                    dve.wait_ge(added, 2 * i + j + 1)
                    dve.wait_ge(d_done, 2 * i + j + 3)
                    dve.wait_ge(cols_ready, 4 * i + 2 * j + 2)
                    dve.tensor_scalar(yb[:, j, 512:1024], psb[7 if j == 0 else 3][:, :], wcol[:, j:j + 1], None,
                                      ALU.mult).then_inc(y_dve, 1)

            for t in range(TILES + 1):
                if t < TILES:
                    st = stat[0:parts(t), 3, t:t + 1]
                    dve.wait_ge(f_ssq, t + 1)
                    dve.tensor_scalar(st, st, 1.0 / D, EPS, ALU.mult, ALU.add).then_inc(f_root, 1)
                if t >= 1:
                    u = t - 1
                    r, s = parts(u), u // PT_
                    y, st = ysh[0:r, u, :], stat[0:r, 3, u:u + 1]
                    dve.wait_ge(f_rn, u + 1)
                    link(dve.reciprocal(st, st))
                    if u == 0:
                        dve.wait_ge(g2_in, 16 * 2)
                    link(dve.scalar_tensor_tensor(y, y, st, g2mod[0:r, s, :], ALU.mult, ALU.mult))
                    dve.tensor_tensor(x1[0:r, u, :], x1[0:r, u, :], y, ALU.add).then_inc(f_out, 1)

        @block.tensor
        def _(pe):
            def close(ins):
                ins.then_inc(fills_done, 1)

            def mm(out, lhsT, rhs, first, last):
                return pe.matmul(out, lhsT, rhs, start=first, stop=last)

            pe.wait_ge(consts_in, 48)
            pe.wait_ge(c_silu, 1)
            bank = bank_for(pe, ("cT",))
            for k in range(KD):
                ins = pe.transpose(bank[:, 16 * k:16 * k + 9], crow[0:9, k:D:KD], ident[0:9, 0:9])
            close(ins)

            def ada_group(g):
                bank = bank_for(pe, ("ada", g))
                w = wait_load(pe, ("ada", g))
                if g == 0:
                    wait_emptied(pe, ("cT",))
                for k in range(KD):
                    ins = mm(bank[0:9, :], cT[:, k, :], w[:, 512 * k:512 * k + 512], k == 0, k == KD - 1)
                close(ins)

            def transposed_rows(key, t, src):
                r = parts(t)
                for h in range(2):
                    bank = bank_for(pe, (key, t, h))
                    for k in range(4):
                        ins = pe.transpose(bank[:, k * r:(k + 1) * r], src[0:r, 4 * h + k:D:KD], ident[0:r, 0:r])
                    close(ins)

            for g in range(4):
                ada_group(g)
            pe.wait_ge(onehots_in, 48)
            pe.wait_ge(onehot_ready, 1)
            for n in range(3):
                bank = bank_for(pe, ("gtab", n))
                close(mm(bank[0:20, 0:GW], relT[0:BINS, :], oh_top[0:BINS, n * GW:(n + 1) * GW], True, True))
            for n in range(7):
                w = min(480, 3 * NT * NK - 480 * n)
                bank = bank_for(pe, ("stab", n))
                close(mm(bank[0:20, 0:w], relT[0:BINS, :], oh_smp[0:BINS, 480 * n:480 * n + w], True, True))
            for g in range(4, 8):
                ada_group(g)
            for t in range(TILES):
                pe.wait_ge(h_ready, t + 1)
                transposed_rows("hT", t, hbuf[:, t % 2, :])
                if t < 4:
                    ada_group(8 + t)
            pe.wait_ge(state_in, 16)
            bank = bank_for(pe, ("state",))
            n = NB * PSTATE
            for g in range(4):
                ins = pe.transpose(bank[:, g * P:g * P + n], staterow[0:n, g * P:(g + 1) * P], ident[0:n, 0:n])
            close(ins)

            def by_channel(key, w, col):
                for h in range(2):
                    bank = bank_for(pe, key + (h,))
                    for k in range(KD):
                        ins = mm(bank[:, 0:288], w[:, 512 * k + col:512 * k + col + P],
                                 hT[:, k, 288 * h:288 * h + 288], k == 0, k == KD - 1)
                    close(ins)

            def by_token(key, w, col, t, folded):
                bank = bank_for(pe, key)
                r = parts(t)
                for k in range(KD):
                    x = hT[:, k, t:SEQ:4] if folded and t < PT_ else hT[:, k, toks(t)]
                    ins = mm(bank[0:r, 0:256], x, w[:, 512 * k + col:512 * k + col + 256], k == 0, k == KD - 1)
                close(ins)

            for t in range(TILES):
                for h in range(2):
                    wait_emptied(pe, ("hT", t, h))
            w = wait_load(pe, ("in", 0))
            for c in range(4):
                by_channel(("u", c), w, c * P)
            w = wait_load(pe, ("in", 1))
            for c in range(4):
                by_channel(("q", c), w, c * P)
            w = wait_load(pe, ("in", 2))
            for c in range(4, 6):
                by_channel(("q", c), w, (c - 4) * P)
            for g in range(3):
                if g == 1:
                    w = wait_load(pe, ("in", 3))
                for t in range(TILES):
                    by_token(("k", g, t), w, (256, 0, 256)[g], t, g > 0)
            for g in range(3):
                if g != 1:
                    w = wait_load(pe, ("in", 4 + g // 2))
                for t in range(TILES):
                    by_token(("v", g, t), w, (0, 256, 0)[g], t, g > 0)
            for c in range(6, 8):
                by_channel(("q", c), w, 256 + (c - 6) * P)
            w = wait_load(pe, ("in", 6))
            for c in range(8, 10):
                by_channel(("q", c), w, (c - 8) * P)
            for t in range(TILES):
                by_token(("kvc", t), w, 256, t, False)
            bank = bank_for(pe, ("uout", 0))
            for c in range(4):
                ins = pe.transpose(bank[0:PSTATE, c * P:(c + 1) * P], uext[:, c, 528 - PSTATE:528], ident[:, :])
            close(ins)
            bank = bank_for(pe, ("uout", 1))
            for c in range(4):
                ins = pe.transpose(bank[0:NS, c * P:(c + 1) * P], uS[:, c, :], ident[:, :])
            close(ins)
            for t in range(TILES):
                for g in range(3):
                    wait_emptied(pe, ("k", g, t))
                wait_emptied(pe, ("kvc", t))
            for m in range(7):
                bank = bank_for(pe, ("kT", m))
                for t in range(PT_):
                    ins = pe.transpose(bank[:, t * P:(t + 1) * P], kTM[:, t, m * P:(m + 1) * P], ident[:, :])
                close(ins)
            bank = bank_for(pe, ("kTs",))
            for m in range(7):
                ins = pe.transpose(bank[:, m * NS:(m + 1) * NS], kTM[0:NS, PT_, m * P:(m + 1) * P], ident[0:NS, 0:NS])
            close(ins)

            for m in range(7):
                wait_emptied(pe, ("kT", m))
            wait_emptied(pe, ("v", 2, 4))
            wait_emptied(pe, ("v", 2, 3))
            for h in range(2):
                wait_emptied(pe, ("q", 9, h))
            for s in range(len(UNITS) + LAGO):
                if s < len(UNITS):
                    kind, t, p = UNITS[s]
                    bank = bank_for(pe, ("S", s))
                    w = head_cols(UNITS[s])
                    for h, hd in enumerate(heads(UNITS[s])):
                        if kind == "C":
                            half, cq, ck = 64 * (hd // 4), 6 + hd % 4, 6
                        else:
                            half, cq, ck = 64 * (hd % 2), 2 * kind + hd // 2, 2 * kind + hd // 2
                        rows = slice(half, half + 64)
                        q = qT[rows, cq, t:SEQ:4] if kind in (1, 2) else qT[rows, cq, toks(t)]
                        blocks = key_blocks(UNITS[s])
                        lo, k0 = blocks[0][1], blocks[0][0] * P
                        width = P * len(blocks)
                        ins = mm(bank[:, h * w + lo:h * w + lo + width], q, kT[rows, ck, k0:k0 + width], True, True)
                    close(ins)
                u = s - LAGT
                if 0 <= u < len(UNITS):
                    bank = bank_for(pe, ("T", u))
                    pe.wait_ge(probs_ready, u + 1)
                    w = head_cols(UNITS[u])
                    n = 0
                    for h in range(2):
                        for _, pos in key_blocks(UNITS[u]):
                            ins = pe.transpose(bank[:, n * P:(n + 1) * P],
                                               sbuf_[:, u % 3, h * w + pos:h * w + pos + P], ident[:, :])
                            n += 1
                    close(ins)
                u = s - LAGO
                if 0 <= u < len(UNITS):
                    kind, t, p = UNITS[u]
                    bank = bank_for(pe, ("O", u))
                    wait_emptied(pe, ("T", u))
                    n = 0
                    blocks = key_blocks(UNITS[u])
                    for h, hd in enumerate(heads(UNITS[u])):
                        col = 768 if kind == "C" else 256 * kind + P * (hd // 2)
                        for i, (kt, _) in enumerate(blocks):
                            ins = mm(bank[:, P * h:P * h + P], pTb[:, u % 2, n * P:(n + 1) * P],
                                     vTM[:, kt, col:col + P], i == 0, i == len(blocks) - 1)
                            n += 1
                    close(ins)
                for key in after_unit(u):
                    bank = bank_for(pe, key)
                    t = key[1]
                    if key[0] == "ocT":
                        wait_emptied(pe, ("O", u))
                        for c in range(4):
                            ins = pe.transpose(bank[:, c * P:(c + 1) * P], octok[:, t % 2, c * P:(c + 1) * P], ident[:, :])
                    else:
                        pe.wait_ge(bsum_ready, 1)
                        for c in range(2):
                            ins = pe.transpose(bank[:, c * P:(c + 1) * P],
                                               stage[:, 0, t * 264 + c * P:t * 264 + (c + 1) * P], ident[:, :])
                    close(ins)

            pe.wait_ge(qbd_ready, 1)
            wait_emptied(pe, ("kTs",))
            for n in range(2):
                bank = bank_for(pe, ("Sn", n))
                for m in range(4 * n, min(4 * n + 4, 6)):
                    ins = mm(bank[0:NS, (m % 4) * P:(m % 4 + 1) * P], kT[:, m, SEQ:TOK], qbd[:, m, :], True, True)
                close(ins)
            bank = bank_for(pe, ("SnC",))
            close(mm(bank[0:NS, :], kT[:, 6, SEQ:TOK], qbdC, True, True))

            def cached(kv, kind, b, r, p):
                if kind == "C":
                    return slot[slot_of((kv, "c0", 0))][:, 128 * b:128 * b + 128]
                if kind == 0:
                    c = 1024 + 256 * b + 128 * p
                    return slot[slot_of((kv, "c0", 0))][:, c:c + 128]
                if kind == 1:
                    c = 1024 * (b % 4) + 256 * r + 128 * p
                    return slot[slot_of((kv, "c1", b // 4))][:, c:c + 128]
                c = 2048 * (b % 2) + 256 * r + 128 * p
                return slot[slot_of((kv, "c2", b // 2))][:, c:c + 128]

            def load_of(kv, kind, b):
                return (kv, "c0", 0) if kind in ("C", 0) else (kv, "c1", b // 4) if kind == 1 else (kv, "c2", b // 2)

            for s in range(NKF + 1):
                if s < NKF:
                    bank = bank_for(pe, ("KT", s))
                    for n, (kind, b, r, p) in enumerate(KEYS[s]):
                        wait_load(pe, load_of("K", kind, b))
                        ins = pe.transpose(bank[:, n * P:(n + 1) * P], cached("K", kind, b, r, p), ident[:, :])
                    close(ins)
                if s >= 1:
                    bank = bank_for(pe, ("SM", s - 1))
                    wait_emptied(pe, ("KT", s - 1))
                    for n, (kind, b, r, p) in enumerate(KEYS[s - 1]):
                        q = qbdC[:, P * (b // 2):P * (b // 2) + P] if kind == "C" else qbd[:, 2 * kind + p, :]
                        ins = mm(bank[:, n * P:(n + 1) * P], ktr[:, (s - 1) % 4, n * P:(n + 1) * P], q, True, True)
                    close(ins)
            for n in range(NKF - 2, NKF):
                wait_emptied(pe, ("SM", n))
            for c in range(4):
                bank = bank_for(pe, ("SRC", c))
                wait_emptied(pe, ("SnC",))
                pe.transpose(bank[:, 0:P], stC[:, c * P:(c + 1) * P], ident[:, :])
                close(pe.transpose(bank[:, P:SK], stCn[0:NS, c * P:(c + 1) * P], ident[0:NS, 0:NS]))
            for g in range(3):
                for p in range(2):
                    m = 2 * g + p
                    bank = bank_for(pe, ("SR", g, p))
                    wait_emptied(pe, ("Sn", m // 4))
                    pe.transpose(bank[:, 0:P], stB[:, m, :], ident[:, :])
                    close(pe.transpose(bank[:, P:SK], stBn[0:NS, m, :], ident[0:NS, 0:NS]))
            pe.wait_ge(sprob_ready, 1)
            bank = bank_for(pe, ("PTC",))
            for c in range(4):
                ins = pe.transpose(bank[:, c * P:(c + 1) * P], sC[:, c, 0:P], ident[:, :])
            close(ins)
            bank = bank_for(pe, ("PTCn",))
            for c in range(4):
                ins = pe.transpose(bank[0:NS, c * P:(c + 1) * P], sC[:, c, P:SK], ident[:, :])
            close(ins)
            for p in range(2):
                bank = bank_for(pe, ("PT", p))
                for g in range(3):
                    ins = pe.transpose(bank[:, g * P:(g + 1) * P], sB[:, p, g * SK:g * SK + P], ident[:, :])
                close(ins)
                bank = bank_for(pe, ("PTn", p))
                for g in range(3):
                    ins = pe.transpose(bank[0:NS, g * P:(g + 1) * P], sB[:, p, g * SK + P:(g + 1) * SK], ident[:, :])
                close(ins)
            oc, ob = bank_for(pe, ("OC",)), [bank_for(pe, ("OB", p)) for p in range(2)]
            for key in (("PTC",), ("PTCn",), ("PT", 0), ("PTn", 0), ("PT", 1), ("PTn", 1)):
                wait_emptied(pe, key)
            close(mm(oc[:, :], vTM[0:NS, PT_, 768:896], pCn[0:NS, :], True, True))
            for p in range(2):
                for g in range(3):
                    c = 256 * g + P * p
                    ins = mm(ob[p][:, 0:P], vTM[0:NS, PT_, c:c + P], pBn[0:NS, 3 * p + g, :], g == 0, g == 2)
                close(ins)
            for s in range(NKF):
                bank = bank_for(pe, ("VO", s))
                for n, (kind, b, r, p) in enumerate(KEYS[s]):
                    wait_load(pe, load_of("V", kind, b))
                    probs = pC[:, P * (b // 2):P * (b // 2) + P] if kind == "C" else pB[:, 3 * p + kind, :]
                    ins = mm(bank[:, n * P:(n + 1) * P], cached("V", kind, b, r, p), probs, True, True)
                close(ins)

            wc = slot[slot_of(("wc",))]
            for m in range(KD):
                wg = wait_load(pe, ("gate", m))
                for h in range(2):
                    cols = slice(288 * h, 288 * h + 288)
                    for j, what in enumerate(("ga", "gb", "gc")):
                        bank = bank_for(pe, (what, m, h))
                        for k in range(KD):
                            c = 1024 * j + P * k
                            ins = mm(bank[:, 0:288], wg[:, c:c + P], hT[:, k, cols], k == 0, k == KD - 1)
                        close(ins)
                    if m == 0 and h == 0:
                        pe.wait_ge(branches_ready, 1)
                        pe.wait_ge(merge_in, 32)
                        pe.wait_ge(z_ready, 1)
                    bank = bank_for(pe, ("oa", m, h))
                    close(mm(bank[:, 0:288], pw[:, m // 2, (m % 2) * P:(m % 2 + 1) * P], zT[:, m // 2, cols], True, True))
                    bank = bank_for(pe, ("ob", m, h))
                    for c in range(2):
                        ins = mm(bank[:, 0:288], wb[:, c, m * P:(m + 1) * P], bT[:, c, cols], c == 0, c == 1)
                    close(ins)
                    wait_load(pe, ("wc",))
                    bank = bank_for(pe, ("oc", m, h))
                    for c in range(4):
                        ins = mm(bank[:, 0:288], wc[:, D * c + m * P:D * c + (m + 1) * P], ocT[:, c, cols], c == 0, c == 3)
                    close(ins)
            w = slot[slot_of(("wsd",))]
            wr = w[:, 2048:2048 + KD * NE]

            def routed(t):
                pe.wait_ge(h_ready, TILES + t + 1)
                transposed_rows("h2T", t, hbuf2[:, t % 2, :])
                r = parts(t)
                bank = bank_for(pe, ("rt", t))
                for h in range(2):
                    wait_emptied(pe, ("h2T", t, h))
                wait_load(pe, ("wsd",))
                for k in range(KD):
                    ins = mm(bank[0:r, 0:NE], h2T[:, k, toks(t)], wr[:, NE * k:NE * (k + 1)], k == 0, k == KD - 1)
                close(ins)

            for t in range(TILES):
                r = parts(t)
                for h in range(2):
                    wo = wait_load(pe, ("wout", h))
                    bank = bank_for(pe, ("mix", t, h))
                    for m in range(KD):
                        if t == 0 and h == 0:
                            pe.wait_ge(mix_ready, 2 * m + 2)
                        ins = mm(bank[0:r, :], mixT[:, m, toks(t)], wo[:, 512 * m:512 * m + 512], m == 0, m == KD - 1)
                    close(ins)
                if t >= 2:
                    routed(t - 2)

            wgu = slot[slot_of(("wsgu",))].rearrange("p (j k n) -> p k j n", j=2, k=KD)

            def shared_down(t):
                r = parts(t)
                bank = bank_for(pe, ("saT", t))
                pe.wait_ge(sact_ready, t + 1)
                for k in range(2):
                    ins = pe.transpose(bank[:, k * r:(k + 1) * r], sact[0:r, k:FF:2], ident[0:r, 0:r])
                close(ins)
                for h in range(2):
                    bank = bank_for(pe, ("sy", t, h))
                    wait_emptied(pe, ("saT", t))
                    for k in range(2):
                        c = D * k + 512 * h
                        ins = mm(bank[0:r, :], saT[:, k, 0:r], w[:, c:c + 512], k == 0, k == 1)
                    close(ins)

            def shared_in(t):
                r = parts(t)
                wait_load(pe, ("wsgu",))
                bank = bank_for(pe, ("sgu", t))
                for k in range(KD):
                    ins = mm(bank[0:r, :], h2T[:, k, toks(t)], wgu[:, k], k == 0, k == KD - 1)
                close(ins)

            routed(TILES - 2)
            shared_in(0)
            routed(TILES - 1)
            shared_in(1)
            shared_down(0)
            pe.wait_ge(moe_in, 32)
            pe.wait_ge(masks_ready, TILES)
            tri = const2[:, 0, :]
            for t in range(TILES):
                r = parts(t)
                bank = bank_for(pe, ("pos", t))
                for u in range(t + 1):
                    n = parts(u)
                    ins = mm(bank[0:r, 0:NE], tri[0:n, 0:r] if u == t else ones[0:n, 0:r], maskt[0:n, u, :],
                             u == 0, u == t)
                close(ins)
            bank = bank_for(pe, ("cnt",))
            for u in range(TILES):
                n = parts(u)
                ins = mm(bank[:, 0:NE], ones[0:n, :], maskt[0:n, u, :], u == 0, u == TILES - 1)
            close(ins)

            def block_rows(t):
                bank = psb[7]
                if t == 0:
                    bank_for(pe, ("rowtok",))
                r = parts(t)
                pe.wait_ge(ohs_ready, t + 1)
                for k in range(TOPK):
                    ins = mm(bank[:, 0:2 * NBLK], ohslot[0:r, k, :], ohblk[0:r, :, k * NBLK:(k + 1) * NBLK],
                             t == 0 and k == 0, t == TILES - 1 and k == TOPK - 1)
                if t < TILES - 1:
                    ins.then_inc(ohs_used, 1)
                else:
                    close(ins)

            for t in range(2, TILES):
                shared_in(t)
                shared_down(t - 1)
                block_rows(t - 2)
            shared_down(TILES - 1)
            block_rows(TILES - 2)
            block_rows(TILES - 1)
            bank = bank_for(pe, ("bexp",))
            pe.wait_ge(bexp_ready, 1)
            for n in range(3):
                mm(bank[0:1, n * P:(n + 1) * P], bexpf[:, 3 + n:4 + n], ident[:, :], True, True)
            for n in range(2):
                ins = mm(bank[0:1, 3 * P + n * NE:3 * P + (n + 1) * NE], bexpf[:, 6 + n:7 + n], ident[:, 0:NE],
                         True, True)
            close(ins)

            pe.wait_ge(tables_ready, 1)
            wait_emptied(pe, ("sy", TILES - 1, 1))
            n_pairs = pe.value_load(pairs[0:1, 0:1], min_val=1, max_val=NBLK // 2)
            pe.sem_inc(t_done, 2)
            pe.sem_inc(gu_done, 2)
            pe.sem_inc(d_done, 2)
            pe.sem_inc(y_act, 1)
            pe.sem_inc(y_dve, 1)
            with pe.Fori(0, n_pairs) as i:
                side = [pe.value_load(blocki[0:1, 2, bass.ds(2 * i + j, 1)], min_val=0, max_val=1) for j in range(2)]
                weights = [arena[:, bass.ds((A_W1 - A_W0) * side[j] + A_W0, 6144)] for j in range(2)]
                for j in range(2):
                    if j == 1:
                        pe.wait_ge(y_act, 2 * i + 1)
                        pe.wait_ge(y_dve, 2 * i + 1)
                    pe.wait_ge(xg_in[j], 16 * i + 16)
                    for k in range(KD):
                        ins = pe.transpose(psb[2 * j + k // 4][:, P * (k % 4):P * (k % 4 + 1)], xg[:, j, k:D:KD],
                                           ident[:, :])
                    ins.then_inc(t_done, 1)
                def gate_up(j, ks):
                    pe.wait_ge(weights_in, 2 * i + j + 1)
                    pe.wait_ge(xt_act, 2 * i + j + 1)
                    pe.wait_ge(xt_dve, 2 * i + j + 1)
                    wv = weights[j][:, 0:4096].rearrange("p (j k n) -> p k j n", j=2, k=KD)
                    for k in ks:
                        ins = mm(psb[4 + j][:, :], xT[:, j, P * k:P * (k + 1)], wv[:, k], k == 0, k == KD - 1)
                    return ins

                def turn(j):
                    pe.wait_ge(a_ready, 2 * i + j + 1)
                    for k in range(2):
                        ins = pe.transpose(psb[j][:, k * P:(k + 1) * P], act3[:, 3 * j + 2, k:FF:2], ident[:, :])
                    ins.then_inc(at_done, 1)

                def down(j, h):
                    pe.wait_ge(at_ready, 2 * i + j + 1)
                    to = psb[(6 if j == 0 else 2) + h]
                    for k in range(2):
                        c = 4096 + D * k + 512 * h
                        ins = mm(to[:, :], aT[:, j, k * P:(k + 1) * P], weights[j][:, c:c + 512], k == 0, k == 1)
                    return ins

                gate_up(0, range(KD)).then_inc(gu_done, 1)
                gate_up(1, range(KD // 2))
                turn(0)
                gate_up(1, range(KD // 2, KD)).then_inc(gu_done, 1)
                down(0, 0)
                turn(1)
                down(0, 1).then_inc(d_done, 1)
                down(1, 0)
                down(1, 1).then_inc(d_done, 1)


_INS = ['x_prompt', 'x_sample', 'cache_b1', 'cache_b2', 'cache_b3', 'cache_c', 'state_pool', 'c_prompt',
        'c_sample', 'rel_bias', 'w_ada', 'b_ada', 'g_pre_mix', 'g_post_mix', 'g_pre_ffn', 'g_post_ffn',
        'w_in', 'pool_w', 'pool_scale', 'w_b_up', 'w_c_up', 'sinks', 'w_out', 'w_router', 'router_bias',
        'we_gate', 'we_up', 'we_down', 'ws_gate', 'ws_up', 'ws_down']
_OUTS = ([(1, SEQ, D), (NB, NT, D)]
         + [(1, 1, min(n, SEQ), 2, 4, HD) for n in CACHE] + [(1, 1, P, 2, 2, HD), (1, 1, PSTATE, 512)]
         + [(1, NB, n, 2, 4, HD) for n in CACHE] + [(1, NB, P, 2, 2, HD), (1, NB, PSTATE, 512)])


def kernel(**inputs):
    import concourse.bacc as bacc
    from concourse.bass_utils import run_bass_kernel_spmd

    nc = bacc.Bacc("TRN2", target_bir_lowering=False, num_devices=1)
    arrays, args = {}, []
    named = [(name, np.ascontiguousarray(inputs[name])) for name in _INS]
    named += list(zip(("onehot_top", "onehot_smp", "const"), consts()))
    for name, a in named:
        arrays["in_" + name] = a
        args.append(nc.dram_tensor("in_" + name, a.shape, mybir.dt.from_np(a.dtype), kind="ExternalInput").ap())
    for i, shape in enumerate(_OUTS):
        args.append(nc.dram_tensor(f"out_{i}", shape, F32, kind="ExternalOutput").ap())
    build(nc, *args)
    r = run_bass_kernel_spmd(nc, [arrays], core_ids=[0])
    return tuple(r.results[0][f"out_{i}"] for i in range(len(_OUTS)))
```
